# Optimizing a Trainium2 kernel written in Bass

```python
import math
import jax, jax.numpy as jnp
from jax import lax
import numpy as np

D_MODEL = 1024
BATCH = 1
SEQ = 256
DEPTH = 2

GRID_W = 64
CTX_LEN = 256
N_MIXERS = 2
N_RET_LAYERS = (DEPTH + 1) // 2
N_DIFF_LAYERS = DEPTH // 2
RET_HEADS = 4
RET_DK = D_MODEL // RET_HEADS
RET_DV = 2 * RET_DK
RET_CHUNK = 128
RET_IN = 2 * RET_HEADS * RET_DK + 3 * RET_HEADS * RET_DV
DIFF_HEADS = 8
DIFF_D = D_MODEL // (2 * DIFF_HEADS)
DIFF_Q_BLOCK = 128
FFN_HIDDEN = ((8 * D_MODEL // 3 + 127) // 128) * 128
CONV_W = 3
ROPE_BASE = 10000.0
EPS = 1e-6


def rms_norm(x, g):
    x32 = x.astype(jnp.float32)
    y = x32 * lax.rsqrt(jnp.mean(x32 * x32, axis=-1, keepdims=True) + EPS)
    return (y * g.astype(jnp.float32)).astype(x.dtype)

def head_norm(x):
    x32 = x.astype(jnp.float32)
    return x32 * lax.rsqrt(jnp.mean(x32 * x32, axis=-1, keepdims=True) + EPS)

def ada_mod(cvec, w, b):
    m = jax.nn.silu(cvec) @ w + b
    return jnp.split(m[:, None, :], 6, axis=-1)

def modulate(xn, shift, scale):
    return xn * (1 + scale) + shift

def grid_positions(n):
    rows = n // GRID_W
    row = jnp.repeat(jnp.arange(rows, dtype=jnp.float32), GRID_W)
    col = jnp.tile(jnp.arange(GRID_W, dtype=jnp.float32), rows)
    return row, col

def rope_1d(x, pos):
    d2 = x.shape[-1]
    inv = ROPE_BASE ** (-jnp.arange(0, d2, 2, dtype=jnp.float32) / d2)
    ang = pos[:, None] * inv[None, :]
    cos, sin = jnp.cos(ang), jnp.sin(ang)
    x32 = x.astype(jnp.float32)
    x1, x2 = x32[..., : d2 // 2], x32[..., d2 // 2:]
    return jnp.concatenate([x1 * cos - x2 * sin, x1 * sin + x2 * cos], axis=-1).astype(x.dtype)

def rope_2d(x, row, col):
    half = x.shape[-1] // 2
    return jnp.concatenate([rope_1d(x[..., :half], row), rope_1d(x[..., half:], col)], axis=-1)

def split_heads(t, h, d):
    b, n = t.shape[0], t.shape[1]
    return t.reshape(b, n, h, d).transpose(0, 2, 1, 3)

def merge_heads(t):
    b, h, n, d = t.shape
    return t.transpose(0, 2, 1, 3).reshape(b, n, h * d)

def retention_scan(q, k, v, log_gamma, r0):
    b, h, n, dk = q.shape
    dv = v.shape[-1]
    nc = n // RET_CHUNK
    q, k, v = q.astype(jnp.float32), k.astype(jnp.float32), v.astype(jnp.float32)
    idx = jnp.arange(RET_CHUNK, dtype=jnp.float32)
    diff = idx[:, None] - idx[None, :]
    lg = log_gamma.astype(jnp.float32)
    dmask = jnp.where(diff >= 0, jnp.exp(lg[:, None, None] * jnp.maximum(diff, 0.0)), 0.0)
    xi = jnp.exp(lg[:, None] * (idx + 1.0))[None, :, :, None]
    zeta = jnp.exp(lg[:, None] * (RET_CHUNK - 1.0 - idx))[None, :, :, None]
    chunk_decay = jnp.exp(lg * RET_CHUNK)[None, :, None, None]

    def step(r, qkv):
        qc, kc, vc = qkv
        s = jnp.einsum('bhid,bhjd->bhij', qc, kc) * dmask
        o = jnp.einsum('bhij,bhjv->bhiv', s, vc) + jnp.einsum('bhid,bhdv->bhiv', qc, r) * xi
        r = r * chunk_decay + jnp.einsum('bhjd,bhjv->bhdv', kc * zeta, vc)
        return r, o

    def to_chunks(t):
        return jnp.moveaxis(t.reshape(b, h, nc, RET_CHUNK, t.shape[-1]), 2, 0)

    r, o = lax.scan(step, r0, (to_chunks(q), to_chunks(k), to_chunks(v)))
    return jnp.moveaxis(o, 0, 2).reshape(b, h, n, dv), r

def retention_mixer(hx, hc, w_in, w_out, logit_f, logit_b, need_ctx):
    hdk, hdv = RET_HEADS * RET_DK, RET_HEADS * RET_DV

    def proj(u):
        p = u @ w_in
        q, k, v, gf, gb = jnp.split(p, [hdk, 2 * hdk, 2 * hdk + hdv, 2 * hdk + 2 * hdv], axis=-1)
        return (split_heads(q, RET_HEADS, RET_DK), split_heads(k, RET_HEADS, RET_DK) * (RET_DK ** -0.5),
                split_heads(v, RET_HEADS, RET_DV), gf, gb)

    qx, kx, vx, gfx, gbx = proj(hx)
    qc, kc, vc, gfc, gbc = proj(hc)
    row, col = grid_positions(hx.shape[1])
    qx, kx = rope_2d(qx, row, col), rope_2d(kx, row, col)
    lg_f = jax.nn.log_sigmoid(logit_f.astype(jnp.float32))
    lg_b = jax.nn.log_sigmoid(logit_b.astype(jnp.float32))
    r0 = jnp.zeros((hx.shape[0], RET_HEADS, RET_DK, RET_DV), jnp.float32)
    flip = lambda t: jnp.flip(t, axis=2)
    oc_f, rc_f = retention_scan(qc, kc, vc, lg_f, r0)
    oc_b, rc_b = retention_scan(flip(qc), flip(kc), flip(vc), lg_b, r0)
    ox_f, _ = retention_scan(qx, kx, vx, lg_f, rc_f)
    ox_b, _ = retention_scan(flip(qx), flip(kx), flip(vx), lg_b, rc_b)

    def merge(of, ob, gf, gb, dt):
        y = (jax.nn.silu(gf.astype(jnp.float32)) * merge_heads(head_norm(of))
             + jax.nn.silu(gb.astype(jnp.float32)) * merge_heads(head_norm(ob)))
        return y.astype(dt) @ w_out

    yx = merge(ox_f, flip(ox_b), gfx, gbx, hx.dtype)
    yc = merge(oc_f, flip(oc_b), gfc, gbc, hc.dtype) if need_ctx else None
    return yx, yc

def diff_attend(q1, q2, k1, k2, v, lam):
    b, h, n, d = q1.shape
    nb = n // DIFF_Q_BLOCK
    scale = d ** -0.5

    def to_blocks(t):
        return jnp.moveaxis(t.reshape(b, h, nb, DIFF_Q_BLOCK, d), 2, 0)

    def one(qs):
        a, c = qs
        s1 = jnp.einsum('bhqd,bhkd->bhqk', a, k1).astype(jnp.float32) * scale
        s2 = jnp.einsum('bhqd,bhkd->bhqk', c, k2).astype(jnp.float32) * scale
        p = jax.nn.softmax(s1, axis=-1) - lam * jax.nn.softmax(s2, axis=-1)
        return jnp.einsum('bhqk,bhkv->bhqv', p.astype(v.dtype), v)

    o = lax.map(one, (to_blocks(q1), to_blocks(q2)))
    return jnp.moveaxis(o, 0, 2).reshape(b, h, n, v.shape[-1])

def diff_mixer(hx, hc, w_in, w_out, lq1, lk1, lq2, lk2, subln_g, lam_init, need_ctx):
    def proj(u):
        bsz, n = u.shape[0], u.shape[1]
        p = u @ w_in
        q, k, v = jnp.split(p, [D_MODEL, 2 * D_MODEL], axis=-1)
        q = q.reshape(bsz, n, DIFF_HEADS, 2, DIFF_D).transpose(0, 2, 3, 1, 4)
        k = k.reshape(bsz, n, DIFF_HEADS, 2, DIFF_D).transpose(0, 2, 3, 1, 4)
        v = split_heads(v, DIFF_HEADS, 2 * DIFF_D)
        return q[:, :, 0], q[:, :, 1], k[:, :, 0], k[:, :, 1], v

    q1x, q2x, k1x, k2x, vx = proj(hx)
    q1c, q2c, k1c, k2c, vc = proj(hc)
    row, col = grid_positions(hx.shape[1])
    q1x, q2x = rope_2d(q1x, row, col), rope_2d(q2x, row, col)
    k1x, k2x = rope_2d(k1x, row, col), rope_2d(k2x, row, col)
    lam = (jnp.exp(jnp.sum(lq1.astype(jnp.float32) * lk1.astype(jnp.float32)))
           - jnp.exp(jnp.sum(lq2.astype(jnp.float32) * lk2.astype(jnp.float32))) + lam_init)
    k1a = jnp.concatenate([k1x, k1c], axis=2)
    k2a = jnp.concatenate([k2x, k2c], axis=2)
    va = jnp.concatenate([vx, vc], axis=2)

    def post(o):
        return merge_heads(rms_norm(o, subln_g) * (1.0 - lam_init)) @ w_out

    yx = post(diff_attend(q1x, q2x, k1a, k2a, va, lam))
    yc = post(diff_attend(q1c, q2c, k1c, k2c, vc, lam)) if need_ctx else None
    return yx, yc

def dwconv3(x, w, b):
    xp = jnp.pad(x, ((0, 0), (1, 1), (0, 0)))
    return xp[:, :-2] * w[0] + xp[:, 1:-1] * w[1] + xp[:, 2:] * w[2] + b

def conv_ffn(u, w_up, conv_w, conv_b, w_down):
    val, gate = jnp.split(u @ w_up, 2, axis=-1)
    return (jax.nn.silu(dwconv3(gate, conv_w, conv_b)) * val) @ w_down

def first_inputs(seed: int = 0) -> dict:
    key = jax.random.key(seed)
    ks = jax.random.split(key, 24)
    f32 = jnp.float32
    nrm = lambda k, s, sc: jax.random.normal(k, s, f32) * sc
    base_logit = jnp.log(2.0 ** (5.0 + jnp.arange(RET_HEADS, dtype=f32)) - 1.0)
    return {
        "x": nrm(ks[0], (BATCH, SEQ, D_MODEL), 1.0),
        "c": nrm(ks[1], (BATCH, D_MODEL), 1.0),
        "ctx": nrm(ks[2], (BATCH, CTX_LEN, D_MODEL), 1.0),
        "c_ctx": nrm(ks[3], (D_MODEL,), 1.0),
        "ada_w": nrm(ks[4], (DEPTH, D_MODEL, 6 * D_MODEL), 0.5 * D_MODEL ** -0.5),
        "ada_b": nrm(ks[5], (DEPTH, 6 * D_MODEL), 0.02),
        "norm_g": 1.0 + nrm(ks[6], (DEPTH, 4, D_MODEL), 0.1),
        "ret_w_in": nrm(ks[7], (N_RET_LAYERS, D_MODEL, RET_IN), D_MODEL ** -0.5),
        "ret_w_out": nrm(ks[8], (N_RET_LAYERS, RET_HEADS * RET_DV, D_MODEL), (RET_HEADS * RET_DV) ** -0.5),
        "ret_decay_f": base_logit + nrm(ks[9], (N_RET_LAYERS, RET_HEADS), 0.05),
        "ret_decay_b": base_logit + nrm(ks[10], (N_RET_LAYERS, RET_HEADS), 0.05),
        "diff_w_in": nrm(ks[11], (N_DIFF_LAYERS, D_MODEL, 3 * D_MODEL), D_MODEL ** -0.5),
        "diff_w_out": nrm(ks[12], (N_DIFF_LAYERS, D_MODEL, D_MODEL), D_MODEL ** -0.5),
        "diff_lq1": nrm(ks[13], (N_DIFF_LAYERS, DIFF_D), 0.1),
        "diff_lk1": nrm(ks[14], (N_DIFF_LAYERS, DIFF_D), 0.1),
        "diff_lq2": nrm(ks[15], (N_DIFF_LAYERS, DIFF_D), 0.1),
        "diff_lk2": nrm(ks[16], (N_DIFF_LAYERS, DIFF_D), 0.1),
        "diff_subln": 1.0 + nrm(ks[17], (N_DIFF_LAYERS, 2 * DIFF_D), 0.1),
        "ffn_w_up": nrm(ks[18], (DEPTH, D_MODEL, 2 * FFN_HIDDEN), D_MODEL ** -0.5),
        "ffn_conv_w": nrm(ks[19], (DEPTH, CONV_W, FFN_HIDDEN), CONV_W ** -0.5),
        "ffn_conv_b": nrm(ks[20], (DEPTH, FFN_HIDDEN), 0.02),
        "ffn_w_down": nrm(ks[21], (DEPTH, FFN_HIDDEN, D_MODEL), FFN_HIDDEN ** -0.5),
    }

def first_block(x, c, ctx, c_ctx, ada_w, ada_b, norm_g, ret_w_in, ret_w_out, ret_decay_f, ret_decay_b,
              diff_w_in, diff_w_out, diff_lq1, diff_lk1, diff_lq2, diff_lk2, diff_subln,
              ffn_w_up, ffn_conv_w, ffn_conv_b, ffn_w_down):
    h_x, h_c = x, ctx
    for l in range(DEPTH):
        last = l == DEPTH - 1
        shm, scm, gm, shf, scf, gf = ada_mod(c, ada_w[l], ada_b[l])
        cshm, cscm, cgm, cshf, cscf, cgf = ada_mod(c_ctx[None, :], ada_w[l], ada_b[l])
        ux = modulate(rms_norm(h_x, norm_g[l, 0]), shm, scm)
        uc = modulate(rms_norm(h_c, norm_g[l, 0]), cshm, cscm)
        i = l // N_MIXERS
        if l % N_MIXERS == 0:
            yx, yc = retention_mixer(ux, uc, ret_w_in[i], ret_w_out[i], ret_decay_f[i], ret_decay_b[i],
                                     not last)
        else:
            lam_init = 0.8 - 0.6 * math.exp(-0.3 * l)
            yx, yc = diff_mixer(ux, uc, diff_w_in[i], diff_w_out[i], diff_lq1[i], diff_lk1[i],
                                diff_lq2[i], diff_lk2[i], diff_subln[i], lam_init, not last)
        h_x = h_x + gm * rms_norm(yx, norm_g[l, 1])
        fx = conv_ffn(modulate(rms_norm(h_x, norm_g[l, 2]), shf, scf),
                      ffn_w_up[l], ffn_conv_w[l], ffn_conv_b[l], ffn_w_down[l])
        h_x = h_x + gf * rms_norm(fx, norm_g[l, 3])
        if not last:
            h_c = h_c + cgm * rms_norm(yc, norm_g[l, 1])
            fc = conv_ffn(modulate(rms_norm(h_c, norm_g[l, 2]), cshf, cscf),
                          ffn_w_up[l], ffn_conv_w[l], ffn_conv_b[l], ffn_w_down[l])
            h_c = h_c + cgf * rms_norm(fc, norm_g[l, 3])
    return h_x


DEPTH_2 = 1

HEAD_DIM = 64
N_HEADS_A = 8
N_HEADS_B = 8
D_A = N_HEADS_A * HEAD_DIM
D_B = N_HEADS_B * HEAD_DIM
N_IDX_HEADS = 8
IDX_DIM = 64
D_RNN = 512
N_RNN_BLOCKS = 8
RNN_BLOCK = D_RNN // N_RNN_BLOCKS
CONV_WIDTH = 4
LRU_C = 8.0
D_FF = 4 * D_MODEL
MOBA_BLOCK = 256
MOBA_TOPK = 3
DSA_MAX_TOPK = 256
Q_BLOCK = 128
N_BUCKETS = 32
MAX_DISTANCE = 128
N_BRANCHES = 3
N_ATTN_HEADS = N_HEADS_A + N_HEADS_B
NEG = -1e30

IN_SPLITS = (D_A, D_A, D_A,
             D_B, D_B, D_B,
             N_IDX_HEADS * IDX_DIM,
             IDX_DIM,
             N_IDX_HEADS,
             D_RNN, D_RNN,
             N_BRANCHES * D_MODEL)
D_IN = sum(IN_SPLITS)
IN_OFFSETS = tuple(int(o) for o in np.cumsum(IN_SPLITS)[:-1])


def rms_norm_2(x, g):
    xf = x.astype(jnp.float32)
    y = xf * lax.rsqrt(jnp.mean(xf * xf, axis=-1, keepdims=True) + EPS)
    return (y * g.astype(jnp.float32)).astype(x.dtype)

def t5_bucket(dist):
    n = jnp.maximum(dist, 0)
    max_exact = N_BUCKETS // 2
    nf = jnp.maximum(n, 1).astype(jnp.float32)
    large = max_exact + (jnp.log(nf / max_exact) / math.log(MAX_DISTANCE / max_exact)
                         * (N_BUCKETS - max_exact)).astype(jnp.int32)
    large = jnp.minimum(large, N_BUCKETS - 1)
    return jnp.where(n < max_exact, n, large)

def moba_attention(q, k, v, bias_tab):
    B, S, H, dh = q.shape
    nb = -(-S // MOBA_BLOCK)
    pad = nb * MOBA_BLOCK - S
    kp = jnp.pad(k, ((0, 0), (0, pad), (0, 0), (0, 0)))
    vp = jnp.pad(v, ((0, 0), (0, pad), (0, 0), (0, 0)))
    kblk = kp.reshape(B, nb, MOBA_BLOCK, H, dh).transpose(0, 3, 1, 2, 4)
    vblk = vp.reshape(B, nb, MOBA_BLOCK, H, dh).transpose(0, 3, 1, 2, 4)
    kmean = jnp.mean(kblk, axis=3)
    n_sel = min(MOBA_TOPK, nb)
    scale = dh ** -0.5
    b_ix = jnp.arange(B)[:, None, None, None]
    h_ix = jnp.arange(H)[None, None, :, None]
    blk_ids = jnp.arange(nb)
    bias_t = bias_tab.T

    def one_block(qb):
        t0 = qb * Q_BLOCK
        cur = t0 // MOBA_BLOCK
        t = t0 + jnp.arange(Q_BLOCK)
        qq = lax.dynamic_slice_in_dim(q, t0, Q_BLOCK, axis=1)
        gate = jnp.einsum('bqhd,bhnd->bqhn', qq, kmean).astype(jnp.float32)
        gate = jnp.where(blk_ids < cur, gate, NEG)
        _, sel = lax.top_k(gate, n_sel)
        sel_ok = sel < cur
        kg = kblk[b_ix, h_ix, sel]
        vg = vblk[b_ix, h_ix, sel]
        s_past = jnp.einsum('bqhd,bqhnkd->bqhnk', qq, kg).astype(jnp.float32) * scale
        pos_past = sel[..., None] * MOBA_BLOCK + jnp.arange(MOBA_BLOCK)
        bias_past = bias_t[h_ix[..., None], t5_bucket(t[None, :, None, None, None] - pos_past)]
        s_past = jnp.where(sel_ok[..., None], s_past + bias_past, NEG)
        k_own = lax.dynamic_slice_in_dim(kp, cur * MOBA_BLOCK, MOBA_BLOCK, axis=1)
        v_own = lax.dynamic_slice_in_dim(vp, cur * MOBA_BLOCK, MOBA_BLOCK, axis=1)
        rel = t[:, None] - (cur * MOBA_BLOCK + jnp.arange(MOBA_BLOCK))[None, :]
        bias_own = bias_tab[t5_bucket(rel)].transpose(0, 2, 1)[None]
        s_own = jnp.einsum('bqhd,bkhd->bqhk', qq, k_own).astype(jnp.float32) * scale + bias_own
        s_own = jnp.where((rel >= 0)[None, :, None, :], s_own, NEG)
        logits = jnp.concatenate([s_past.reshape(B, Q_BLOCK, H, n_sel * MOBA_BLOCK), s_own], axis=-1)
        p = jax.nn.softmax(logits, axis=-1).astype(v.dtype)
        p_past = p[..., :n_sel * MOBA_BLOCK].reshape(B, Q_BLOCK, H, n_sel, MOBA_BLOCK)
        p_own = p[..., n_sel * MOBA_BLOCK:]
        return (jnp.einsum('bqhnk,bqhnkd->bqhd', p_past, vg)
                + jnp.einsum('bqhk,bkhd->bqhd', p_own, v_own))

    out = lax.map(one_block, jnp.arange(S // Q_BLOCK))
    return out.transpose(1, 0, 2, 3, 4).reshape(B, S, H * dh)

def dsa_attention(q, k, v, qi, ki, wi, bias_tab):
    B, S, H, dh = q.shape
    n_keep = min(DSA_MAX_TOPK, S // 4)
    scale = dh ** -0.5
    idx_scale = (N_IDX_HEADS ** -0.5) * (IDX_DIM ** -0.5)
    s_all = jnp.arange(S)

    def one_block(qb):
        t0 = qb * Q_BLOCK
        t = t0 + jnp.arange(Q_BLOCK)
        qq = lax.dynamic_slice_in_dim(q, t0, Q_BLOCK, axis=1)
        qiq = lax.dynamic_slice_in_dim(qi, t0, Q_BLOCK, axis=1)
        wq = lax.dynamic_slice_in_dim(wi, t0, Q_BLOCK, axis=1)
        dots = jnp.einsum('bqhd,bsd->bqhs', qiq, ki)
        score = jnp.einsum('bqh,bqhs->bqs', wq, jax.nn.relu(dots)).astype(jnp.float32) * idx_scale
        score = jnp.where((s_all[None, :] <= t[:, None])[None], score, NEG)
        _, idx = lax.top_k(score, n_keep)
        ok = idx <= t[None, :, None]
        kg = jax.vmap(lambda kk, ii: kk[ii])(k, idx)
        vg = jax.vmap(lambda vv, ii: vv[ii])(v, idx)
        bias = bias_tab[t5_bucket(t[None, :, None] - idx)].transpose(0, 1, 3, 2)
        logits = jnp.einsum('bqhd,bqkhd->bqhk', qq, kg).astype(jnp.float32) * scale + bias
        logits = jnp.where(ok[:, :, None, :], logits, NEG)
        p = jax.nn.softmax(logits, axis=-1).astype(v.dtype)
        return jnp.einsum('bqhk,bqkhd->bqhd', p, vg)

    out = lax.map(one_block, jnp.arange(S // Q_BLOCK))
    return out.transpose(1, 0, 2, 3, 4).reshape(B, S, H * dh)

def causal_depthwise_conv(x, w, b):
    S = x.shape[1]
    xp = jnp.pad(x, ((0, 0), (CONV_WIDTH - 1, 0), (0, 0)))
    y = b
    for i in range(CONV_WIDTH):
        y = y + w[i] * xp[:, i:i + S]
    return y

def rg_lru(x, w_r, b_r, w_i, b_i, lam):
    B, S, C = x.shape
    xb = x.reshape(B, S, N_RNN_BLOCKS, RNN_BLOCK)
    r = jax.nn.sigmoid(jnp.einsum('bsnc,ncd->bsnd', xb, w_r).reshape(B, S, C) + b_r)
    i = jax.nn.sigmoid(jnp.einsum('bsnc,ncd->bsnd', xb, w_i).reshape(B, S, C) + b_i)
    log_a = -LRU_C * r.astype(jnp.float32) * jax.nn.softplus(-lam.astype(jnp.float32))
    a = jnp.exp(log_a)
    u = jnp.sqrt(-jnp.expm1(2.0 * log_a)) * (i * x).astype(jnp.float32)

    def combine(left, right):
        a1, b1 = left
        a2, b2 = right
        return a1 * a2, a2 * b1 + b2

    _, h = lax.associative_scan(combine, (a, u), axis=1)
    return h.astype(x.dtype)

def token_mixer(xn, w_in, conv_w, conv_b, w_r, b_r, w_i, b_i, lam, w_pa, w_pb, w_pc, w_o, rel_bias):
    B, S, _ = xn.shape
    proj = xn @ w_in
    (qa, ka, va, qb, kb, vb, qi, ki, wi, xc, yc, gates) = jnp.split(proj, IN_OFFSETS, axis=-1)
    heads_a = lambda z: z.reshape(B, S, N_HEADS_A, HEAD_DIM)
    heads_b = lambda z: z.reshape(B, S, N_HEADS_B, HEAD_DIM)
    y_a = moba_attention(heads_a(qa), heads_a(ka), heads_a(va), rel_bias[:, :N_HEADS_A])
    y_b = dsa_attention(heads_b(qb), heads_b(kb), heads_b(vb),
                        qi.reshape(B, S, N_IDX_HEADS, IDX_DIM), ki, wi, rel_bias[:, N_HEADS_A:])
    y_c = rg_lru(causal_depthwise_conv(xc, conv_w, conv_b), w_r, b_r, w_i, b_i, lam) * jax.nn.gelu(yc)
    g = jax.nn.sigmoid(gates).reshape(B, S, N_BRANCHES, D_MODEL)
    merged = g[:, :, 0] * (y_a @ w_pa) + g[:, :, 1] * (y_b @ w_pb) + g[:, :, 2] * (y_c @ w_pc)
    return merged @ w_o

def squared_relu_mlp(xn, w_up, w_down):
    return jnp.square(jax.nn.relu(xn @ w_up)) @ w_down

def second_inputs(seed: int = 0) -> dict:
    key = jax.random.key(seed)
    ks = jax.random.split(key, 20)
    f32 = jnp.float32
    nrm = lambda k, shape, s: jax.random.normal(k, shape, f32) * s
    u = jax.random.uniform(ks[10], (DEPTH_2, D_RNN), f32, minval=0.9, maxval=0.999)
    a = u ** (1.0 / LRU_C)
    lam = jnp.log(a) - jnp.log1p(-a)
    return {
        "x": nrm(ks[0], (BATCH, SEQ, D_MODEL), 1.0),
        "rel_bias": nrm(ks[1], (N_BUCKETS, N_ATTN_HEADS), 0.5),
        "norm_mix_g": 1.0 + nrm(ks[2], (DEPTH_2, D_MODEL), 0.05),
        "w_in": nrm(ks[3], (DEPTH_2, D_MODEL, D_IN), D_MODEL ** -0.5),
        "conv_w": nrm(ks[4], (DEPTH_2, CONV_WIDTH, D_RNN), CONV_WIDTH ** -0.5),
        "conv_b": nrm(ks[5], (DEPTH_2, D_RNN), 0.02),
        "w_r": nrm(ks[6], (DEPTH_2, N_RNN_BLOCKS, RNN_BLOCK, RNN_BLOCK), RNN_BLOCK ** -0.5),
        "b_r": nrm(ks[7], (DEPTH_2, D_RNN), 0.1),
        "w_i": nrm(ks[8], (DEPTH_2, N_RNN_BLOCKS, RNN_BLOCK, RNN_BLOCK), RNN_BLOCK ** -0.5),
        "b_i": nrm(ks[9], (DEPTH_2, D_RNN), 0.1),
        "lru_lambda": lam,
        "w_pa": nrm(ks[11], (DEPTH_2, D_A, D_MODEL), D_A ** -0.5),
        "w_pb": nrm(ks[12], (DEPTH_2, D_B, D_MODEL), D_B ** -0.5),
        "w_pc": nrm(ks[13], (DEPTH_2, D_RNN, D_MODEL), D_RNN ** -0.5),
        "w_o": nrm(ks[14], (DEPTH_2, D_MODEL, D_MODEL), D_MODEL ** -0.5),
        "norm_mlp_g": 1.0 + nrm(ks[15], (DEPTH_2, D_MODEL), 0.05),
        "w_up": nrm(ks[16], (DEPTH_2, D_MODEL, D_FF), D_MODEL ** -0.5),
        "w_down": nrm(ks[17], (DEPTH_2, D_FF, D_MODEL), D_FF ** -0.5),
        "final_norm_g": 1.0 + nrm(ks[18], (D_MODEL,), 0.05),
    }

def second_block(x, rel_bias, norm_mix_g, w_in, conv_w, conv_b, w_r, b_r, w_i, b_i, lru_lambda,
              w_pa, w_pb, w_pc, w_o, norm_mlp_g, w_up, w_down, final_norm_g):
    for l in range(DEPTH_2):
        x = x + token_mixer(rms_norm_2(x, norm_mix_g[l]), w_in[l], conv_w[l], conv_b[l],
                            w_r[l], b_r[l], w_i[l], b_i[l], lru_lambda[l],
                            w_pa[l], w_pb[l], w_pc[l], w_o[l], rel_bias)
        x = x + squared_relu_mlp(rms_norm_2(x, norm_mlp_g[l]), w_up[l], w_down[l])
    return rms_norm_2(x, final_norm_g)


def setup_inputs(seed=0):
    out = dict(first_inputs(seed))
    for name, value in second_inputs(seed + 1).items():
        if name != "x":
            out[name + "_2"] = value
    return out


def reference(
    x, c, ctx, c_ctx, ada_w, ada_b, norm_g, ret_w_in, ret_w_out, ret_decay_f, ret_decay_b,
    diff_w_in, diff_w_out, diff_lq1, diff_lk1, diff_lq2, diff_lk2, diff_subln, ffn_w_up,
    ffn_conv_w, ffn_conv_b, ffn_w_down, rel_bias_2, norm_mix_g_2, w_in_2, conv_w_2, conv_b_2,
    w_r_2, b_r_2, w_i_2, b_i_2, lru_lambda_2, w_pa_2, w_pb_2, w_pc_2, w_o_2, norm_mlp_g_2,
    w_up_2, w_down_2, final_norm_g_2,
):
    x = first_block(
        x, c, ctx, c_ctx, ada_w, ada_b, norm_g, ret_w_in, ret_w_out, ret_decay_f, ret_decay_b,
        diff_w_in, diff_w_out, diff_lq1, diff_lk1, diff_lq2, diff_lk2, diff_subln, ffn_w_up,
        ffn_conv_w, ffn_conv_b, ffn_w_down,
    )
    return second_block(
        x, rel_bias_2, norm_mix_g_2, w_in_2, conv_w_2, conv_b_2, w_r_2, b_r_2, w_i_2, b_i_2,
        lru_lambda_2, w_pa_2, w_pb_2, w_pc_2, w_o_2, norm_mlp_g_2, w_up_2, w_down_2,
        final_norm_g_2,
    )


_drawn_inputs = setup_inputs


def setup_inputs(seed=0):
    import zlib

    import numpy as np

    out = dict(_drawn_inputs(seed))
    spreads = {}
    factors = {'diff_lq1': 2.963,
     'diff_lk1': 4.29,
     'diff_lq2': 2.922,
     'diff_lk2': 3.953,
     'ffn_conv_b': 5.168,
     'b_r_2': 8.0,
     'b_i_2': 4.522}
    for name, (base, spread) in spreads.items():
        noise = np.random.default_rng([zlib.crc32(name.encode()), seed]).standard_normal(out[name].shape)
        drawn = base * np.exp(spread * noise) if base else spread * noise
        out[name] = __import__('jax').numpy.asarray(drawn.astype(out[name].dtype))
    for name, factor in factors.items():
        out[name] = (out[name] * factor).astype(out[name].dtype)
    return out
```

```python
import math
from contextlib import ExitStack

import numpy as np

import concourse.bass as bass
from concourse import mybir

ALU = mybir.AluOpType
ACT = mybir.ActivationFunctionType
AX = mybir.AxisListType
F32 = mybir.dt.float32
F32R = mybir.dt.float32r
BF16 = mybir.dt.bfloat16

P = 128
D = 1024
KD = D // P
SEQ, CTX = 256, 256
TOK = SEQ + CTX
EPS = 1e-6
NEG = -1e30
RH, RDK, RDV = 4, 256, 512
FH = 2816
FT = FH // P
DH, DD = 8, 64
LAM_INIT = 0.8 - 0.6 * math.exp(-0.3)
HD = 64
NH = 8
TOPK = min(256, SEQ // 4)
MH = 4 * D
MT = MH // P
UNIT = 1024
SLOTS = 4
GRID_W = 64
BUCKETS, MAX_DIST = 32, 128
MARK = -3e38
W2 = {}
_o = 0
for _n, _w in (("qa", 512), ("ka", 512), ("va", 512), ("qb", 512), ("kb", 512), ("vb", 512),
               ("qi", 512), ("kw", 72), ("xc", 512), ("yc", 512), ("g", 3072)):
    W2[_n] = _o
    _o += _w


def rope_tables(width, heads_first):
    half = width // 2
    inv = (10000.0 ** (-np.arange(0, half, 2, dtype=np.float32) / np.float32(half))).astype(np.float32)
    t = np.arange(SEQ)
    cos, sin = np.zeros((SEQ, width), np.float32), np.zeros((SEQ, width), np.float32)
    for n, pos in enumerate((t // GRID_W, t % GRID_W)):
        ang = pos.astype(np.float32)[:, None] * inv[None, :]
        c, s = np.cos(ang), np.sin(ang)
        cos[:, n * half:(n + 1) * half] = np.concatenate([c, c], 1)
        sin[:, n * half:(n + 1) * half] = np.concatenate([-s, s], 1)
    return cos, sin


def shape_constants():
    p = np.arange(P)[:, None].astype(np.float32)
    u = np.arange(512)[None, :].astype(np.float32)
    fwd, bwd = u - p, 384 + p - u
    dist = np.stack([np.maximum(fwd, 0), np.maximum(bwd, 0)], 1)
    mask = np.stack([(fwd >= 0)[:, 0:128], (bwd >= 0)[:, 384:512]], 1).astype(np.float32)
    rc, rs = rope_tables(RDK, True)
    dc, ds = rope_tables(DD, True)
    tile2 = lambda a: a.reshape(2, P, -1).transpose(1, 0, 2).reshape(P, -1)
    t = np.arange(SEQ)
    causal = np.where(t[None, :] <= t[:, None], 0.0, NEG).astype(np.float32)
    dist2 = 255 - np.arange(384)
    n = np.maximum(dist2, 0)
    exact = BUCKETS // 2
    nf = np.maximum(n, 1).astype(np.float32)
    large = exact + (np.log(nf / np.float32(exact)) / np.float32(math.log(MAX_DIST / exact))
                     * np.float32(BUCKETS - exact)).astype(np.int32)
    bucket = np.where(n < exact, n, np.minimum(large, BUCKETS - 1))
    hot = np.zeros((BUCKETS + 1, 384), np.float32)
    hot[bucket, np.arange(384)] = 1.0
    hot[:, dist2 < 0] = 0.0
    hot[BUCKETS, dist2 < 0] = 1.0
    return {
        "k_ident": np.eye(P, dtype=np.float32),
        "k_ret": np.ascontiguousarray(np.concatenate(
            [dist.reshape(P, -1), mask.reshape(P, -1), tile2(rc), tile2(rs)], 1)),
        "k_dif": np.ascontiguousarray(np.concatenate([tile2(dc), tile2(ds)], 1)),
        "k_causal": np.ascontiguousarray(tile2(causal)),
        "k_hot": hot,
    }


FWD_BLOCKS = [(0, 0, 256, 0), (1, 128, 128, 0), (2, 0, 256, 256), (3, 0, 256, 128), (2, 256, 256, 0), (3, 384, 128, 0)]
BWD_BLOCKS = [(0, 0, 128, 384), (1, 0, 256, 256), (2, 0, 256, 128), (3, 0, 256, 0), (2, 256, 128, 384), (3, 256, 256, 256)]


def reads_of(blocks):
    out, o = [[] for _ in range(4)], 0
    for k, q0, w, _ in blocks:
        for q in range(q0, q0 + w, P):
            out[q // P].append((o + q - q0, k))
        o += w
    return out


FWD_READS, BWD_READS = reads_of(FWD_BLOCKS), reads_of(BWD_BLOCKS)
MIXG0, MLPG0, CW0, CB0, BR0, BI0, LAM0, SUB0 = 64, 72, 80, 96, 100, 104, 108, 112


class Track:

    def __init__(self, eng):
        self.eng, self.n, self.i, self.per, self.start, self.last = eng, {}, None, {}, {}, None

    def value(self, sem):
        v = self.n.get(sem.name, 0)
        return v + self.i * self.per[sem.name] if self.per.get(sem.name) else v

    def mark(self, ins, sem):
        ins.then_inc(sem, 1)
        self.n[sem.name] = self.n.get(sem.name, 0) + 1
        self.last = sem

    def settle(self):
        self.eng.wait_ge(self.last, self.value(self.last))

    def enter(self, i, per):
        self.i, self.per, self.start = i, {s.name: c for s, c in per.items()}, dict(self.n)

    def leave(self, rounds):
        for name in set(self.n) | set(self.per):
            grown = self.n.get(name, 0) - self.start.get(name, 0)
            assert grown == self.per.get(name, 0), (name, grown, self.per.get(name, 0))
            self.n[name] = self.n.get(name, 0) + (rounds - 1) * grown
        self.i, self.per = None, {}


class Count:

    def __init__(self):
        self.base, self.i, self.per, self.start = 0, None, 0, 0

    def now(self):
        return self.base if self.i is None else self.base + self.i * self.per

    def next(self):
        v = self.now()
        self.base += 1
        return v

    def enter(self, i, per):
        self.i, self.per, self.start = i, per, self.base

    def leave(self, rounds):
        assert self.base - self.start == self.per, (self.base, self.start, self.per)
        self.base += (rounds - 1) * self.per
        self.i = None


def ds(i, n):
    return slice(i, i + n) if isinstance(i, int) else bass.ds(i, n)


def build(nc, a, out):
    ctx = ExitStack()
    with ctx:
        def sb(name, shape, dt=F32):
            return ctx.enter_context(nc.sbuf_tensor(name, shape, dt))

        def sem(name):
            return ctx.enter_context(nc.semaphore(name))

        mods = nc.dram_tensor("mods", (2, 2, 6 * D), F32, kind="Internal").ap()
        zrow = nc.dram_tensor("zrow", (2 * NH, P, 384), F32, kind="Internal").ap()

        raw = sb("raw", [P, SLOTS, UNIT])
        wh = sb("wh", [P, SLOTS, UNIT], F32R)
        wl = sb("wl", [P, SLOTS, UNIT], F32R)
        uh = sb("uh", [P, KD, TOK], F32R)
        ul = sb("ul", [P, KD, TOK], F32R)
        ah = sb("ah", [P, SLOTS, TOK], F32R)
        al = sb("al", [P, SLOTS, TOK], F32R)
        ch = sb("cvec", [P, KD, P], F32R)
        res = sb("res", [P, 4, D])
        junk = sb("junk", [P, D], BF16)
        ident = sb("ident", [P, P])
        kdif = sb("kdif", [P, 256])
        adat = sb("adat", [64, 2, 512])
        rows = sb("rows", [P, 2, P])
        gcol = sb("gcol", [P, 113])
        fcol = sb("fcol", [P, 104])
        mcol = sb("mcol", [P, 2, 48])
        acol = sb("acol", [P, 2, 8])
        cs = sb("cs", [P, 8, 2])
        st = sb("st", [P, 64])
        lgt = sb("lgt", [P, 5, 12])
        lamt = sb("lamt", [P, 8])
        lamq = sb("lamq", [P, 4, DD])
        epsc = sb("epsc", [P, 1])
        spare = sb("spare", [1, 1])
        ARENA = 79 * 256
        arena = sb("arena", [P, ARENA])
        ps = ctx.enter_context(nc.psum_tensor("ps", [P, 8, 512], F32))

        def area(kb, *shape):
            n = int(np.prod(shape))
            o = int(kb * 256)
            assert o + n <= ARENA, (kb, shape)
            v = arena[:, o:o + n]
            if len(shape) == 1:
                return v
            names = "abcd"[:len(shape)]
            return v.rearrange(f"p ({' '.join(names)}) -> p {' '.join(names)}",
                               **dict(zip(names[1:], shape[1:])))

        yt = area(0, 16, TOK)
        qk = area(32, 4, 512)
        pf, pb = area(32, 1280), area(37, 1280)
        qkt = area(42, 4, 512)
        rtmp = area(42, 512)
        sgb = area(50, 4, 512)
        dec = area(58, 2, 512)
        kret = area(62, 2304)
        vres = res[:, 0:2, :].rearrange("p a (b c) -> p (a b) c", b=2)
        sgf = res[:, 2:4, :].rearrange("p a (b c) -> p (a b) c", b=2)
        kdist = kret[:, 0:1024].rearrange("p (a b) -> p a b", a=2)
        kmask = kret[:, 1024:1280].rearrange("p (a b) -> p a b", a=2)
        kcos = kret[:, 1280:1792].rearrange("p (a b) -> p a b", a=2)
        ksin = kret[:, 1792:2304].rearrange("p (a b) -> p a b", a=2)
        xn = area(44, 4, D)
        ptmp = area(0, 4, 512)
        gb = area(44, 2, D)
        gn = area(52, D)
        ytmp = area(68, 2, D)

        hid = area(0, FT, TOK)
        hid2 = area(0, FT, SEQ)
        hid3 = area(0, MT, SEQ)
        lin = area(60, 2, 2, TOK)
        ah8, al8 = (v[:, :, :].rearrange("p j (k n) -> p (j k) n", k=2) for v in (ah, al))
        dqk = area(0, 4, 512)
        drot = area(8, 2, 512)
        dqt = area(12, 2, SEQ)
        dkt = area(14, 2, TOK)
        dv = area(18, 4, 256)
        dpr = area(22, 2, 4, TOK)
        dpt = area(60, 2, 4, SEQ)
        dy = area(38, 2, 2, P)
        dcos = kdif[:, 0:128].rearrange("p (a b) -> p a b", a=2)
        dsin = kdif[:, 128:256].rearrange("p (a b) -> p a b", a=2)
        qkt5 = area(0, 5, 4, SEQ)
        zt = area(20, 2, 4, SEQ)
        ki2 = area(28, 2, P)
        kit = area(29, SEQ)
        wiw = area(30, 2, 8)
        maskb = area(31, 2, SEQ)
        wk = area(33, 2, SEQ)
        causal = area(35, 2, SEQ)
        xcv = area(37, 4, SEQ)
        gy = area(41, 4, SEQ)
        rt, it = area(45, 4, SEQ), area(49, 4, SEQ)
        la, lt = area(53, 4, SEQ), area(57, 4, SEQ)
        wri = area(61, 2, 4, 64)
        lg = area(53, 2, 6 * SEQ)
        pts = area(65, 6 * SEQ)
        rl = area(71, 8, SEQ)
        g3 = area(53, 3, 2, 2, 512)
        mg, mt = area(0, 4, 512), area(8, 4, 512)
        vab = res[:, 2:4, :].rearrange("p a (b c) -> p (a b) c", b=2)
        hot, tab, zst = area(71, 384)[0:33], area(73, 16)[0:33], area(76, 384)[0:16]
        fout = area(44, 2, D)

        def parts_of(u, nt, half):
            if nt == 4:
                return u[:, half * 4:half * 4 + 4, :], ptmp
            return u[:, :, 0:256], ptmp.rearrange("p b (c n) -> p (b c) n", c=2)

        raw_loaded = [sem(f"raw_loaded{j}") for j in range(SLOTS)]
        hi_done = sem("hi_done")
        lo_done = sem("lo_done")
        ak_hi, ak_lo = sem("ak_hi"), sem("ak_lo")
        unit_used = sem("unit_used")
        turned = sem("turned")
        act_evac = sem("act_evac")
        emptied = sem("emptied")
        act_own = sem("act_own")
        vec_own = sem("vec_own")
        ident_loaded, const_loaded = sem("ident_loaded"), sem("const_loaded")
        kdif_loaded = sem("kdif_loaded")
        eps_set = sem("eps_set")
        rows_loaded = [sem("rows_loaded0"), sem("rows_loaded1")]
        cols_ready = sem("cols_ready")
        silu_c, cvec_hi, cvec_lo = sem("silu_c"), sem("cvec_hi"), sem("cvec_lo")
        bias_loaded, ada_sum, ada_stored = sem("bias_loaded"), sem("ada_sum"), sem("ada_stored")
        x_loaded, decay_loaded = sem("x_loaded"), sem("decay_loaded")
        h_ready = sem("h_ready")
        rms_done = sem("rms_done")
        rstd_ready = sem("rstd_ready")
        xn_act, xn_vec = sem("xn_act"), sem("xn_vec")
        acol_ready = sem("acol_ready")
        u_half = sem("u_half")
        gate_loaded = sem("gate_loaded")
        z_abs, lg_exp, lg_ready = sem("z_abs"), sem("lg_exp"), sem("lg_ready")
        decay_exp = sem("decay_exp")
        qk_rot = sem("qk_rot")
        y_ready = sem("y_ready")
        ffn_lin, ffn_conv = sem("ffn_lin"), sem("ffn_conv")
        hot_loaded, tab_set, zrow_ready, zrow_stored = sem("hot_loaded"), sem("tab_set"), sem("zrow_ready"), sem("zrow_stored")
        z_loaded, z_used = [sem("z_loaded0"), sem("z_loaded1")], sem("z_used")
        mix_loaded, causal_loaded = sem("mix_loaded"), sem("causal_loaded")
        out_stored = sem("out_stored")
        lam_loaded, lam_dots, lam_exp = sem("lam_loaded"), sem("lam_dots"), sem("lam_exp")
        exp_done = sem("exp_done")
        nmax_ready = sem("nmax_ready")
        prob_ready = sem("prob_ready")
        xc_lin, lru_arg, lru_fun, lru_sq, lru_root, yc_ready, yc_hi = (sem(n) for n in (
            "xc_lin", "lru_arg", "lru_fun", "lru_sq", "lru_root", "yc_ready", "yc_hi"))
        yc_lo = sem("yc_lo")
        merged = sem("merged")
        gain_loaded, out_ready = sem("gain_loaded"), sem("out_ready")

        block = ctx.enter_context(nc.Block())


        S_RETO = 4 + 6 * RH
        S_UP0 = S_RETO + 4
        S_DIF = S_UP0 + 23 + 6
        S_UP1 = S_DIF + 8 + 2
        S_MIX = S_UP1 + 11 + 6
        S_MUP = S_MIX + 16 + 3 + 2

        @block.sync
        def _(sp):
            S = Count()

            def load(parts):
                s = S.next()
                for j in range(SLOTS):
                    if not (isinstance(s, int) and s == 0):
                        sp.wait_ge(lo_done, s * SLOTS + (j - SLOTS + 1))
                    pieces = parts(j)
                    for dst, src in pieces:
                        sp.dma_start(dst, src).then_inc(raw_loaded[j], 32 // len(pieces))

            def cols(w, c0, n=512):
                v = w.rearrange("(j k p) n -> j p k n", k=2, p=P)
                return lambda j: [(raw[:, j, 0:2 * n].rearrange("p (k n) -> p k n", k=2),
                                   v[j][:, :, ds(c0, n)])]

            def pair(w, c0, c1):
                v = w.rearrange("(j k p) n -> j p k n", k=2, p=P)
                return lambda j: [(raw[:, j, :].rearrange("p (k z n) -> p k z n", k=2, z=2)[:, :, z, :],
                                   v[j][:, :, ds(c, 256)]) for z, c in enumerate((c0, c1))]

            def down(w, k0):
                v = w.rearrange("(k p) n -> p k n", p=P)
                return lambda j: [(raw[:, j, :], v[:, k0 + j, :])]

            def down_half(w, k0):
                v = w.rearrange("(k p) n -> p k n", p=P)
                return lambda j: [(raw[:, j, 0:512], v[:, k0 + j // 2, (j % 2) * 512:(j % 2) * 512 + 512])]

            for c in range(4):
                load(cols(a["ada_w"][0], c * 512))
            w = a["ret_w_in"][0]
            kq, kk, kv = RH * RDK, 2 * RH * RDK, RH * RDV
            with sp.Fori(0, RH) as h:
                S.enter(h, 6)
                load(pair(w, h * RDK, h * RDK + kq))
                load(cols(w, h * RDV + kk))
                load(cols(w, h * RDV + (kk + kv)))
                load(cols(w, h * RDV + (kk + 2 * kv)))
                load(cols(a["ada_w"][0], h * 1024 + 4 * 512))
                load(cols(a["ada_w"][0], h * 1024 + 5 * 512))
            S.leave(RH)
            with sp.Fori(0, RH) as i:
                S.enter(i, 1)
                load(down(a["ret_w_out"][0], i * 4))
            S.leave(RH)
            up = a["ffn_w_up"][0]
            with sp.Fori(0, 5) as i:
                S.enter(i, 4)
                load(pair(up, i * 512, i * 512 + FH))
                load(pair(up, i * 512 + 256, i * 512 + (256 + FH)))
                load(cols(a["ada_w"][1], i * 1024))
                load(cols(a["ada_w"][1], i * 1024 + 512))
            S.leave(5)
            load(pair(up, 2560, 2560 + FH))
            load(cols(a["ada_w"][1], 5120))
            load(cols(a["ada_w"][1], 5632))
            with sp.Fori(0, 5) as i:
                S.enter(i, 1)
                load(down(a["ffn_w_down"][0], i * 4))
            S.leave(5)
            load(down_half(a["ffn_w_down"][0], 20))
            w = a["diff_w_in"][0]
            with sp.Fori(0, 4) as i:
                S.enter(i, 2)
                load(pair(w, i * 256, i * 256 + D))
                load(cols(w, i * 256 + 2 * D, 256))
            S.leave(4)
            with sp.Fori(0, 2) as i:
                S.enter(i, 1)
                load(down(a["diff_w_out"][0], i * 4))
            S.leave(2)
            up = a["ffn_w_up"][1]
            with sp.Fori(0, 11) as i:
                S.enter(i, 1)
                load(pair(up, i * 256, i * 256 + FH))
            S.leave(11)
            with sp.Fori(0, 5) as i:
                S.enter(i, 1)
                load(down(a["ffn_w_down"][1], i * 4))
            S.leave(5)
            load(down_half(a["ffn_w_down"][1], 20))
            w = a["w_in_2"][0]
            with sp.Fori(0, 7) as i:
                S.enter(i, 1)
                load(cols(w, i * 512))
            S.leave(7)
            load(cols(w, W2["kw"], 72))
            with sp.Fori(0, 8) as i:
                S.enter(i, 1)
                load(cols(w, i * 512 + W2["xc"]))
            S.leave(8)
            for name in ("w_pa_2", "w_pb_2", "w_pc_2"):
                load(down(a[name][0], 0))
            with sp.Fori(0, 2) as i:
                S.enter(i, 1)
                load(down(a["w_o_2"][0], i * 4))
            S.leave(2)
            with sp.Fori(0, 8) as i:
                S.enter(i, 1)
                load(cols(a["w_up_2"][0], i * 512))
            S.leave(8)
            with sp.Fori(0, 8) as i:
                S.enter(i, 1)
                load(down(a["w_down_2"][0], i * 4))
            S.leave(8)

        @block.tensor
        def _(pe):
            S, G, A = Count(), Count(), Count()

            def open_group():
                half = 4 * (G.base % 2)
                g = G.next()
                if not (isinstance(g, int) and g < 2):
                    pe.wait_ge(emptied, g - 1)
                return half

            def three(o, lh, ll, rh, rl, first, last):
                pe.matmul(o, lh, rh, start=first, stop=False)
                pe.matmul(o, lh, rl, start=False, stop=False)
                return pe.matmul(o, ll, rh, start=False, stop=last)

            def units():
                s = S.next()
                for j in range(SLOTS):
                    pe.wait_ge(lo_done, s * SLOTS + (j + 1))
                    yield j

            def step_tokens(tiles, n=512, skip=lambda t: 0):
                hb = open_group()
                for j in units():
                    for k in range(2):
                        for t in tiles:
                            c = skip(t)
                            rh, rl = (w[:, j, k * n + c:(k + 1) * n] for w in (wh, wl))
                            f = 2 * j + k
                            mm = three(ps[:, hb + t, c:n], uh[:, f, t * P:(t + 1) * P], ul[:, f, t * P:(t + 1) * P],
                                       rh, rl, f == 0, f == KD - 1)
                    mm.then_inc(unit_used, 1)

            def step_features(n):
                hb = open_group()
                for j in units():
                    for k in range(2):
                        for m in range(4):
                            f = 2 * j + k
                            lh, ll = (w[:, j, k * 512 + m * P:k * 512 + (m + 1) * P] for w in (wh, wl))
                            mm = three(ps[:, hb + m, 0:n], lh, ll, uh[:, f, 0:n], ul[:, f, 0:n],
                                       f == 0, f == KD - 1)
                    mm.then_inc(unit_used, 1)

            def step_ada():
                hb = open_group()
                for j in units():
                    for k in range(2):
                        f = 2 * j + k
                        pe.matmul(ps[:, hb, :], ch[:, f, :], wh[:, j, k * 512:(k + 1) * 512],
                                  start=f == 0, stop=False)
                        mm = pe.matmul(ps[:, hb, :], ch[:, f, :], wl[:, j, k * 512:(k + 1) * 512],
                                       start=False, stop=f == KD - 1)
                    mm.then_inc(unit_used, 1)

            def step_down(bank0, tiles, first, last, late=True, kt=None, half=False, src=None):
                if late:
                    x = A.next()
                for j in units():
                    if late:
                        pe.wait_ge(ak_lo, x * SLOTS + (j + 1))
                    for t in tiles:
                        if kt is None:
                            lh, ll = ah[:, j, t * P:(t + 1) * P], al[:, j, t * P:(t + 1) * P]
                        else:
                            lh, ll = (v[:, kt + j, t * P:(t + 1) * P] for v in (src or (ah8, al8)))
                        for c in ((j % 2,) if half else (0, 1)):
                            w0 = 0 if half else c * 512
                            mm = three(ps[:, bank0(t) + c, :], lh, ll, wh[:, j, w0:w0 + 512], wl[:, j, w0:w0 + 512],
                                       first and j == 0, last and (j >= 2 if half else j == SLOTS - 1))
                    mm.then_inc(unit_used, 1)

            def turn_rows(batch, n, loads):
                pe.wait_ge(rows_loaded[batch % 2], 16 * loads)
                hb = open_group()
                pe.transpose(ps[:, hb, 0:n], rows[0:n, batch % 2, :], ident[0:n, 0:n]).then_inc(turned, 1)

            def turn_normed(nt, norms):
                pe.wait_ge(xn_act, norms)
                pe.wait_ge(xn_vec, norms)
                if nt == 4:
                    for half in range(2):
                        hb = open_group()
                        for b in range(4):
                            for t in range(4):
                                f = half * 4 + b
                                mm = pe.transpose(ps[:, hb + b, t * P:(t + 1) * P], xn[:, t, f * P:(f + 1) * P], ident[:, :])
                        mm.then_inc(turned, 1)
                else:
                    hb = open_group()
                    for f in range(KD):
                        for t in range(2):
                            c = (f % 2) * 256 + t * P
                            mm = pe.transpose(ps[:, hb + f // 2, c:c + P], xn[:, t, f * P:(f + 1) * P], ident[:, :])
                    mm.then_inc(turned, 1)

            def all_emptied():
                pe.wait_ge(emptied, G.now())

            pe.wait_ge(ident_loaded, 16)
            turn_rows(0, 104, 4)
            turn_rows(1, 113, 9)
            pe.wait_ge(cvec_lo, 1)
            for _ in range(4):
                step_ada()
            pe.wait_ge(hot_loaded, 32)
            pe.wait_ge(tab_set, 1)
            hb = open_group()
            pe.matmul(ps[0:16, hb, 0:384], tab, hot, start=True, stop=True).then_inc(turned, 1)
            turn_rows(2, 32, 6)
            turn_normed(4, 1)
            all_emptied()

            def attend(v0, reads):
                hb = open_group()
                for t, blocks in enumerate(reads):
                    for n, (c, k) in enumerate(blocks):
                        mm = pe.matmul(ps[:, hb + t, :], v0[:, c:c + P], vres[:, k, :],
                                       start=n == 0, stop=n == len(blocks) - 1)
                mm.then_inc(turned, 1)

            with pe.Fori(0, RH) as h:
                S.enter(h, 6)
                G.enter(h, 12)
                step_tokens(range(4))
                step_tokens(range(4))
                pe.wait_ge(qk_rot, h + 1)
                hb = open_group()
                for b in range(4):
                    for t in range(4):
                        mm = pe.transpose(ps[:, hb + b, t * P:(t + 1) * P], qk[:, t, b * P:(b + 1) * P], ident[:, :])
                mm.then_inc(turned, 1)
                step_tokens(range(4))
                pe.wait_ge(emptied, G.now() - 1)
                hb = open_group()
                for k in range(4):
                    n = 256 if k < 2 else 512
                    for f in range(2):
                        mm = pe.matmul(ps[:, hb + k, 0:n], qkt[:, 2 + f, k * P:(k + 1) * P], qkt[:, f, 0:n],
                                       start=f == 0, stop=f == 1)
                mm.then_inc(turned, 1)
                step_tokens(range(4))
                pe.wait_ge(emptied, G.now() - 1)
                attend(pf, FWD_READS)
                attend(pb, BWD_READS)
                step_ada()
                step_ada()
                pe.wait_ge(y_ready, h + 1)
                for pairs in range(2):
                    hb = open_group()
                    for b in range(2):
                        for t in range(4):
                            f = 2 * pairs + b
                            mm = pe.transpose(ps[:, hb + b, t * P:(t + 1) * P], sgf[:, t, f * P:(f + 1) * P], ident[:, :])
                    mm.then_inc(turned, 1)
            S.leave(RH)
            G.leave(RH)


            def project(nt, steps, late=True, src=None, half_last=False, kt=0):
                halves = [open_group() for _ in range(nt // 2)]
                bank0 = lambda t: halves[t // 2] + 2 * (t % 2)
                tiles = range(nt)
                k = lambda s: None if late else kt + 4 * s
                step_down(bank0, tiles, True, steps == 1, late, k(0))
                if steps > 2 and late:
                    with pe.Fori(0, steps - 2) as i:
                        S.enter(i, 1)
                        A.enter(i, 1)
                        step_down(bank0, tiles, False, False)
                    S.leave(steps - 2)
                    A.leave(steps - 2)
                if steps > 1:
                    step_down(bank0, tiles, False, True, late, k(steps - 1), half_last)

            project(4, 4)
            turn_rows(3, 96, 11)
            turn_normed(4, 2)
            all_emptied()
            with pe.Fori(0, 5) as i:
                S.enter(i, 4)
                G.enter(i, 4)
                step_features(TOK)
                step_features(TOK)
                step_ada()
                step_ada()
            S.leave(5)
            G.leave(5)
            step_features(TOK)
            step_ada()
            step_ada()
            project(4, 6, half_last=True)
            turn_rows(4, 88, 8)
            turn_rows(5, 96, 13)
            turn_normed(4, 3)
            all_emptied()

            with pe.Fori(0, DH // 2) as i:
                S.enter(i, 2)
                G.enter(i, 10)
                step_tokens(range(4), 512, lambda t: 0 if t < 2 else 256)
                step_tokens(range(4), 256)
                pe.wait_ge(qk_rot, i + (RH + 1))
                hb = open_group()
                for h in range(2):
                    for t in range(2):
                        pe.transpose(ps[:, hb, h * SEQ + t * P:h * SEQ + (t + 1) * P], dqk[:, t, h * P:(h + 1) * P], ident[:, :])
                    for t in range(4):
                        mm = pe.transpose(ps[:, hb + 1 + h, t * P:(t + 1) * P],
                                          dqk[:, t, 256 + h * P:256 + (h + 1) * P], ident[:, :])
                mm.then_inc(turned, 1)
                pe.wait_ge(emptied, G.now())
                for h in range(2):
                    hb = open_group()
                    for c in range(2):
                        for t in range(2):
                            r = slice(64 * c, 64 * c + 64)
                            mm = pe.matmul(ps[:, hb + 2 * c + t, :], dqt[r, h, t * P:(t + 1) * P], dkt[r, h, :],
                                           start=True, stop=True)
                    mm.then_inc(turned, 1)
                for h in range(2):
                    pe.wait_ge(prob_ready, i * 2 + (h + 1))
                    hb = open_group()
                    for k in range(4):
                        for t in range(2):
                            c = (k % 2) * SEQ + t * P
                            mm = pe.transpose(ps[:, hb + k // 2, c:c + P], dpr[:, h, t, k * P:(k + 1) * P], ident[:, :])
                    mm.then_inc(turned, 1)
                for h in range(2):
                    pe.wait_ge(emptied, G.now() - 1)
                    hb = open_group()
                    for t in range(2):
                        for k in range(4):
                            mm = pe.matmul(ps[:, hb, t * P:(t + 1) * P], dpt[:, h, k, t * P:(t + 1) * P],
                                           dv[:, k, h * P:(h + 1) * P], start=k == 0, stop=k == 3)
                    mm.then_inc(turned, 1)
                pe.wait_ge(emptied, G.now())
                hb = open_group()
                for h in range(2):
                    for t in range(2):
                        mm = pe.transpose(ps[:, hb, h * SEQ + t * P:h * SEQ + (t + 1) * P], dy[:, h, t, :], ident[:, :])
                mm.then_inc(turned, 1)
            S.leave(DH // 2)
            G.leave(DH // 2)
            all_emptied()
            project(2, 2, late=False)
            turn_normed(2, 4)
            all_emptied()
            with pe.Fori(0, 5) as i:
                S.enter(i, 2)
                G.enter(i, 2)
                step_features(SEQ)
                step_features(SEQ)
            S.leave(5)
            G.leave(5)
            step_features(SEQ)
            project(2, 6, half_last=True)
            turn_normed(2, 5)
            all_emptied()

            for kind in "fftfftf":
                if kind == "f":
                    step_features(SEQ)
                else:
                    step_tokens(range(2))
            step_tokens(range(2), 72)
            step_features(SEQ)
            step_features(SEQ)
            all_emptied()
            hb = open_group()
            for t in range(2):
                mm = pe.transpose(ps[:, hb, t * P:(t + 1) * P], ki2[:, t, :], ident[:, :])
            mm.then_inc(turned, 1)
            pe.wait_ge(mix_loaded, 64)
            hb = open_group()
            for z in range(2):
                for b in range(8):
                    r, m = slice(64 * (b % 2), 64 * (b % 2) + 64), b // 2
                    mm = pe.matmul(ps[r, hb + 2 * z + m // 2, (m % 2) * SEQ:(m % 2 + 1) * SEQ], wri[r, z, m, :],
                                   xcv[r, m, :], start=True, stop=True)
            mm.then_inc(turned, 1)

            def head_rows(h):
                return slice(64 * (h % 2), 64 * (h % 2) + 64), h // 2

            all_emptied()
            for t, n in ((1, SEQ), (0, P)):
                hb = open_group()
                for h in range(8):
                    r, m = head_rows(h)
                    c = ((h % 2) * 4 + h // 2) * n
                    mm = pe.matmul(ps[:, hb + c // 512, c % 512:c % 512 + n], qkt5[r, 4, m, t * P:(t + 1) * P],
                                   kit[r, 0:n], start=True, stop=True)
                mm.then_inc(turned, 1)

            def attention(z, g):
                hb = open_group()
                for x in range(4):
                    r, m = head_rows(4 * g + x)
                    i = x // 2
                    pe.matmul(ps[:, hb + x % 2, i * SEQ:(i + 1) * SEQ], qkt5[r, 2 * z, m, P:SEQ],
                              qkt5[r, 2 * z + 1, m, :], start=True, stop=True)
                    mm = pe.matmul(ps[:, hb + 2 + x % 2, i * P:(i + 1) * P], qkt5[r, 2 * z, m, 0:P],
                                   qkt5[r, 2 * z + 1, m, 0:P], start=True, stop=True)
                mm.then_inc(turned, 1)
                n = 2 * z + g
                pe.wait_ge(prob_ready, DH + n + 1)
                e = lg[:, g, :]
                hb = open_group()
                for x in range(4):
                    o = (x % 2) * SEQ
                    pe.transpose(ps[:, hb + x // 2, o:o + P], e[:, 1024 + x * P:1024 + (x + 1) * P], ident[:, :])
                    pe.transpose(ps[:, hb + x // 2, o + P:o + SEQ], e[:, x * SEQ:x * SEQ + P], ident[:, :])
                    mm = pe.transpose(ps[:, hb + 2, x * P:(x + 1) * P], e[:, x * SEQ + P:(x + 1) * SEQ], ident[:, :])
                mm.then_inc(turned, 1)
                pe.wait_ge(emptied, G.now())
                hb = open_group()
                for x in range(4):
                    h = 4 * g + x
                    r = head_rows(h)[0]
                    o = (x // 2) * SEQ
                    i = (x % 2) * 2 + x // 2
                    pe.matmul(ps[r, hb, o:o + SEQ], vab[:, 2 * z, h * HD:(h + 1) * HD], pts[:, i * SEQ:(i + 1) * SEQ],
                              start=True, stop=False)
                    mm = pe.matmul(ps[r, hb, o + P:o + SEQ], vab[:, 2 * z + 1, h * HD:(h + 1) * HD],
                                   pts[:, 1024 + i * P:1024 + (i + 1) * P], start=False, stop=True)
                mm.then_inc(turned, 1)

            for z in range(2):
                for g in range(2):
                    attention(z, g)
            with pe.Fori(0, 3) as i:
                S.enter(i, 2)
                G.enter(i, 2)
                step_tokens(range(2))
                step_tokens(range(2))
            S.leave(3)
            G.leave(3)
            pe.wait_ge(yc_lo, 1)
            for lh8, ll8, kt in ((ah8, al8, 0), (ah8, al8, 4), (uh[:, :, SEQ:TOK], ul[:, :, SEQ:TOK], 0)):
                hb = open_group()
                step_down(lambda t: hb + 2 * t, range(2), True, True, late=False, kt=kt, src=(lh8, ll8))
            pe.wait_ge(merged, 1)
            hb = open_group()
            for f in range(KD):
                for t in range(2):
                    c = (f % 2) * SEQ + t * P
                    mm = pe.transpose(ps[:, hb + f // 2, c:c + P], mg[:, 2 * t + f // 4, (f % 4) * P:(f % 4 + 1) * P], ident[:, :])
            mm.then_inc(turned, 1)
            all_emptied()
            hb = open_group()
            for n in range(2):
                step_down(lambda t: hb + 2 * t, range(2), n == 0, n == 1, late=False, kt=4 * n,
                          src=(uh[:, :, SEQ:TOK], ul[:, :, SEQ:TOK]))
            turn_normed(2, 6)
            all_emptied()
            with pe.Fori(0, 4) as i:
                S.enter(i, 2)
                G.enter(i, 2)
                step_features(SEQ)
                step_features(SEQ)
            S.leave(4)
            G.leave(4)
            project(2, 8)

        @block.scalar
        def _(act):
            T = Track(act)
            W, S, Q = Count(), Count(), Count()
            par = Count()
            A = Count()
            norms = [0]

            def split(size=UNIT):
                s = W.next()
                for j in range(SLOTS):
                    act.wait_ge(raw_loaded[j], s * 32 + 32)
                    if not (isinstance(s, int) and s == 0):
                        act.wait_ge(unit_used, s * SLOTS + (j - SLOTS + 1))
                    T.mark(act.activation(wh[:, j, 0:size], raw[:, j, 0:size], ACT.Copy), hi_done)

            def step_full():
                half = 4 * (par.base % 2)
                par.next()
                T.settle()
                act.wait_ge(unit_used, S.next() * SLOTS + SLOTS)
                return half

            def group_full():
                half = 4 * (par.base % 2)
                par.next()
                T.settle()
                act.wait_ge(turned, Q.next() + 1)
                return half

            def skip_group():
                par.next()
                Q.next()

            def read_ada():
                hb = step_full()
                if not (isinstance(par.now(), int) and S.now() == 1):
                    act.wait_ge(ada_stored, 16 * ada.now())
                ada.next()
                T.mark(act.activation(adat[:, 1, :], ps[64:128, hb, :], ACT.Copy), act_evac)

            ada = Count()

            def rms(tiles, src, width, cols, waits=None):
                for t in tiles:
                    if waits:
                        waits(t)
                    if T.last is not None:
                        T.settle()
                    T.mark(act.activation(junk[:, 0:width], src(t), ACT.Square, scale=float(width) ** -0.5,
                                          accum_out=st[:, cols[0] + t:cols[0] + t + 1]), act_own)
                T.settle()
                n = len(tiles)
                return act.activation(st[:, cols[1]:cols[1] + n], st[:, cols[0]:cols[0] + n], ACT.Sqrt,
                                      bias=epsc[:, 0:1])

            def prep(nt):
                norms[0] += 1
                T.mark(rms(range(nt), lambda t: res[:, t, :], D, (0, 4)), rms_done)
                act.wait_ge(rstd_ready, norms[0])
                for t in range(1, nt, 2):
                    ins = act.activation(xn[:, t, :], res[:, t, :], ACT.Copy, scale=st[:, 8 + t:9 + t])
                    T.mark(ins, xn_act if t == nt - 1 else act_own)
                act.wait_ge(acol_ready, norms[0])
                for half in range(nt // 2):
                    hb = group_full()
                    if half:
                        act.wait_ge(emptied, par.now() - 1)
                    for b in range(2):
                        for c in range(2):
                            f, k = (half * 4 + b, c) if nt == 4 else (2 * b + c, 0)
                            T.mark(act.activation(ptmp[:, b, c * 256:(c + 1) * 256], ps[:, hb + b, c * 256:(c + 1) * 256],
                                                  ACT.Identity, scale=acol[:, k, f:f + 1], bias=shift(k, f)), act_own)
                    act.wait_ge(u_half, halves[0] + 1)
                    halves[0] += 1
                    T.settle()
                    T.mark(act.activation(*parts_of(uh, nt, half), ACT.Copy), act_evac)

            shift0 = [0]
            halves = [0]

            def shift(k, f):
                return 0.0 if shift0[0] is None else mcol[:, k, shift0[0] + f:shift0[0] + f + 1]

            split()
            skip_group()
            skip_group()
            act.wait_ge(cols_ready, 1)
            T.mark(act.activation(cs[:, :, :].rearrange("p f c -> p c f"),
                                  fcol[:, 0:16].rearrange("p (c f) -> p c f", c=2), ACT.Silu), silu_c)
            T.settle()
            T.mark(act.activation(ch[:, :, 0:64].rearrange("p f (c n) -> p f c n", c=2),
                                  cs[:, :, :].unsqueeze(3).to_broadcast([P, 8, 2, 32]), ACT.Copy), cvec_hi)
            for c in range(4):
                split()
                read_ada()
            skip_group()
            skip_group()
            act.wait_ge(eps_set, 1)
            act.wait_ge(x_loaded, 32)
            act.wait_ge(z_abs, 1)
            T.mark(act.activation(lgt[:, 2, :], lgt[:, 1, :], ACT.Exp, scale=-1.0), lg_exp)
            act.wait_ge(x_loaded, 32)
            prep(4)

            act.wait_ge(const_loaded, 16)
            act.wait_ge(lg_ready, 1)
            with act.Fori(0, RH) as h:
                for c, n in ((W, 6), (S, 6), (Q, 6), (par, 12), (ada, 2)):
                    c.enter(h, n)
                T.enter(h, {hi_done: 24, act_evac: 11, act_own: 9, decay_exp: 1})
                split()
                hb = step_full()
                T.mark(act.activation(qk[:, 2:4, :], ps[:, hb + 2:hb + 4, :], ACT.Copy), act_evac)
                split()
                hb = step_full()
                T.mark(act.activation(vres, ps[:, hb:hb + 4, :], ACT.Copy), act_evac)
                for z in range(2):
                    T.mark(act.activation(dec[:, z, :], kdist[:, z, :], ACT.Exp,
                                          scale=lgt[:, 4, ds(h + 4 * z, 1)]), (act_own, decay_exp)[z])
                hb = group_full()
                T.mark(act.activation(qkt[:, 0:2, :], ps[:, hb:hb + 2, :], ACT.Copy), act_evac)
                split()
                hb = step_full()
                T.mark(act.activation(sgf, ps[:, hb:hb + 4, :], ACT.Silu), act_evac)
                skip_group()
                split()
                hb = step_full()
                T.mark(act.activation(sgb, ps[:, hb:hb + 4, :], ACT.Silu), act_evac)
                for z in range(2):
                    hb = group_full()
                    T.mark(rms(range(4), lambda t: ps[:, hb + t, :], RDV, (16 + 4 * z, 24 + 4 * z)), act_evac)
                split()
                read_ada()
                split()
                read_ada()
                for pairs in range(2):
                    hb = group_full()
                    T.mark(act.activation(yt[:, h * 4 + 2 * pairs, :], ps[:, hb, :], ACT.Copy), act_evac)
            for c in (W, S, Q, par, ada):
                c.leave(RH)
            T.leave(RH)


            def split_late(src, n):
                A.next()
                for j in range(SLOTS):
                    T.mark(act.activation(ah[:, j, 0:n], src(j), ACT.Copy), ak_hi)

            def project(nt, steps, source, after, last_size=UNIT, next_size=UNIT):
                n = nt * P
                act.wait_ge(emptied, after)
                T.settle()
                split_late(lambda j: source(j), n)
                if steps > 2:
                    with act.Fori(0, steps - 2) as i:
                        W.enter(i, 1)
                        A.enter(i, 1)
                        T.enter(i, {hi_done: 4, ak_hi: 4})
                        split()
                        split_late(lambda j: source(i * 4 + (4 + j)), n)
                    W.leave(steps - 2)
                    A.leave(steps - 2)
                    T.leave(steps - 2)
                split(last_size)
                k0 = 4 * (steps - 1)
                split_late(lambda j: source(k0 + (j // 2 if last_size < UNIT else j)), n)
                split(next_size)
                S.base += steps
                out_rms(nt)

            def out_rms(nt):
                halves = [4 * ((par.base + z) % 2) for z in range(nt // 2)]
                par.base += nt // 2
                act.wait_ge(unit_used, S.now() * SLOTS)
                T.mark(rms(range(nt), lambda t: ps[:, halves[t // 2] + 2 * (t % 2):halves[t // 2] + 2 * (t % 2) + 2, :],
                           D, (0, 4)), act_evac)
                projections[0] += 1

            projections = [0]
            F = Count()

            def read_ffn(ft, n):
                p = par.base % 2
                hb = step_full()
                for m in range(2):
                    T.mark(act.activation(lin[:, p, m, 0:n], ps[:, hb + 2 + m, 0:n], ACT.Identity,
                                          scale=fcol[:, ds(ft + (16 + FT + m), 1)], bias=fcol[:, ds(ft + (16 + 3 * FT + m), 1)]),
                           (act_own, ffn_lin)[m])
                act.wait_ge(ffn_conv, F.next() + 1)
                T.mark(act.activation(lin[:, p, :, 0:n], lin[:, p, :, 0:n], ACT.Silu), act_evac)

            def wait_residual():
                act.wait_ge(h_ready, projections[0])

            project(4, 4, lambda k: yt[:, k, :], par.now())
            skip_group()
            wait_residual()
            shift0[0] = 24
            prep(4)
            with act.Fori(0, 5) as i:
                for c, n in ((W, 4), (S, 4), (par, 4), (ada, 2), (F, 2)):
                    c.enter(i, n)
                T.enter(i, {hi_done: 16, act_evac: 4, act_own: 2, ffn_lin: 2})
                split()
                read_ffn(i * 4, TOK)
                split()
                read_ffn(i * 4 + 2, TOK)
                split()
                read_ada()
                split()
                read_ada()
            for c in (W, S, par, ada, F):
                c.leave(5)
            T.leave(5)
            split()
            read_ffn(20, TOK)
            split()
            read_ada()
            split()
            read_ada()
            project(4, 6, lambda k: hid[:, k, :], par.now(), 512)
            skip_group()
            skip_group()
            wait_residual()
            shift0[0] = 0
            prep(4)

            act.wait_ge(lam_dots, 1)
            T.mark(act.activation(lamt[:, 2:4], lamt[:, 0:2], ACT.Exp), lam_exp)
            with act.Fori(0, DH // 2) as i:
                for c, n in ((W, 2), (S, 2), (Q, 8), (par, 10)):
                    c.enter(i, n)
                T.enter(i, {hi_done: 8, act_evac: 10, act_own: 11})
                split(512)
                hb = step_full()
                T.mark(act.activation(dqk[:, 2:4, 256:512], ps[:, hb + 2:hb + 4, 256:512], ACT.Copy), act_evac)
                split()
                hb = step_full()
                T.mark(act.activation(dv[:, 0:2, :], ps[:, hb:hb + 2, 0:256], ACT.Copy), act_evac)
                hb = group_full()
                T.mark(act.activation(dqt, ps[:, hb, :].rearrange("p (h n) -> p h n", h=2), ACT.Copy), act_own)
                T.mark(act.activation(dkt[:, 0, :], ps[:, hb + 1, :], ACT.Copy), act_evac)
                for h in range(2):
                    hb = group_full()
                    act.wait_ge(nmax_ready, i * 2 + (h + 1))
                    for b in range(4):
                        T.mark(act.activation(dpr[:, h, b, :], ps[:, hb + b, :], ACT.Exp, scale=DD ** -0.5,
                                              bias=st[:, 40 + 4 * h + b:41 + 4 * h + b],
                                              accum_out=st[:, 48 + 4 * h + b:49 + 4 * h + b]),
                               act_evac if b == 3 else act_own)
                for h in range(2):
                    hb = group_full()
                    T.mark(act.activation(dpt[:, h, 0:2, :], ps[:, hb, :].rearrange("p (k n) -> p k n", k=2), ACT.Copy), act_evac)
                for h in range(2):
                    hb = group_full()
                    T.mark(rms(range(2), lambda t: ps[:, hb, t * P:(t + 1) * P], P, (16 + 2 * h, 20 + 2 * h)), act_evac)
                hb = group_full()
                T.mark(act.activation(ah8[:, ds(i * 2, 2), :], ps[:, hb, :].rearrange("p (h n) -> p h n", h=2), ACT.Copy,
                                      scale=lamt[:, 5:6]), act_evac)
            for c in (W, S, Q, par):
                c.leave(DH // 2)
            T.leave(DH // 2)
            split()
            split()
            S.base += 2
            out_rms(2)
            wait_residual()
            shift0[0] = 24
            prep(2)
            with act.Fori(0, 5) as i:
                for c, n in ((W, 2), (S, 2), (par, 2), (F, 2)):
                    c.enter(i, n)
                T.enter(i, {hi_done: 8, act_evac: 2, act_own: 2, ffn_lin: 2})
                split()
                read_ffn(i * 4, SEQ)
                split()
                read_ffn(i * 4 + 2, SEQ)
            for c in (W, S, par, F):
                c.leave(5)
            T.leave(5)
            split()
            read_ffn(20, SEQ)
            project(2, 6, lambda k: hid2[:, k, :], par.now(), 512)
            wait_residual()
            shift0[0] = None
            prep(2)

            def read_half(dst):
                hb = step_full()
                T.mark(act.activation(dst[:, 0:2, :], ps[:, hb:hb + 2, 0:SEQ], ACT.Copy), act_evac)

            def read_values(dst):
                hb = step_full()
                T.mark(act.activation(dst, ps[:, hb, :], ACT.Copy), act_evac)

            split()
            read_half(qkt5[:, 0])
            split()
            read_half(qkt5[:, 1])
            split()
            read_values(vab[:, 0, :])
            split()
            read_half(qkt5[:, 2])
            split()
            read_half(qkt5[:, 3])
            split()
            read_values(vab[:, 2, :])
            split(144)
            read_half(qkt5[:, 4])
            split()
            hb = step_full()
            for t in range(2):
                T.mark(act.activation(ki2[:, t, :].rearrange("p (z n) -> p z n", z=2),
                                      ps[:, hb + t, 0:64].unsqueeze(1).to_broadcast([P, 2, 64]), ACT.Copy), (act_own, act_evac)[t])
            split()
            hb = step_full()
            for m in range(4):
                T.mark(act.activation(xcv[:, m, :], ps[:, hb + m, 0:SEQ], ACT.Identity,
                                      scale=gcol[:, CW0 + 12 + m:CW0 + 13 + m], bias=gcol[:, CB0 + m:CB0 + m + 1]),
                       xc_lin if m == 3 else act_own)
            split()
            hb = step_full()
            T.mark(act.activation(gy, ps[:, hb:hb + 4, 0:SEQ], ACT.Gelu_apprx_tanh), act_evac)
            skip_group()
            hb = group_full()
            for z, (dst, b0) in enumerate(((rt, BR0), (it, BI0))):
                for m in range(4):
                    T.mark(act.activation(dst[:, m, :], ps[:, hb + 2 * z + m // 2, (m % 2) * SEQ:(m % 2 + 1) * SEQ],
                                          ACT.Sigmoid, bias=gcol[:, b0 + m:b0 + m + 1]),
                           act_evac if (z, m) == (1, 3) else act_own)
            act.wait_ge(lru_arg, 1)
            T.mark(act.activation(la, rt, ACT.Exp, scale=-1.0), act_own)
            T.mark(act.activation(lt, rt, ACT.Tanh), lru_fun)
            act.wait_ge(lru_sq, 1)
            T.mark(act.activation(lt, lt, ACT.Sqrt), lru_root)
            act.wait_ge(yc_ready, 1)
            T.mark(act.activation(uh[:, 0:4, SEQ:TOK], gy, ACT.Copy), yc_hi)
            for t, n in ((1, SEQ), (0, P)):
                hb = group_full()
                if t == 0:
                    act.wait_ge(emptied, par.now() - 1)
                banks = 4 if n == SEQ else 2
                T.mark(act.activation(rl[:, 0:banks * 2, :], ps[:, hb:hb + banks, :].rearrange("p b (x n) -> p (b x) n", x=2),
                                      ACT.Relu), act_evac)
            for z in range(2):
                for g in range(2):
                    skip_group()
                    n = 2 * z + g
                    act.wait_ge(nmax_ready, DH + n + 1)
                    e = lg[:, g, :]
                    for x in range(8):
                        c0, w = (x * SEQ, SEQ) if x < 4 else (1024 + (x - 4) * P, P)
                        T.mark(act.activation(e[:, c0:c0 + w], e[:, c0:c0 + w], ACT.Exp, bias=st[:, 40 + x:41 + x],
                                              accum_out=st[:, 48 + x:49 + x]), exp_done if x == 7 else act_own)
                    hb = group_full()
                    T.mark(act.activation(pts[:, 0:1024].rearrange("p (b n) -> p b n", b=2), ps[:, hb:hb + 2, :], ACT.Copy), act_evac)
                    hb = group_full()
                    T.mark(act.activation(ah8[:, 4 * z + 2 * g:4 * z + 2 * g + 2, :],
                                          ps[:, hb, :].rearrange("p (x n) -> p x n", x=2), ACT.Copy), act_evac)
            act.wait_ge(emptied, par.now())
            with act.Fori(0, 3) as i:
                for c, n in ((W, 2), (S, 2), (par, 2)):
                    c.enter(i, n)
                T.enter(i, {hi_done: 8, act_evac: 2})
                for c in range(2):
                    split()
                    hb = step_full()
                    T.mark(act.activation(g3[:, i, :, c, :], ps[:, hb:hb + 2, :], ACT.Sigmoid), act_evac)
            for c in (W, S, par):
                c.leave(3)
            T.leave(3)
            for _ in range(3):
                split()
                S.next()
                par.next()
            hb = group_full()
            T.mark(act.activation(uh[:, :, SEQ:TOK], ps[:, hb:hb + 4, :].rearrange("p b (x n) -> p (b x) n", x=2), ACT.Copy), act_evac)
            split()
            split()
            S.base += 2
            par.next()
            act.wait_ge(h_ready, projections[0] + 1)
            prep(2)
            with act.Fori(0, 4) as i:
                for c, n in ((W, 2), (S, 2), (par, 2)):
                    c.enter(i, n)
                T.enter(i, {hi_done: 8, act_evac: 2})
                for z in range(2):
                    split()
                    hb = step_full()
                    T.mark(act.activation(hid3[:, ds(i * 8 + 4 * z, 4), :], ps[:, hb:hb + 4, 0:SEQ], ACT.Relu), act_evac)
            for c in (W, S, par):
                c.leave(4)
            T.leave(4)
            act.wait_ge(emptied, par.now())
            T.settle()
            split_late(lambda j: hid3[:, j, :], SEQ)
            with act.Fori(0, 7) as i:
                W.enter(i, 1)
                A.enter(i, 1)
                T.enter(i, {hi_done: 4, ak_hi: 4})
                split()
                split_late(lambda j: hid3[:, i * 4 + (4 + j), :], SEQ)
            W.leave(7)
            A.leave(7)
            T.leave(7)
            act.wait_ge(h_ready, projections[0] + 2)
            T.mark(rms(range(2), lambda t: res[:, t, :], D, (0, 4)), rms_done)

        @block.vector
        def _(vec):
            T = Track(vec)
            W, S, Q, par, E = Count(), Count(), Count(), Count(), Count()
            norms = [0]

            def split(size=UNIT):
                s = W.next()
                for j in range(SLOTS):
                    vec.wait_ge(hi_done, s * SLOTS + (j + 1))
                    T.mark(vec.tensor_tensor(wl[:, j, 0:size], raw[:, j, 0:size], wh[:, j, 0:size], ALU.subtract), lo_done)

            def step_full():
                half = 4 * (par.base % 2)
                par.next()
                T.settle()
                vec.wait_ge(unit_used, S.next() * SLOTS + SLOTS)
                return half

            def group_full():
                half = 4 * (par.base % 2)
                par.next()
                T.settle()
                vec.wait_ge(turned, Q.next() + 1)
                return half

            def tick(sem):
                T.settle()
                T.mark(vec.memset(spare[:, :], 0.0), sem)

            def act_read():
                vec.wait_ge(act_evac, E.next() + 1)

            def close():
                act_read()
                tick(emptied)

            def take_cols(dst, n):
                hb = group_full()
                T.mark(vec.tensor_copy(dst, ps[:, hb, 0:n].rearrange(*SHAPES[len(dst.shape)](dst)[0], **SHAPES[len(dst.shape)](dst)[1])
                       if len(dst.shape) == 3 else ps[:, hb, 0:n]), cols_ready)
                tick(emptied)

            SHAPES = {3: lambda d: (("p (a b) -> p a b",), {"a": d.shape[1]})}

            def read_ada():
                n = ada.next()
                hb = step_full()
                vec.wait_ge(bias_loaded, n * 16 + 16)
                act_read()
                T.mark(vec.tensor_tensor(adat[:, 1, :], adat[:, 1, :], adat[:, 0, :], ALU.add), vec_own)
                T.settle()
                T.mark(vec.tensor_tensor(adat[:, 1, :], ps[0:64, hb, :], adat[:, 1, :], ALU.add), ada_sum)
                tick(emptied)

            ada = Count()

            def prep(nt, gain0, scale0):
                norms[0] += 1
                for k in range(nt // 2):
                    if scale0 is None:
                        ins = vec.tensor_copy(acol[:, k, :], gcol[:, gain0:gain0 + 8])
                    else:
                        ins = vec.scalar_tensor_tensor(out=acol[:, k, :], in0=mcol[:, k, scale0:scale0 + 8], scalar=1.0,
                                                       in1=gcol[:, gain0:gain0 + 8], op0=ALU.add, op1=ALU.mult)
                    T.mark(ins, acol_ready if k == nt // 2 - 1 else vec_own)
                vec.wait_ge(rms_done, norms[0])
                T.mark(vec.reciprocal(st[:, 8:8 + nt], st[:, 4:4 + nt]), rstd_ready)
                T.settle()
                for t in range(0, nt, 2):
                    T.mark(vec.tensor_scalar(xn[:, t, :], res[:, t, :], st[:, 8 + t:9 + t], None, ALU.mult),
                           xn_vec if t == nt - 2 else vec_own)
                for half in range(nt // 2):
                    hb = group_full()
                    for b in range(2, 4):
                        for c in range(2):
                            f, k = (half * 4 + b, c) if nt == 4 else (2 * b + c, 0)
                            T.mark(vec.tensor_scalar(ptmp[:, b, c * 256:(c + 1) * 256], ps[:, hb + b, c * 256:(c + 1) * 256],
                                                     acol[:, k, f:f + 1],
                                                     mcol[:, k, scale0 - 8 + f:scale0 - 7 + f] if scale0 is not None else 0.0,
                                                     ALU.mult, ALU.add), u_half if (b, c) == (3, 1) else vec_own)
                    act_read()
                    u, x = parts_of(uh, nt, half)
                    T.mark(vec.tensor_tensor(parts_of(ul, nt, half)[0], x, u, ALU.subtract), emptied)

            split()
            take_cols(fcol[:, 0:104], 104)
            take_cols(gcol[:, 0:113], 113)
            vec.wait_ge(cvec_hi, 1)
            T.mark(vec.tensor_tensor(ch[:, :, 64:128].rearrange("p f (c n) -> p f c n", c=2),
                                     cs[:, :, :].unsqueeze(3).to_broadcast([P, 8, 2, 32]),
                                     ch[:, :, 0:64].rearrange("p f (c n) -> p f c n", c=2), ALU.subtract), cvec_lo)
            for c in range(4):
                split()
                read_ada()
            hb = group_full()
            T.mark(vec.tensor_copy(zst, ps[0:16, hb, 0:384]), zrow_ready)
            tick(emptied)
            take_cols(mcol[:, :, 0:16], 32)
            vec.wait_ge(decay_loaded, 32)
            T.mark(vec.tensor_copy(lgt[:, 0, 8:12], gcol[:, LAM0:LAM0 + 4]), vec_own)
            T.settle()
            T.mark(vec.scalar_tensor_tensor(out=lgt[:, 1, :], in0=lgt[:, 0, :], scalar=-1.0, in1=lgt[:, 0, :],
                                            op0=ALU.mult, op1=ALU.max), z_abs)
            vec.wait_ge(lg_exp, 1)

            def own(ins):
                T.mark(ins, vec_own)
                T.settle()
            e, s, q = lgt[:, 2, :], lgt[:, 1, :], lgt[:, 3, :]
            own(vec.tensor_scalar(s, e, 2.0, None, ALU.add))
            own(vec.reciprocal(s, s))
            own(vec.tensor_tensor(s, e, s, ALU.mult))
            own(vec.tensor_tensor(e, s, s, ALU.mult))
            own(vec.tensor_scalar(q, e, 1.0 / 17, None, ALU.mult))
            for n in (15, 13, 11, 9, 7, 5, 3):
                own(vec.scalar_tensor_tensor(out=q, in0=q, scalar=1.0 / n, in1=e, op0=ALU.add, op1=ALU.mult))
            own(vec.scalar_tensor_tensor(out=q, in0=q, scalar=1.0, in1=s, op0=ALU.add, op1=ALU.mult))
            own(vec.tensor_scalar(s, lgt[:, 0, :], 0.0, None, ALU.min))
            T.mark(vec.scalar_tensor_tensor(out=lgt[:, 4, :], in0=q, scalar=-2.0, in1=s, op0=ALU.mult, op1=ALU.add), lg_ready)
            prep(4, 0, 8)

            vec.wait_ge(const_loaded, 16)
            with vec.Fori(0, RH) as h:
                for c, n in ((W, 6), (S, 6), (Q, 6), (par, 12), (ada, 2), (E, 11)):
                    c.enter(h, n)
                T.enter(h, {lo_done: 24, emptied: 12, vec_own: 34, qk_rot: 1, y_ready: 1, ada_sum: 2})
                split()
                hb = step_full()
                for t in range(2):
                    q4 = ps[:, hb + t, :].rearrange("p (z h x n) -> p z h x n", z=2, h=2, x=2)
                    r4 = qkt[:, t, :].rearrange("p (z h x n) -> p z h x n", z=2, h=2, x=2)
                    s3 = ksin[:, t, :].rearrange("p (h x n) -> p h x n", h=2, x=2)
                    T.mark(vec.tensor_tensor(qk[:, t, :].rearrange("p (z n) -> p z n", z=2),
                                             ps[:, hb + t, :].rearrange("p (z n) -> p z n", z=2),
                                             kcos[:, t, :].unsqueeze(1).to_broadcast([P, 2, 256]), ALU.mult), vec_own)
                    for x in range(2):
                        T.mark(vec.tensor_tensor(r4[:, :, :, x, :], q4[:, :, :, 1 - x, :],
                                                 s3[:, :, x, :].unsqueeze(1).to_broadcast([P, 2, 2, 64]), ALU.mult), vec_own)
                T.settle()
                T.mark(vec.tensor_tensor(qk[:, 0, :], qk[:, 0, :], qkt[:, 0, :], ALU.add), vec_own)
                T.mark(vec.tensor_tensor(qk[:, 1, :], qk[:, 1, :], qkt[:, 1, :], ALU.add), vec_own)
                act_read()
                tick(qk_rot)
                tick(emptied)
                split()
                step_full()
                close()
                hb = group_full()
                T.mark(vec.tensor_copy(qkt[:, 2:4, :], ps[:, hb + 2:hb + 4, :]), vec_own)
                close()
                split()
                step_full()
                close()
                vec.wait_ge(decay_exp, h + 1)
                T.mark(vec.tensor_tensor(dec[:, 0, 0:128], dec[:, 0, 0:128], kmask[:, 0, :], ALU.mult), vec_own)
                T.mark(vec.tensor_tensor(dec[:, 1, 384:512], dec[:, 1, 384:512], kmask[:, 1, :], ALU.mult), vec_own)
                T.settle()
                hb = group_full()
                for z, blocks in enumerate((FWD_BLOCKS, BWD_BLOCKS)):
                    o = 0
                    for n, (k, q0, w, d0) in enumerate(blocks):
                        last = z == 1 and n == len(blocks) - 1
                        T.mark(vec.scalar_tensor_tensor(out=(pf, pb)[z][:, o:o + w], in0=ps[:, hb + k, q0:q0 + w],
                                                        scalar=RDK ** -0.5, in1=dec[:, z, d0:d0 + w],
                                                        op0=ALU.mult, op1=ALU.mult), emptied if last else vec_own)
                        o += w
                split()
                step_full()
                close()
                for z, gate in enumerate((sgf, sgb)):
                    hb = group_full()
                    act_read()
                    T.mark(vec.reciprocal(st[:, 32 + 4 * z:36 + 4 * z], st[:, 24 + 4 * z:28 + 4 * z]), vec_own)
                    T.settle()
                    for t in range(4):
                        T.mark(vec.scalar_tensor_tensor(out=gate[:, t, :], in0=ps[:, hb + t, :],
                                                        scalar=st[:, 32 + 4 * z + t:33 + 4 * z + t], in1=gate[:, t, :],
                                                        op0=ALU.mult, op1=ALU.mult), emptied if t == 3 else vec_own)
                T.settle()
                T.mark(vec.tensor_tensor(sgf, sgf, sgb, ALU.add), y_ready)
                split()
                read_ada()
                split()
                read_ada()
                for pairs in range(2):
                    hb = group_full()
                    T.mark(vec.tensor_copy(yt[:, h * 4 + (2 * pairs + 1), :], ps[:, hb + 1, :]), vec_own)
                    close()
            for c in (W, S, Q, par, ada, E):
                c.leave(RH)
            T.leave(RH)


            def split_late(src, n):
                x = A.next()
                for j in range(SLOTS):
                    vec.wait_ge(ak_hi, x * SLOTS + (j + 1))
                    T.mark(vec.tensor_tensor(al[:, j, 0:n], src(j), ah[:, j, 0:n], ALU.subtract), ak_lo)

            A, F = Count(), Count()
            gates = [0, 0]

            def project(nt, steps, source, gate_dmas, last_size=UNIT, next_size=UNIT):
                n = nt * P
                T.settle()
                split_late(lambda j: source(j), n)
                if steps > 2:
                    with vec.Fori(0, steps - 2) as i:
                        W.enter(i, 1)
                        A.enter(i, 1)
                        T.enter(i, {lo_done: 4, ak_lo: 4})
                        split()
                        split_late(lambda j: source(i * 4 + (4 + j)), n)
                    W.leave(steps - 2)
                    A.leave(steps - 2)
                    T.leave(steps - 2)
                split(last_size)
                k0 = 4 * (steps - 1)
                split_late(lambda j: source(k0 + (j // 2 if last_size < UNIT else j)), n)
                split(next_size)
                S.base += steps
                add_normed(nt, gate_dmas)

            def add_normed(nt, gate_dmas):
                halves = [4 * ((par.base + z) % 2) for z in range(nt // 2)]
                par.base += nt // 2
                if gates[0] == 0:
                    vec.wait_ge(x_loaded, 64)
                gates[0] += 16 * gate_dmas
                vec.wait_ge(gate_loaded, gates[0])
                for k in range(nt // 2):
                    T.mark(vec.tensor_tensor(gb[:, k, :], gb[:, k, :], gn, ALU.mult), vec_own)
                act_read()
                T.mark(vec.reciprocal(st[:, 8:8 + nt], st[:, 4:4 + nt]), vec_own)
                for t in range(nt):
                    T.settle()
                    b = halves[t // 2] + 2 * (t % 2)
                    T.mark(vec.scalar_tensor_tensor(out=ytmp[:, t % 2, :].rearrange("p (c n) -> p c n", c=2), in0=ps[:, b:b + 2, :],
                                                    scalar=st[:, 8 + t:9 + t],
                                                    in1=gb[:, t // 2, :].rearrange("p (c n) -> p c n", c=2),
                                                    op0=ALU.mult, op1=ALU.mult), emptied if t % 2 else vec_own)
                    if t % 2:
                        T.settle()
                        T.mark(vec.tensor_tensor(res[:, t - 1:t + 1, :], res[:, t - 1:t + 1, :], ytmp, ALU.add),
                               h_ready if t == nt - 1 else vec_own)
                T.settle()

            def read_ffn(ft, n):
                p = par.base % 2
                hb = step_full()
                seqs = n // SEQ
                vec.wait_ge(ffn_lin, F.next() + 1)
                views = [(lin[:, p, m, 0:n].rearrange("p (s n) -> p s n", s=seqs),
                          ps[:, hb + 2 + m, 0:n].rearrange("p (s n) -> p s n", s=seqs)) for m in range(2)]
                for tap in (0, 2):
                    for m, (x, g) in enumerate(views):
                        o, i_ = (x[:, :, 1:SEQ], g[:, :, 0:SEQ - 1]) if tap == 0 else (x[:, :, 0:SEQ - 1], g[:, :, 1:SEQ])
                        T.mark(vec.scalar_tensor_tensor(out=o, in0=i_, scalar=fcol[:, ds(ft + (16 + tap * FT + m), 1)],
                                                        in1=o, op0=ALU.mult, op1=ALU.add),
                               ffn_conv if (tap, m) == (2, 1) else vec_own)
                    if tap == 0:
                        T.settle()
                act_read()
                dst = hid if n == TOK else hid2
                T.mark(vec.tensor_tensor(dst[:, ds(ft, 2), :], lin[:, p, :, 0:n], ps[:, hb:hb + 2, 0:n], ALU.mult), emptied)

            project(4, 4, lambda k: yt[:, k, :], 3)
            take_cols(mcol[:, :, :], 96)
            prep(4, 16, 32)
            with vec.Fori(0, 5) as i:
                for c, n in ((W, 4), (S, 4), (par, 4), (ada, 2), (F, 2), (E, 4)):
                    c.enter(i, n)
                T.enter(i, {lo_done: 16, emptied: 4, vec_own: 8, ffn_conv: 2, ada_sum: 2})
                split()
                read_ffn(i * 4, TOK)
                split()
                read_ffn(i * 4 + 2, TOK)
                split()
                read_ada()
                split()
                read_ada()
            for c in (W, S, par, ada, F, E):
                c.leave(5)
            T.leave(5)
            split()
            read_ffn(20, TOK)
            split()
            read_ada()
            split()
            read_ada()
            project(4, 6, lambda k: hid[:, k, :], 3, 512)
            take_cols(fcol[:, 16:104], 88)
            take_cols(mcol[:, :, :], 96)
            prep(4, 32, 8)

            vec.wait_ge(lam_loaded, 64)
            for z in range(2):
                own(vec.tensor_tensor(lamq[:, z, :], lamq[:, z, :], lamq[:, 2 + z, :], ALU.mult))
                T.mark(vec.tensor_reduce(lamt[:, z:z + 1], lamq[:, z, :], AX.X, ALU.add), (vec_own, lam_dots)[z])
            vec.wait_ge(lam_exp, 1)
            own(vec.tensor_tensor(lamt[:, 4:5], lamt[:, 3:4], lamt[:, 2:3], ALU.subtract))
            own(vec.tensor_scalar(lamt[:, 4:5], lamt[:, 4:5], -LAM_INIT, None, ALU.add))
            own(vec.tensor_scalar(lamt[:, 5:6], gcol[:, SUB0:SUB0 + 1], 1.0 - LAM_INIT, None, ALU.mult))
            with vec.Fori(0, DH // 2) as i:
                for c, n in ((W, 2), (S, 2), (Q, 8), (par, 10), (E, 10)):
                    c.enter(i, n)
                T.enter(i, {lo_done: 8, emptied: 10, vec_own: 27, qk_rot: 1, nmax_ready: 2, prob_ready: 2})
                split(512)
                hb = step_full()
                for t in range(2):
                    z4 = ps[:, hb + t, :].rearrange("p (z h x n) -> p z h x n", z=8, h=2, x=2)
                    r4 = drot[:, t, :].rearrange("p (z h x n) -> p z h x n", z=8, h=2, x=2)
                    s3 = dsin[:, t, :].rearrange("p (h x n) -> p h x n", h=2, x=2)
                    T.mark(vec.tensor_tensor(dqk[:, t, :].rearrange("p (z n) -> p z n", z=8),
                                             ps[:, hb + t, :].rearrange("p (z n) -> p z n", z=8),
                                             dcos[:, t, :].unsqueeze(1).to_broadcast([P, 8, 64]), ALU.mult), vec_own)
                    for x in range(2):
                        T.mark(vec.tensor_tensor(r4[:, :, :, x, :], z4[:, :, :, 1 - x, :],
                                                 s3[:, :, x, :].unsqueeze(1).to_broadcast([P, 8, 2, 16]), ALU.mult), vec_own)
                T.settle()
                T.mark(vec.tensor_tensor(dqk[:, 0:2, :], dqk[:, 0:2, :], drot, ALU.add), vec_own)
                act_read()
                tick(qk_rot)
                tick(emptied)
                split()
                hb = step_full()
                T.mark(vec.tensor_copy(dv[:, 2:4, :], ps[:, hb + 2:hb + 4, 0:256]), vec_own)
                close()
                hb = group_full()
                T.mark(vec.tensor_copy(dkt[:, 1, :], ps[:, hb + 2, :]), vec_own)
                close()
                for h in range(2):
                    hb = group_full()
                    T.mark(vec.tensor_reduce(st[:, 40 + 4 * h:44 + 4 * h], ps[:, hb:hb + 4, :], AX.X, ALU.max), vec_own)
                    T.settle()
                    T.mark(vec.tensor_scalar(st[:, 40 + 4 * h:44 + 4 * h], st[:, 40 + 4 * h:44 + 4 * h], -(DD ** -0.5), None, ALU.mult), nmax_ready)
                    close()
                    o = 48 + 4 * h
                    own(vec.reciprocal(st[:, o:o + 4], st[:, o:o + 4]))
                    own(vec.tensor_scalar(st[:, o + 2:o + 4], st[:, o + 2:o + 4], lamt[:, 4:5], None, ALU.mult))
                    for t in range(2):
                        T.mark(vec.tensor_scalar(dpr[:, h, 2 + t, :], dpr[:, h, 2 + t, :], st[:, o + 2 + t:o + 3 + t], None, ALU.mult), vec_own)
                    T.settle()
                    for t in range(2):
                        T.mark(vec.scalar_tensor_tensor(out=dpr[:, h, t, :], in0=dpr[:, h, t, :], scalar=st[:, o + t:o + 1 + t],
                                                        in1=dpr[:, h, 2 + t, :], op0=ALU.mult, op1=ALU.add), (vec_own, prob_ready)[t])
                for h in range(2):
                    hb = group_full()
                    T.mark(vec.tensor_copy(dpt[:, h, 2:4, :], ps[:, hb + 1, :].rearrange("p (k n) -> p k n", k=2)), vec_own)
                    close()
                for h in range(2):
                    hb = group_full()
                    act_read()
                    o = 24 + 2 * h
                    own(vec.reciprocal(st[:, o:o + 2], st[:, o - 4:o - 2]))
                    for t in range(2):
                        T.mark(vec.tensor_scalar(dy[:, h, t, :], ps[:, hb, t * P:(t + 1) * P], st[:, o + t:o + 1 + t], None, ALU.mult),
                               (vec_own, emptied)[t])
                hb = group_full()
                act_read()
                T.mark(vec.scalar_tensor_tensor(out=al8[:, ds(i * 2, 2), :], in0=ps[:, hb, :].rearrange("p (h n) -> p h n", h=2),
                                                scalar=lamt[:, 5:6], in1=ah8[:, ds(i * 2, 2), :],
                                                op0=ALU.mult, op1=ALU.subtract), emptied)
            for c in (W, S, Q, par, E):
                c.leave(DH // 2)
            T.leave(DH // 2)
            split()
            split()
            S.base += 2
            add_normed(2, 2)
            prep(2, 48, 32)
            with vec.Fori(0, 5) as i:
                for c, n in ((W, 2), (S, 2), (par, 2), (F, 2), (E, 2)):
                    c.enter(i, n)
                T.enter(i, {lo_done: 8, emptied: 2, vec_own: 6, ffn_conv: 2})
                split()
                read_ffn(i * 4, SEQ)
                split()
                read_ffn(i * 4 + 2, SEQ)
            for c in (W, S, par, F, E):
                c.leave(5)
            T.leave(5)
            split()
            read_ffn(20, SEQ)
            project(2, 6, lambda k: hid2[:, k, :], 2, 512)
            prep(2, MIXG0, None)

            def read_half(dst):
                hb = step_full()
                T.mark(vec.tensor_copy(dst[:, 2:4, :], ps[:, hb + 2:hb + 4, 0:SEQ]), vec_own)
                close()

            def read_values(dst):
                hb = step_full()
                T.mark(vec.tensor_copy(dst, ps[:, hb + 1, :]), vec_own)
                close()

            split()
            read_half(qkt5[:, 0])
            split()
            read_half(qkt5[:, 1])
            split()
            read_values(vab[:, 1, :])
            split()
            read_half(qkt5[:, 2])
            split()
            read_half(qkt5[:, 3])
            split()
            read_values(vab[:, 3, :])
            split(144)
            read_half(qkt5[:, 4])
            split()
            hb = step_full()
            act_read()
            T.mark(vec.tensor_copy(wiw, ps[:, hb:hb + 2, 64:72]), emptied)
            split()
            hb = step_full()
            vec.wait_ge(xc_lin, 1)
            for d in (1, 2, 3):
                T.settle()
                for m in range(4):
                    c = CW0 + 4 * (3 - d) + m
                    T.mark(vec.scalar_tensor_tensor(out=xcv[:, m, d:SEQ], in0=ps[:, hb + m, 0:SEQ - d], scalar=gcol[:, c:c + 1],
                                                    in1=xcv[:, m, d:SEQ], op0=ALU.mult, op1=ALU.add),
                           emptied if (d, m) == (3, 3) else vec_own)
            split()
            step_full()
            close()
            hb = group_full()
            T.mark(vec.tensor_copy(kit, ps[:, hb, 0:SEQ]), emptied)
            group_full()
            close()
            for m in range(4):
                T.mark(vec.tensor_scalar(rt[:, m, :], rt[:, m, :], lgt[:, 4, 8 + m:9 + m], -8.0, ALU.mult, ALU.mult),
                       lru_arg if m == 3 else vec_own)
            T.mark(vec.tensor_tensor(it, it, xcv, ALU.mult), vec_own)
            vec.wait_ge(lru_fun, 1)
            T.settle()
            own(vec.tensor_scalar(rt, lt, 1.0, None, ALU.add))
            own(vec.reciprocal(rt, rt))
            own(vec.scalar_tensor_tensor(out=lt, in0=lt, scalar=2.0, in1=rt, op0=ALU.mult, op1=ALU.mult))
            T.mark(vec.tensor_scalar(lt, lt, 1e-30, None, ALU.max), lru_sq)
            vec.wait_ge(lru_root, 1)
            own(vec.tensor_tensor(it, it, lt, ALU.mult))
            for m in range(4):
                T.mark(vec.tensor_tensor_scan(out=xcv[:, m, :], data0=la[:, m, :], data1=it[:, m, :], initial=0.0,
                                              op0=ALU.mult, op1=ALU.add), vec_own)
            T.settle()
            T.mark(vec.tensor_tensor(gy, gy, xcv, ALU.mult), yc_ready)
            vec.wait_ge(yc_hi, 1)
            T.mark(vec.tensor_tensor(ul[:, 0:4, SEQ:TOK], gy, uh[:, 0:4, SEQ:TOK], ALU.subtract), yc_lo)

            for t, n in ((1, SEQ), (0, P)):
                group_full()
                act_read()
                v = rl.rearrange("p a b -> p (a b)")[:, 0:8 * n].rearrange("p (h n) -> p h n", h=8)
                own(vec.tensor_scalar(wk[:, t, 0:n], v[:, 0, :], wiw[:, t, 0:1], None, ALU.mult))
                for i in range(1, 8):
                    h = (i % 4) * 2 + i // 4
                    own(vec.scalar_tensor_tensor(out=wk[:, t, 0:n], in0=v[:, i, :], scalar=wiw[:, t, h:h + 1],
                                                 in1=wk[:, t, 0:n], op0=ALU.mult, op1=ALU.add))
                if t == 1:
                    vec.wait_ge(causal_loaded, 16)
                own(vec.scalar_tensor_tensor(out=wk[:, t, 0:n], in0=wk[:, t, 0:n], scalar=float(8 * HD) ** -0.5,
                                             in1=causal[:, t, 0:n], op0=ALU.mult, op1=ALU.add))
                tick(emptied)
            for r in range(TOPK // 8):
                for t, n in ((1, SEQ), (0, P)):
                    T.mark(vec.max(out=st[:, 24 + 8 * t:32 + 8 * t], in_=wk[:, t, 0:n]), vec_own)
                T.settle()
                for t, n in ((1, SEQ), (0, P)):
                    T.mark(vec.match_replace(out=wk[:, t, 0:n], in_to_replace=st[:, 24 + 8 * t:32 + 8 * t],
                                             in_values=wk[:, t, 0:n], imm_value=MARK), vec_own)
                T.settle()
            for t, n in ((1, SEQ), (0, P)):
                T.mark(vec.tensor_scalar(maskb[:, t, 0:n], wk[:, t, 0:n], MARK / 2, NEG, ALU.is_gt, ALU.mult), vec_own)

            for z in range(2):
                for g in range(2):
                    n = 2 * z + g
                    hb = group_full()
                    e = lg[:, g, :]
                    e1, e0 = (e[:, 0:1024].rearrange("p (x n) -> p x n", x=4), e[:, 1024:1536].rearrange("p (x n) -> p x n", x=4))
                    vec.wait_ge(z_loaded[g], 32 * (z + 1))
                    T.mark(vec.scalar_tensor_tensor(out=e1, in0=ps[:, hb:hb + 2, :].rearrange("p b (x n) -> p (b x) n", x=2),
                                                    scalar=HD ** -0.5, in1=zt[:, g, :, :], op0=ALU.mult, op1=ALU.add), vec_own)
                    T.mark(vec.scalar_tensor_tensor(out=e0.rearrange("p (b x) n -> p b x n", b=2),
                                                    in0=ps[:, hb + 2:hb + 4, 0:2 * P].rearrange("p b (x n) -> p b x n", x=2),
                                                    scalar=HD ** -0.5, in1=zt[:, g, :, P:SEQ].rearrange("p (b x) n -> p b x n", b=2),
                                                    op0=ALU.mult, op1=ALU.add), z_used)
                    tick(emptied)
                    if z:
                        T.mark(vec.tensor_tensor(e1, e1, maskb[:, 1, :].unsqueeze(1).to_broadcast([P, 4, SEQ]), ALU.add), vec_own)
                        T.mark(vec.tensor_tensor(e0, e0, maskb[:, 0, 0:P].unsqueeze(1).to_broadcast([P, 4, P]), ALU.add), vec_own)
                        T.settle()
                    T.mark(vec.tensor_reduce(st[:, 40:44], e1, AX.X, ALU.max, negate=True), vec_own)
                    T.mark(vec.tensor_reduce(st[:, 44:48], e0, AX.X, ALU.max, negate=True), nmax_ready)
                    vec.wait_ge(exp_done, n + 1)
                    own(vec.reciprocal(st[:, 48:56], st[:, 48:56]))
                    T.mark(vec.tensor_tensor(e1, e1, st[:, 48:52].unsqueeze(2).to_broadcast([P, 4, SEQ]), ALU.mult), vec_own)
                    T.mark(vec.tensor_tensor(e0, e0, st[:, 52:56].unsqueeze(2).to_broadcast([P, 4, P]), ALU.mult), prob_ready)
                    hb = group_full()
                    T.mark(vec.tensor_copy(pts[:, 1024:1536], ps[:, hb + 2, :]), vec_own)
                    close()
                    hb = group_full()
                    act_read()
                    k = 4 * z + 2 * g
                    T.mark(vec.tensor_tensor(al8[:, k:k + 2, :], ps[:, hb, :].rearrange("p (x n) -> p x n", x=2),
                                             ah8[:, k:k + 2, :], ALU.subtract), emptied)
            with vec.Fori(0, 3) as i:
                for c, n in ((W, 2), (S, 2), (par, 2), (E, 2)):
                    c.enter(i, n)
                T.enter(i, {lo_done: 8, emptied: 2})
                for c in range(2):
                    split()
                    step_full()
                    close()
            for c in (W, S, par, E):
                c.leave(3)
            T.leave(3)
            for b in range(3):
                split()
                hb = step_full()
                o = mg if b == 0 else mt
                T.mark(vec.tensor_tensor(o, ps[:, hb:hb + 4, :], g3[:, b, :, :, :].rearrange("p t c n -> p (t c) n"), ALU.mult), emptied)
                if b:
                    T.settle()
                    T.mark(vec.tensor_tensor(mg, mg, mt, ALU.add), (None, vec_own, merged)[b])
            hb = group_full()
            act_read()
            T.mark(vec.tensor_tensor(ul[:, :, SEQ:TOK], ps[:, hb:hb + 4, :].rearrange("p b (x n) -> p (b x) n", x=2),
                                     uh[:, :, SEQ:TOK], ALU.subtract), emptied)
            split()
            split()

            def add_plain():
                hb = 4 * (par.base % 2)
                par.next()
                vec.wait_ge(unit_used, S.now() * SLOTS)
                r4 = res[:, 0:2, :].rearrange("p t (c n) -> p (t c) n", c=2)
                T.mark(vec.tensor_tensor(r4, r4, ps[:, hb:hb + 4, :], ALU.add), h_ready)
                tick(emptied)

            S.base += 2
            add_plain()
            prep(2, MLPG0, None)
            with vec.Fori(0, 4) as i:
                for c, n in ((W, 2), (S, 2), (par, 2), (E, 2)):
                    c.enter(i, n)
                T.enter(i, {lo_done: 8, emptied: 2})
                for z in range(2):
                    split()
                    hb = step_full()
                    act_read()
                    v = hid3[:, ds(i * 8 + 4 * z, 4), :]
                    T.mark(vec.tensor_tensor(v, v, v, ALU.mult), emptied)
            for c in (W, S, par, E):
                c.leave(4)
            T.leave(4)
            T.settle()
            split_late(lambda j: hid3[:, j, :], SEQ)
            with vec.Fori(0, 7) as i:
                W.enter(i, 1)
                A.enter(i, 1)
                T.enter(i, {lo_done: 4, ak_lo: 4})
                split()
                split_late(lambda j: hid3[:, i * 4 + (4 + j), :], SEQ)
            W.leave(7)
            A.leave(7)
            T.leave(7)
            S.base += 8
            add_plain()
            vec.wait_ge(rms_done, norms[0] + 1)
            own(vec.reciprocal(st[:, 8:10], st[:, 4:6]))
            vec.wait_ge(gain_loaded, 16)
            for t in range(2):
                T.mark(vec.scalar_tensor_tensor(out=fout[:, t, :], in0=res[:, t, :], scalar=st[:, 8 + t:9 + t], in1=gn,
                                                op0=ALU.mult, op1=ALU.mult), out_ready)

        @block.gpsimd
        def _(pool):
            ada = Count()

            def row_view(name, *idx):
                v = a[name]
                for i in idx:
                    v = v[i]
                return v

            def load_rows(batch, parts, wait):
                if wait:
                    pool.wait_ge(cols_ready, wait)
                r = 0
                for v in parts:
                    n = int(np.prod(v.shape)) // P
                    src = bass.AP(v.tensor, v.offset, [[P, n], [1, P]])
                    pool.dma_start(rows[r:r + n, batch % 2, :], src).then_inc(rows_loaded[batch % 2], 16)
                    r += n

            def ada_rows(l, c0):
                n = ada.next()
                if not (isinstance(n, int) and n == 0):
                    pool.wait_ge(ada_sum, n)
                pool.wait_ge(ident_loaded, 16)
                pool.dma_start(adat[:, 0, :], a["ada_b"][l, ds(c0, 512)].unsqueeze(0).to_broadcast([64, 512])).then_inc(bias_loaded, 16)
                pool.wait_ge(ada_sum, n + 1)
                pool.wait_ge(ident_loaded, 16)
                pool.dma_start(mods[l, :, ds(c0, 512)], adat[0:64:32, 1, :]).then_inc(ada_stored, 16)

            pool.dma_start(ident[:, :], a["k_ident"]).then_inc(ident_loaded, 16)
            load_rows(0, [a["c"][0], a["c_ctx"], a["ffn_conv_w"][0], a["ffn_conv_b"][0]], 0)
            load_rows(1, [a["norm_g"], a["norm_mix_g_2"], a["norm_mlp_g_2"], a["conv_w_2"], a["conv_b_2"],
                          a["b_r_2"], a["b_i_2"], a["lru_lambda_2"], a["diff_subln"]], 0)
            pool.memset(epsc[:, :], EPS).then_inc(eps_set, 1)
            pool.dma_start(res[:, 0:2, :], a["x"][0].rearrange("(t p) n -> p t n", p=P)).then_inc(x_loaded, 16)
            pool.dma_start(res[:, 2:4, :], a["ctx"][0].rearrange("(t p) n -> p t n", p=P)).then_inc(x_loaded, 16)
            for z, name in enumerate(("ret_decay_f", "ret_decay_b")):
                pool.dma_start(lgt[:, 0, 4 * z:4 * z + 4], a[name].to_broadcast([P, RH])).then_inc(decay_loaded, 16)
            pool.dma_start(kret, a["k_ret"]).then_inc(const_loaded, 16)
            pool.dma_start(kdif[:, :], a["k_dif"]).then_inc(kdif_loaded, 16)
            pool.wait_ge(eps_set, 1)
            pool.memset(tab[32:33, :], NEG).then_inc(tab_set, 1)
            pool.dma_start(tab[0:32, :], a["rel_bias_2"]).then_inc(hot_loaded, 16)
            pool.dma_start(hot, a["k_hot"]).then_inc(hot_loaded, 16)
            for c in range(4):
                ada_rows(0, c * 512)
            pool.wait_ge(ada_stored, 64)
            load_rows(2, [mods[0, 0, 0:2 * D], mods[0, 1, 0:2 * D]], 1)
            pool.wait_ge(zrow_ready, 1)
            pool.dma_start(zrow, zst.unsqueeze(1).to_broadcast([2 * NH, P, 384])).then_inc(zrow_stored, 16)
            for c in range(4, 12):
                ada_rows(0, c * 512)
            pool.wait_ge(unit_used, S_RETO * SLOTS + 1)
            pool.dma_start(res[:, 0:2, :], a["x"][0].rearrange("(t p) n -> p t n", p=P)).then_inc(x_loaded, 16)
            pool.dma_start(res[:, 2:4, :], a["ctx"][0].rearrange("(t p) n -> p t n", p=P)).then_inc(x_loaded, 16)
            pool.wait_ge(ada_stored, 16 * 12)

            def load_gates(l, conds, part, gain):
                for c in range(conds):
                    pool.dma_start(gb[:, c, :], mods[l, c, part * D:(part + 1) * D].unsqueeze(0).to_broadcast([P, D])).then_inc(gate_loaded, 16)
                pool.dma_start(gn, a["norm_g"][l, gain].unsqueeze(0).to_broadcast([P, D])).then_inc(gate_loaded, 16)

            load_gates(0, 2, 2, 1)
            load_rows(3, [mods[0, 0, :], mods[0, 1, :]], 2)
            pool.wait_ge(unit_used, S_UP0 * SLOTS + 1)
            load_gates(0, 2, 5, 3)
            load_rows(4, [a["ffn_conv_w"][1], a["ffn_conv_b"][1]], 3)
            for c in range(12):
                ada_rows(1, c * 512)
            pool.wait_ge(ada_stored, 16 * 24)
            load_rows(5, [mods[1, 0, :], mods[1, 1, :]], 4)
            for z, name in enumerate(("diff_lq1", "diff_lq2", "diff_lk1", "diff_lk2")):
                pool.dma_start(lamq[:, z, :], a[name].to_broadcast([P, DD])).then_inc(lam_loaded, 16)
            pool.wait_ge(unit_used, S_DIF * SLOTS + 1)
            load_gates(1, 1, 2, 1)
            pool.wait_ge(unit_used, S_UP1 * SLOTS + 1)
            load_gates(1, 1, 5, 3)
            pool.wait_ge(unit_used, S_MIX * SLOTS + 1)
            for z, name in enumerate(("w_r_2", "w_i_2")):
                for half in range(2):
                    pool.dma_start(wri[64 * half:64 * half + 64, z, :, :],
                                   a[name][0].rearrange("(m b) c d -> b c m d", b=2)[half]).then_inc(mix_loaded, 16)
            pool.dma_start(causal, a["k_causal"].rearrange("p (t n) -> p t n", t=2)).then_inc(causal_loaded, 16)
            pool.wait_ge(zrow_stored, 16)
            for n in range(4):
                if n >= 2:
                    pool.wait_ge(z_used, n - 1)
                for odd in range(2):
                    skew = bass.AP(zrow.tensor, zrow.offset + (4 * n + odd) * P * 384 + 127, [[383, P], [2 * P * 384, 2], [1, SEQ]])
                    pool.dma_start(zt[:, n % 2, 2 * odd:2 * odd + 2, :], skew).then_inc(z_loaded[n % 2], 16)
            pool.wait_ge(unit_used, S_MUP * SLOTS + 1)
            pool.dma_start(gn, a["final_norm_g_2"].unsqueeze(0).to_broadcast([P, D])).then_inc(gain_loaded, 16)
            o2 = out[0].rearrange("(t p) n -> t p n", p=P)
            for t in range(2):
                pool.wait_ge(out_ready, t + 1)
                pool.dma_start(o2[t], fout[:, t, :]).then_inc(out_stored, 16)
            pool.wait_ge(out_stored, 32)


def kernel(**inputs):
    import concourse.bacc as bacc
    from concourse.bass_utils import run_bass_kernel_spmd

    nc = bacc.Bacc("TRN2", target_bir_lowering=False, num_devices=1)
    arrays = {**{k: np.ascontiguousarray(v) for k, v in inputs.items()}, **shape_constants()}
    feed, aps = {}, {}
    for name, v in arrays.items():
        feed[f"in_{name}"] = v
        aps[name] = nc.dram_tensor(f"in_{name}", v.shape, mybir.dt.from_np(v.dtype), kind="ExternalInput").ap()
    out = nc.dram_tensor("out_x", (1, SEQ, D), F32, kind="ExternalOutput").ap()
    build(nc, aps, out)
    r = run_bass_kernel_spmd(nc, [feed], core_ids=[0])
    return r.results[0]["out_x"]
```

```python
import math
from contextlib import ExitStack

import numpy as np

import concourse.bass as bass
from concourse import mybir

ALU = mybir.AluOpType
ACT = mybir.ActivationFunctionType
AX = mybir.AxisListType
F32 = mybir.dt.float32
F32R = mybir.dt.float32r
BF16 = mybir.dt.bfloat16

P = 128
D = 1024
KD = D // P
SEQ, CTX = 256, 256
TOK = SEQ + CTX
EPS = 1e-6
NEG = -1e30
RH, RDK, RDV = 4, 256, 512
FH = 2816
FT = FH // P
DH, DD = 8, 64
LAM_INIT = 0.8 - 0.6 * math.exp(-0.3)
HD = 64
NH = 8
TOPK = min(256, SEQ // 4)
MH = 4 * D
MT = MH // P
UNIT = 1024
SLOTS = 4
GRID_W = 64
BUCKETS, MAX_DIST = 32, 128
MARK = -3e38
W2 = {}
_o = 0
for _n, _w in (("qa", 512), ("ka", 512), ("va", 512), ("qb", 512), ("kb", 512), ("vb", 512),
               ("qi", 512), ("kw", 72), ("xc", 512), ("yc", 512), ("g", 3072)):
    W2[_n] = _o
    _o += _w


def rope_tables(width):
    half = width // 2
    inv = (10000.0 ** (-np.arange(0, half, 2, dtype=np.float32) / np.float32(half))).astype(np.float32)
    t = np.arange(SEQ)
    cos, sin = np.zeros((SEQ, width), np.float32), np.zeros((SEQ, width), np.float32)
    for n, pos in enumerate((t // GRID_W, t % GRID_W)):
        ang = pos.astype(np.float32)[:, None] * inv[None, :]
        c, s = np.cos(ang), np.sin(ang)
        cos[:, n * half:(n + 1) * half] = np.concatenate([c, c], 1)
        sin[:, n * half:(n + 1) * half] = np.concatenate([-s, s], 1)
    return cos, sin


def shape_constants():
    p = np.arange(P)[:, None].astype(np.float32)
    u = np.arange(512)[None, :].astype(np.float32)
    fwd, bwd = u - p, 384 + p - u
    dist = np.stack([np.maximum(fwd, 0), np.maximum(bwd, 0)], 1)
    mask = np.stack([(fwd >= 0)[:, 0:128], (bwd >= 0)[:, 384:512]], 1).astype(np.float32)
    rc, rs = rope_tables(RDK)
    dc, ds = rope_tables(DD)
    tile2 = lambda a: a.reshape(2, P, -1).transpose(1, 0, 2).reshape(P, -1)
    t = np.arange(SEQ)
    causal = np.where(t[None, :] <= t[:, None], 0.0, NEG).astype(np.float32)
    dist2 = 255 - np.arange(384)
    n = np.maximum(dist2, 0)
    exact = BUCKETS // 2
    nf = np.maximum(n, 1).astype(np.float32)
    large = exact + (np.log(nf / np.float32(exact)) / np.float32(math.log(MAX_DIST / exact))
                     * np.float32(BUCKETS - exact)).astype(np.int32)
    bucket = np.where(n < exact, n, np.minimum(large, BUCKETS - 1))
    hot = np.zeros((BUCKETS + 1, 384), np.float32)
    hot[bucket, np.arange(384)] = 1.0
    hot[:, dist2 < 0] = 0.0
    hot[BUCKETS, dist2 < 0] = 1.0
    return {
        "k_ident": np.eye(P, dtype=np.float32),
        "k_ret": np.ascontiguousarray(np.concatenate(
            [dist.reshape(P, -1), mask.reshape(P, -1), tile2(rc), tile2(rs)], 1)),
        "k_dif": np.ascontiguousarray(np.concatenate([tile2(dc), tile2(ds)], 1)),
        "k_causal": np.ascontiguousarray(tile2(causal)),
        "k_hot": hot,
    }


FWD_BLOCKS = [(0, 0, 256, 0), (1, 128, 128, 0), (2, 0, 256, 256), (3, 0, 256, 128), (2, 256, 256, 0), (3, 384, 128, 0)]
BWD_BLOCKS = [(0, 0, 128, 384), (1, 0, 256, 256), (2, 0, 256, 128), (3, 0, 256, 0), (2, 256, 128, 384), (3, 256, 256, 256)]


def reads_of(blocks):
    out, o = [[] for _ in range(4)], 0
    for k, q0, w, _ in blocks:
        for q in range(q0, q0 + w, P):
            out[q // P].append((o + q - q0, k))
        o += w
    return out


FWD_READS, BWD_READS = reads_of(FWD_BLOCKS), reads_of(BWD_BLOCKS)
MIXG0, MLPG0, CW0, CB0, BR0, BI0, LAM0, SUB0 = 64, 72, 80, 96, 100, 104, 108, 112


class Track:

    def __init__(self, eng):
        self.eng, self.n, self.i, self.per, self.start, self.last = eng, {}, None, {}, {}, None

    def value(self, sem):
        v = self.n.get(sem.name, 0)
        return v + self.i * self.per[sem.name] if self.per.get(sem.name) else v

    def mark(self, ins, sem):
        ins.then_inc(sem, 1)
        self.n[sem.name] = self.n.get(sem.name, 0) + 1
        self.last = sem

    def settle(self):
        self.eng.wait_ge(self.last, self.value(self.last))

    def enter(self, i, per):
        self.i, self.per, self.start = i, {s.name: c for s, c in per.items()}, dict(self.n)

    def leave(self, rounds):
        for name in set(self.n) | set(self.per):
            grown = self.n.get(name, 0) - self.start.get(name, 0)
            assert grown == self.per.get(name, 0), (name, grown, self.per.get(name, 0))
            self.n[name] = self.n.get(name, 0) + (rounds - 1) * grown
        self.i, self.per = None, {}


class Count:

    def __init__(self):
        self.base, self.i, self.per, self.start = 0, None, 0, 0

    def now(self):
        return self.base if self.i is None else self.base + self.i * self.per

    def next(self):
        v = self.now()
        self.base += 1
        return v

    def enter(self, i, per):
        self.i, self.per, self.start = i, per, self.base

    def leave(self, rounds):
        assert self.base - self.start == self.per, (self.base, self.start, self.per)
        self.base += (rounds - 1) * self.per
        self.i = None


def ds(i, n):
    return slice(i, i + n) if isinstance(i, int) else bass.ds(i, n)


def build(nc, a, out):
    ctx = ExitStack()
    with ctx:
        def sb(name, shape, dt=F32):
            return ctx.enter_context(nc.sbuf_tensor(name, shape, dt))

        def sem(name):
            return ctx.enter_context(nc.semaphore(name))

        mods = nc.dram_tensor("mods", (2, 2, 6 * D), F32, kind="Internal").ap()
        zrow = nc.dram_tensor("zrow", (2 * NH, P, 384), F32, kind="Internal").ap()

        raw = sb("raw", [P, SLOTS, UNIT])
        wh = sb("wh", [P, SLOTS, UNIT], F32R)
        wl = sb("wl", [P, SLOTS, UNIT], F32R)
        uh = sb("uh", [P, KD, TOK], F32R)
        ul = sb("ul", [P, KD, TOK], F32R)
        ah = sb("ah", [P, SLOTS, TOK], F32R)
        al = sb("al", [P, SLOTS, TOK], F32R)
        ch = sb("cvec", [P, KD, P], F32R)
        res = sb("res", [P, 4, D])
        junk = sb("junk", [P, D], BF16)
        ident = sb("ident", [P, P])
        kdif = sb("kdif", [P, 256])
        adat = sb("adat", [64, 2, 512])
        rows = sb("rows", [P, 2, P])
        gcol = sb("gcol", [P, 113])
        fcol = sb("fcol", [P, 104])
        fcol2 = sb("fcol2", [P, 88])
        mcol = sb("mcol", [P, 2, 48])
        acol = sb("acol", [P, 2, 8])
        cs = sb("cs", [P, 8, 2])
        st = sb("st", [P, 72])
        lgt = sb("lgt", [P, 5, 12])
        lamt = sb("lamt", [P, 8])
        lamq = sb("lamq", [P, 4, DD])
        epsc = sb("epsc", [P, 1])
        spare = sb("spare", [1, 1])
        ARENA = 79 * 256
        arena = sb("arena", [P, ARENA])
        ps = ctx.enter_context(nc.psum_tensor("ps", [P, 8, 512], F32))

        def area(kb, *shape):
            n = int(np.prod(shape))
            o = int(kb * 256)
            assert o + n <= ARENA, (kb, shape)
            v = arena[:, o:o + n]
            if len(shape) == 1:
                return v
            names = "abcd"[:len(shape)]
            return v.rearrange(f"p ({' '.join(names)}) -> p {' '.join(names)}",
                               **dict(zip(names[1:], shape[1:])))

        yt = area(0, 16, TOK)
        qk = area(32, 4, 512)
        pf, pb = area(32, 1280), area(37, 1280)
        qkt = area(42, 4, 512)
        rtmp = area(42, 512)
        sgb = area(50, 4, 512)
        dec = area(58, 2, 512)
        kret = area(62, 2304)
        vres = res[:, 0:2, :].rearrange("p a (b c) -> p (a b) c", b=2)
        sgf = res[:, 2:4, :].rearrange("p a (b c) -> p (a b) c", b=2)
        kdist = kret[:, 0:1024].rearrange("p (a b) -> p a b", a=2)
        kmask = kret[:, 1024:1280].rearrange("p (a b) -> p a b", a=2)
        kcos = kret[:, 1280:1792].rearrange("p (a b) -> p a b", a=2)
        ksin = kret[:, 1792:2304].rearrange("p (a b) -> p a b", a=2)
        xn = area(8, 4, D)
        ptmp = area(0, 4, 512)
        gb = area(44, 2, D)
        gn = area(52, D)
        ytmp = area(68, 2, D)

        hid = area(0, FT, TOK)
        hid2 = area(0, FT, SEQ)
        hid3 = area(0, MT, SEQ)
        lin = area(60, 2, 2, TOK)
        ah8, al8 = (v[:, :, :].rearrange("p j (k n) -> p (j k) n", k=2) for v in (ah, al))
        dqk = area(0, 4, 512)
        drot = area(8, 2, 512)
        dqt = area(12, 2, SEQ)
        dkt = area(14, 2, TOK)
        dv = area(18, 4, 256)
        dpr = area(22, 2, 4, TOK)
        dpt = area(60, 2, 4, SEQ)
        dy = area(38, 2, 2, P)
        dcos = kdif[:, 0:128].rearrange("p (a b) -> p a b", a=2)
        dsin = kdif[:, 128:256].rearrange("p (a b) -> p a b", a=2)
        qkt5 = area(0, 5, 4, SEQ)
        zt = area(20, 2, 4, SEQ)
        ki2 = area(28, 2, P)
        kit = area(29, SEQ)
        wiw = area(30, 2, 8)
        maskb = area(31, 2, SEQ)
        wk = area(33, 2, SEQ)
        causal = area(35, 2, SEQ)
        xcv = area(37, 4, SEQ)
        gy = area(41, 4, SEQ)
        rt, it = area(45, 4, SEQ), area(49, 4, SEQ)
        la, lt = area(53, 4, SEQ), area(57, 4, SEQ)
        wri = area(61, 2, 4, 64)
        lg = area(51, 2, 6 * SEQ)
        pts = area(45, 6 * SEQ)
        rl = area(71, 8, SEQ)
        gates3 = [area(kb, 2, 2, 512) for kb in (63, 37, 71)]
        mg, mt = area(0, 4, 512), area(8, 4, 512)
        vab = res[:, 2:4, :].rearrange("p a (b c) -> p (a b) c", b=2)
        hot, tab, zst = area(71, 384)[0:33], area(73, 16)[0:33], area(76, 384)[0:16]
        fout = area(44, 2, D)

        def conv_col(n, k):
            return fcol[:, ds(k + 16, 1)] if n == TOK else fcol2[:, ds(k, 1)]

        def sums_row(row):
            return adat[:, 1, :] if row == 1 else area(30, 512)[0:64]

        def parts_of(u, nt, half):
            if nt == 4:
                return u[:, half * 4:half * 4 + 4, :], ptmp
            return (u[:, half * 4:half * 4 + 4, 0:SEQ],
                    ptmp.rearrange("p b (c n) -> p (b c) n", c=2)[:, half * 4:half * 4 + 4, :])

        def blocks_of(nt, half, mine):
            if nt == 4:
                return [(b, c, half * 4 + b, c) for b in (2 * mine, 2 * mine + 1) for c in range(2)]
            return [(mine, c, half * 4 + 2 * mine + c, 0) for c in range(2)]

        def normed_block(nt, half, b, c):
            x = parts_of(uh, nt, half)[1]
            return x[:, b, c * 256:(c + 1) * 256] if nt == 4 else x[:, 2 * b + c, :]

        def tiles_of(nt, part):
            return range(part * nt // 2, (part + 1) * nt // 2)

        raw_loaded = [sem(f"raw_loaded{j}") for j in range(SLOTS)]
        hi_done = sem("hi_done")
        lo_done = sem("lo_done")
        ak_hi, ak_lo = sem("ak_hi"), sem("ak_lo")
        unit_used = sem("unit_used")
        turned = sem("turned")
        act_evac = sem("act_evac")
        emptied = sem("emptied")
        act_own = sem("act_own")
        vec_own = sem("vec_own")
        ident_loaded, const_loaded = sem("ident_loaded"), sem("const_loaded")
        kdif_loaded = sem("kdif_loaded")
        eps_set = sem("eps_set")
        rows_loaded = [sem("rows_loaded0"), sem("rows_loaded1")]
        cols_ready = sem("cols_ready")
        silu_c = sem("silu_c")
        cvec_hi, cvec_lo = sem("cvec_hi"), sem("cvec_lo")
        bias_loaded = sem("bias_loaded")
        ada_sum = sem("ada_sum")
        ada_stored = sem("ada_stored")
        x_loaded, decay_loaded = sem("x_loaded"), sem("decay_loaded")
        rows_done = sem("rows_done")
        h_ready = sem("h_ready")
        rms_done = sem("rms_done")
        rstd_ready = sem("rstd_ready")
        xn_act, xn_vec = sem("xn_act"), sem("xn_vec")
        acol_ready = sem("acol_ready")
        u_half = sem("u_half")
        u_high = sem("u_high")
        u_low = sem("u_low")
        gate_loaded = sem("gate_loaded")
        z_abs, lg_exp, lg_ready = sem("z_abs"), sem("lg_exp"), sem("lg_ready")
        decay_exp = sem("decay_exp")
        qk_rot = sem("qk_rot")
        y_ready = sem("y_ready")
        ffn_lin = sem("ffn_lin")
        ffn_conv = sem("ffn_conv")
        hot_loaded, tab_set, zrow_ready, zrow_stored = sem("hot_loaded"), sem("tab_set"), sem("zrow_ready"), sem("zrow_stored")
        z_loaded, z_used = [sem("z_loaded0"), sem("z_loaded1")], sem("z_used")
        mix_loaded, causal_loaded = sem("mix_loaded"), sem("causal_loaded")
        out_stored = sem("out_stored")
        lam_loaded, lam_dots, lam_exp = sem("lam_loaded"), sem("lam_dots"), sem("lam_exp")
        exp_done = sem("exp_done")
        nmax_ready = sem("nmax_ready")
        prob_ready = sem("prob_ready")
        xc_lin = sem("xc_lin")
        lru_arg = sem("lru_arg")
        lru_fun = sem("lru_fun")
        lru_sq, lru_root = sem("lru_sq"), sem("lru_root")
        yc_ready = sem("yc_ready")
        yc_hi, yc_lo = sem("yc_hi"), sem("yc_lo")
        merged = sem("merged")
        gain_loaded, out_ready = sem("gain_loaded"), sem("out_ready")

        block = ctx.enter_context(nc.Block())

        S_RETO = 4 + 8 * RH + 4
        S_UP0 = S_RETO + 4
        S_DIF = S_UP0 + 11 + 6
        S_UP1 = S_DIF + 8 + 2
        S_MIX = S_UP1 + 11 + 6
        S_MUP = S_MIX + 16 + 3 + 2

        @block.sync
        def _(sp):
            S = Count()

            def load(parts):
                s = S.next()
                for j in range(SLOTS):
                    if not (isinstance(s, int) and s == 0):
                        sp.wait_ge(lo_done, s * SLOTS + (j - SLOTS + 1))
                    pieces = parts(j)
                    for dst, src in pieces:
                        sp.dma_start(dst, src).then_inc(raw_loaded[j], 32 // len(pieces))

            def cols(w, c0, n=512):
                v = w.rearrange("(j k p) n -> j p k n", k=2, p=P)
                return lambda j: [(raw[:, j, 0:2 * n].rearrange("p (k n) -> p k n", k=2),
                                   v[j][:, :, ds(c0, n)])]

            def pair(w, c0, c1):
                v = w.rearrange("(j k p) n -> j p k n", k=2, p=P)
                return lambda j: [(raw[:, j, :].rearrange("p (k z n) -> p k z n", k=2, z=2)[:, :, z, :],
                                   v[j][:, :, ds(c, 256)]) for z, c in enumerate((c0, c1))]

            def down(w, k0):
                v = w.rearrange("(k p) n -> p k n", p=P)
                return lambda j: [(raw[:, j, :], v[:, k0 + j, :])]

            def down_half(w, k0):
                v = w.rearrange("(k p) n -> p k n", p=P)
                return lambda j: [(raw[:, j, 0:512], v[:, k0 + j // 2, (j % 2) * 512:(j % 2) * 512 + 512])]

            for c in range(4):
                load(cols(a["ada_w"][0], c * 512))
            w = a["ret_w_in"][0]
            kq, kk, kv = RH * RDK, 2 * RH * RDK, RH * RDV
            with sp.Fori(0, RH) as h:
                S.enter(h, 8)
                load(pair(w, h * RDK, h * RDK + kq))
                load(cols(w, h * RDV + kk))
                load(cols(a["ada_w"][0], h * 1024 + 4 * 512))
                load(cols(a["ada_w"][0], h * 1024 + 5 * 512))
                load(cols(w, h * RDV + (kk + kv)))
                load(cols(a["ada_w"][1], h * 1024))
                load(cols(a["ada_w"][1], h * 1024 + 512))
                load(cols(w, h * RDV + (kk + 2 * kv)))
            S.leave(RH)
            for c in range(8, 12):
                load(cols(a["ada_w"][1], c * 512))
            with sp.Fori(0, RH) as i:
                S.enter(i, 1)
                load(down(a["ret_w_out"][0], i * 4))
            S.leave(RH)
            up = a["ffn_w_up"][0]
            with sp.Fori(0, 11) as i:
                S.enter(i, 1)
                load(pair(up, i * 256, i * 256 + FH))
            S.leave(11)
            with sp.Fori(0, 5) as i:
                S.enter(i, 1)
                load(down(a["ffn_w_down"][0], i * 4))
            S.leave(5)
            load(down_half(a["ffn_w_down"][0], 20))
            w = a["diff_w_in"][0]
            with sp.Fori(0, 4) as i:
                S.enter(i, 2)
                load(pair(w, i * 256, i * 256 + D))
                load(cols(w, i * 256 + 2 * D, 256))
            S.leave(4)
            with sp.Fori(0, 2) as i:
                S.enter(i, 1)
                load(down(a["diff_w_out"][0], i * 4))
            S.leave(2)
            up = a["ffn_w_up"][1]
            with sp.Fori(0, 11) as i:
                S.enter(i, 1)
                load(pair(up, i * 256, i * 256 + FH))
            S.leave(11)
            with sp.Fori(0, 5) as i:
                S.enter(i, 1)
                load(down(a["ffn_w_down"][1], i * 4))
            S.leave(5)
            load(down_half(a["ffn_w_down"][1], 20))
            w = a["w_in_2"][0]
            with sp.Fori(0, 7) as i:
                S.enter(i, 1)
                load(cols(w, i * 512))
            S.leave(7)
            load(cols(w, W2["kw"], 72))
            with sp.Fori(0, 8) as i:
                S.enter(i, 1)
                load(cols(w, i * 512 + W2["xc"]))
            S.leave(8)
            for name in ("w_pa_2", "w_pb_2", "w_pc_2"):
                load(down(a[name][0], 0))
            with sp.Fori(0, 2) as i:
                S.enter(i, 1)
                load(down(a["w_o_2"][0], i * 4))
            S.leave(2)
            with sp.Fori(0, 8) as i:
                S.enter(i, 1)
                load(cols(a["w_up_2"][0], i * 512))
            S.leave(8)
            with sp.Fori(0, 8) as i:
                S.enter(i, 1)
                load(down(a["w_down_2"][0], i * 4))
            S.leave(8)

        @block.tensor
        def _(pe):
            S, G, A = Count(), Count(), Count()

            def open_group():
                half = 4 * (G.base % 2)
                g = G.next()
                if not (isinstance(g, int) and g < 2):
                    pe.wait_ge(emptied, g - 1)
                return half

            def three(o, lh, ll, rh, rl, first, last):
                pe.matmul(o, lh, rh, start=first, stop=False)
                pe.matmul(o, lh, rl, start=False, stop=False)
                return pe.matmul(o, ll, rh, start=False, stop=last)

            def units(fresh=False):
                s = S.next()
                for j in range(SLOTS):
                    pe.wait_ge(lo_done, s * SLOTS + (j + 1))
                    if fresh:
                        pe.wait_ge(u_low, SLOTS * (turned_norms[0] - 1) + (j + 1))
                    yield j

            def step_tokens(tiles, n=512, skip=lambda t: 0, fresh=False):
                hb = open_group()
                for j in units(fresh):
                    for k in range(2):
                        for t in tiles:
                            c = skip(t)
                            rh, rl = (w[:, j, k * n + c:(k + 1) * n] for w in (wh, wl))
                            f = 2 * j + k
                            mm = three(ps[:, hb + t, c:n], uh[:, f, t * P:(t + 1) * P], ul[:, f, t * P:(t + 1) * P],
                                       rh, rl, f == 0, f == KD - 1)
                    mm.then_inc(unit_used, 1)

            def step_features(n, fresh=False):
                hb = open_group()
                for j in units(fresh):
                    for k in range(2):
                        for m in range(4):
                            f = 2 * j + k
                            lh, ll = (w[:, j, k * 512 + m * P:k * 512 + (m + 1) * P] for w in (wh, wl))
                            mm = three(ps[:, hb + m, 0:n], lh, ll, uh[:, f, 0:n], ul[:, f, 0:n],
                                       f == 0, f == KD - 1)
                    mm.then_inc(unit_used, 1)

            def step_ada():
                hb = open_group()
                for j in units():
                    for k in range(2):
                        f = 2 * j + k
                        pe.matmul(ps[:, hb, :], ch[:, f, :], wh[:, j, k * 512:(k + 1) * 512],
                                  start=f == 0, stop=False)
                        mm = pe.matmul(ps[:, hb, :], ch[:, f, :], wl[:, j, k * 512:(k + 1) * 512],
                                       start=False, stop=f == KD - 1)
                    mm.then_inc(unit_used, 1)

            def step_down(bank0, tiles, first, last, late=True, kt=None, half=False, src=None, finish=False):
                if late:
                    x = A.next()
                s, n = S.next(), len(tiles) // 2
                passes = [tiles[:n], tiles[n:]] if finish else [tiles]
                for p, some in enumerate(passes):
                    for j in range(SLOTS):
                        if p == 0:
                            pe.wait_ge(lo_done, s * SLOTS + (j + 1))
                            if late:
                                pe.wait_ge(ak_lo, x * SLOTS + (j + 1))
                        for t in some:
                            if kt is None:
                                lh, ll = ah[:, j, t * P:(t + 1) * P], al[:, j, t * P:(t + 1) * P]
                            else:
                                lh, ll = (v[:, kt + j, t * P:(t + 1) * P] for v in (src or (ah8, al8)))
                            for c in ((j % 2,) if half else (0, 1)):
                                w0 = 0 if half else c * 512
                                mm = three(ps[:, bank0(t) + c, :], lh, ll, wh[:, j, w0:w0 + 512], wl[:, j, w0:w0 + 512],
                                           first and j == 0, last and (j >= 2 if half else j == SLOTS - 1))
                        if p == len(passes) - 1:
                            mm.then_inc(unit_used, 1)
                        elif j == SLOTS - 1:
                            mm.then_inc(rows_done, 1)

            def turn_rows(batch, n, loads):
                pe.wait_ge(rows_loaded[batch % 2], 16 * loads)
                hb = open_group()
                pe.transpose(ps[:, hb, 0:n], rows[0:n, batch % 2, :], ident[0:n, 0:n]).then_inc(turned, 1)

            turned_norms = [0]

            def turn_normed(nt):
                halves = [open_group()]
                turned_norms[0] += 1

                def turn(hb, half, part):
                    for b in range(4):
                        for t in tiles_of(nt, part):
                            f = half * 4 + b
                            o = ps[:, hb + b, t * P:(t + 1) * P] if nt == 4 else \
                                ps[:, hb + b // 2, (b % 2) * 256 + t * P:(b % 2) * 256 + (t + 1) * P]
                            mm = pe.transpose(o, xn[:, t, f * P:(f + 1) * P], ident[:, :])
                    return mm

                for part in range(2):
                    for t in tiles_of(nt, part):
                        v, x = (vec_turned, act_turned)[t % 2], (xn_vec, xn_act)[t % 2]
                        v[0] += 1
                        pe.wait_ge(x, v[0])
                    for half in range(2):
                        if half and not part:
                            if turned_norms[0] > 1:
                                keep_clock(ps[:, halves[0] + 3, 384:TOK], 16)
                            halves.append(open_group())
                        mm = turn(halves[half], half, part)
                        if part:
                            mm.then_inc(turned, 1)
                    if not part and turned_norms[0] > 1:
                        keep_clock(ps[:, halves[0] + 3, 384:TOK], 10)

            vec_turned, act_turned = [0], [0]

            def keep_clock(o, n):
                for _ in range(n):
                    pe.matmul(o, ident[:, :], ident[:, :], start=True, stop=True)

            def all_emptied():
                pe.wait_ge(emptied, G.now())

            pe.wait_ge(ident_loaded, 16)
            turn_rows(0, 104, 4)
            turn_rows(1, 113, 9)
            pe.wait_ge(cvec_lo, 1)
            def turn_sums(c):
                pe.wait_ge(ada_sum, c + 1)
                hb = open_group()
                for b in range(4):
                    mm = pe.transpose(ps[:, hb, b * 64:(b + 1) * 64], sums_row(1 + c % 2)[:, b * P:(b + 1) * P], ident[0:64, 0:64])
                mm.then_inc(turned, 1)

            for c in range(4):
                step_ada()
                if c:
                    turn_sums(c - 1)
            turn_sums(3)
            pe.wait_ge(hot_loaded, 32)
            pe.wait_ge(tab_set, 1)
            hb = open_group()
            pe.matmul(ps[0:16, hb, 0:384], tab, hot, start=True, stop=True).then_inc(turned, 1)
            turn_normed(4)

            def attend(v0, reads):
                hb = open_group()
                for t, blocks in enumerate(reads):
                    for n, (c, k) in enumerate(blocks):
                        mm = pe.matmul(ps[:, hb + t, :], v0[:, c:c + P], vres[:, k, :],
                                       start=n == 0, stop=n == len(blocks) - 1)
                mm.then_inc(turned, 1)

            def turn_gated():
                for pairs in range(2):
                    hb = open_group()
                    for b in range(2):
                        for t in range(4):
                            f = 2 * pairs + b
                            mm = pe.transpose(ps[:, hb + b, t * P:(t + 1) * P], sgf[:, t, f * P:(f + 1) * P], ident[:, :])
                    mm.then_inc(turned, 1)

            def head(h, before):
                step_tokens(range(4), fresh=True)
                step_tokens(range(4))
                step_ada()
                if before:
                    pe.wait_ge(y_ready, h)
                    turn_gated()
                pe.wait_ge(qk_rot, h + 1)
                hb = open_group()
                for b in range(4):
                    for t in range(4):
                        mm = pe.transpose(ps[:, hb + b, t * P:(t + 1) * P], qk[:, t, b * P:(b + 1) * P], ident[:, :])
                mm.then_inc(turned, 1)
                rotated = G.now()
                step_ada()
                step_tokens(range(4))
                pe.wait_ge(emptied, rotated)
                hb = open_group()
                for k in range(4):
                    n = 256 if k < 2 else 512
                    for f in range(2):
                        mm = pe.matmul(ps[:, hb + k, 0:n], qkt[:, 2 + f, k * P:(k + 1) * P], qkt[:, f, 0:n],
                                       start=f == 0, stop=f == 1)
                mm.then_inc(turned, 1)
                step_ada()
                step_ada()
                step_tokens(range(4))
                pe.wait_ge(emptied, G.now() - 1)
                attend(pf, FWD_READS)
                attend(pb, BWD_READS)

            head(0, False)
            with pe.Fori(0, RH - 1) as i:
                S.enter(i, 8)
                G.enter(i, 14)
                head(i + 1, True)
            S.leave(RH - 1)
            G.leave(RH - 1)
            turn_rows(3, 96, 11)
            turn_rows(4, 88, 6)
            for _ in range(4):
                step_ada()
            pe.wait_ge(y_ready, RH)
            turn_gated()


            def project(nt, steps, late=True, src=None, half_last=False, kt=0):
                halves = [open_group() for _ in range(nt // 2)]
                bank0 = lambda t: halves[t // 2] + 2 * (t % 2)
                tiles = range(nt)
                k = lambda s: None if late else kt + 4 * s
                step_down(bank0, tiles, True, False, late, k(0), src=src)
                if steps > 2 and late:
                    with pe.Fori(0, steps - 2) as i:
                        S.enter(i, 1)
                        A.enter(i, 1)
                        step_down(bank0, tiles, False, False)
                    S.leave(steps - 2)
                    A.leave(steps - 2)
                step_down(bank0, tiles, False, True, late, k(steps - 1), half_last, src=src, finish=True)

            project(4, 4)
            turn_normed(4)
            with pe.Fori(0, 5) as i:
                S.enter(i, 2)
                G.enter(i, 2)
                step_features(TOK, fresh=True)
                step_features(TOK)
            S.leave(5)
            G.leave(5)
            step_features(TOK)
            turn_rows(5, 96, 13)
            project(4, 6, half_last=True)
            turn_normed(4)

            def attend_pair(i, steps):
                pe.wait_ge(qk_rot, i + (RH + 1))
                hb = open_group()
                for h in range(2):
                    for t in range(2):
                        pe.transpose(ps[:, hb, h * SEQ + t * P:h * SEQ + (t + 1) * P], dqk[:, t, h * P:(h + 1) * P], ident[:, :])
                    for t in range(4):
                        mm = pe.transpose(ps[:, hb + 1 + h, t * P:(t + 1) * P],
                                          dqk[:, t, 256 + h * P:256 + (h + 1) * P], ident[:, :])
                mm.then_inc(turned, 1)
                pe.wait_ge(emptied, G.now())
                for h in range(2):
                    hb = open_group()
                    for t in range(2):
                        for c in range(2):
                            r = slice(64 * c, 64 * c + 64)
                            mm = pe.matmul(ps[:, hb + 2 * c + t, :], dqt[r, h, t * P:(t + 1) * P], dkt[r, h, :],
                                           start=True, stop=True)
                    mm.then_inc(turned, 1)
                if steps:
                    step_tokens(range(4), 512, lambda t: 0 if t < 2 else 256)
                for h in range(2):
                    pe.wait_ge(prob_ready, i * 2 + (h + 1))
                    hb = open_group()
                    for k in range(4):
                        for t in range(2):
                            c = (k % 2) * SEQ + t * P
                            mm = pe.transpose(ps[:, hb + k // 2, c:c + P], dpr[:, h, t, k * P:(k + 1) * P], ident[:, :])
                    mm.then_inc(turned, 1)
                for h in range(2):
                    pe.wait_ge(emptied, G.now() - 1)
                    hb = open_group()
                    for t in range(2):
                        for k in range(4):
                            mm = pe.matmul(ps[:, hb, t * P:(t + 1) * P], dpt[:, h, k, t * P:(t + 1) * P],
                                           dv[:, k, h * P:(h + 1) * P], start=k == 0, stop=k == 3)
                    mm.then_inc(turned, 1)
                outputs = G.now()
                if steps:
                    step_tokens(range(4), 256)
                pe.wait_ge(emptied, outputs)
                hb = open_group()
                for h in range(2):
                    for t in range(2):
                        mm = pe.transpose(ps[:, hb, h * SEQ + t * P:h * SEQ + (t + 1) * P], dy[:, h, t, :], ident[:, :])
                mm.then_inc(turned, 1)
                keep_clock(ps[:, hb + 3, 0:P], 6)

            step_tokens(range(4), 512, lambda t: 0 if t < 2 else 256, fresh=True)
            step_tokens(range(4), 256)
            with pe.Fori(0, DH // 2 - 1) as i:
                S.enter(i, 2)
                G.enter(i, 10)
                attend_pair(i, True)
            S.leave(DH // 2 - 1)
            G.leave(DH // 2 - 1)
            attend_pair(DH // 2 - 1, False)
            all_emptied()
            project(2, 2, late=False)
            turn_normed(2)
            with pe.Fori(0, 5) as i:
                S.enter(i, 2)
                G.enter(i, 2)
                step_features(SEQ, fresh=True)
                step_features(SEQ)
            S.leave(5)
            G.leave(5)
            step_features(SEQ)
            project(2, 6, half_last=True)
            turn_normed(2)

            for n, kind in enumerate("fftfftf"):
                if kind == "f":
                    step_features(SEQ, fresh=n == 0)
                else:
                    step_tokens(range(2))
            step_tokens(range(2), 72)
            keys = G.now()
            step_features(SEQ)
            conv = G.now()
            step_features(SEQ)
            pe.wait_ge(emptied, keys)
            hb = open_group()
            for t in range(2):
                mm = pe.transpose(ps[:, hb, t * P:(t + 1) * P], ki2[:, t, :], ident[:, :])
            mm.then_inc(turned, 1)
            keys = G.now()
            step_tokens(range(2))
            pe.wait_ge(mix_loaded, 64)
            pe.wait_ge(emptied, conv)
            hb = open_group()
            for z in range(2):
                for b in range(8):
                    r, m = slice(64 * (b % 2), 64 * (b % 2) + 64), b // 2
                    mm = pe.matmul(ps[r, hb + 2 * z + m // 2, (m % 2) * SEQ:(m % 2 + 1) * SEQ], wri[r, z, m, :],
                                   xcv[r, m, :], start=True, stop=True)
            mm.then_inc(turned, 1)

            def head_rows(h):
                return slice(64 * (h % 2), 64 * (h % 2) + 64), h // 2

            pe.wait_ge(emptied, keys)
            for t, n in ((1, SEQ), (0, P)):
                hb = open_group()
                for h in range(8):
                    r, m = head_rows(h)
                    c = ((h % 2) * 4 + h // 2) * n
                    mm = pe.matmul(ps[:, hb + c // 512, c % 512:c % 512 + n], qkt5[r, 4, m, t * P:(t + 1) * P],
                                   kit[r, 0:n], start=True, stop=True)
                mm.then_inc(turned, 1)
                if t == 1:
                    step_tokens(range(2))

            def attend_scores(n):
                z, g = n // 2, n % 2
                hb = open_group()
                for t, bank, n in ((1, 0, SEQ), (0, 2, P)):
                    for x in range(4):
                        r, m = head_rows(4 * g + x)
                        i = x // 2
                        mm = pe.matmul(ps[:, hb + bank + x % 2, i * n:(i + 1) * n], qkt5[r, 2 * z, m, t * P:(t + 1) * P],
                                       qkt5[r, 2 * z + 1, m, 0:n], start=True, stop=True)
                mm.then_inc(turned, 1)

            def turn_probabilities(n):
                pe.wait_ge(prob_ready, DH + n + 1)
                e = lg[:, n % 2, :]
                hb = open_group()
                for x in range(4):
                    o = (x % 2) * SEQ
                    pe.transpose(ps[:, hb + x // 2, o:o + P], e[:, 1024 + x * P:1024 + (x + 1) * P], ident[:, :])
                    pe.transpose(ps[:, hb + x // 2, o + P:o + SEQ], e[:, x * SEQ:x * SEQ + P], ident[:, :])
                    mm = pe.transpose(ps[:, hb + 2, x * P:(x + 1) * P], e[:, x * SEQ + P:(x + 1) * SEQ], ident[:, :])
                mm.then_inc(turned, 1)

            def attend_values(n, probabilities):
                z, g = n // 2, n % 2
                pe.wait_ge(emptied, probabilities)
                hb = open_group()
                for pair in range(2):
                    for t in range(2):
                        for x in (2 * pair, 2 * pair + 1):
                            h = 4 * g + x
                            r = head_rows(h)[0]
                            o = pair * SEQ
                            i = (x % 2) * 2 + pair
                            w, c = (SEQ, i * SEQ) if t == 0 else (P, 1024 + i * P)
                            mm = pe.matmul(ps[r, hb, o + SEQ - w:o + SEQ], vab[:, 2 * z + t, h * HD:(h + 1) * HD],
                                           pts[:, c:c + w], start=t == 0, stop=t == 1)
                mm.then_inc(turned, 1)

            attend_scores(0)
            for n in range(4):
                step_tokens(range(2))
                turn_probabilities(n)
                probabilities = G.now()
                if n < 3:
                    attend_scores(n + 1)
                attend_values(n, probabilities)
            values = G.now()
            pe.wait_ge(yc_lo, 1)
            for lh8, ll8, kt in ((ah8, al8, 0), (ah8, al8, 4), (uh[:, :, SEQ:TOK], ul[:, :, SEQ:TOK], 0)):
                if kt == 4:
                    pe.wait_ge(emptied, values)
                hb = open_group()
                step_down(lambda t: hb + 2 * t, range(2), True, True, late=False, kt=kt, src=(lh8, ll8))
            pe.wait_ge(merged, 1)
            hb = open_group()
            for f in range(KD):
                for t in range(2):
                    c = (f % 2) * SEQ + t * P
                    mm = pe.transpose(ps[:, hb + f // 2, c:c + P], mg[:, 2 * t + f // 4, (f % 4) * P:(f % 4 + 1) * P], ident[:, :])
            mm.then_inc(turned, 1)
            all_emptied()
            project(2, 2, late=False, src=(uh[:, :, SEQ:TOK], ul[:, :, SEQ:TOK]))
            turn_normed(2)
            with pe.Fori(0, 4) as i:
                S.enter(i, 2)
                G.enter(i, 2)
                step_features(SEQ, fresh=True)
                step_features(SEQ)
            S.leave(4)
            G.leave(4)
            project(2, 8)

        @block.scalar
        def _(act):
            T = Track(act)
            W, S, Q = Count(), Count(), Count()
            par = Count()
            A = Count()
            norms = [0]

            def split(size=UNIT, late=None, n=0):
                s = W.next()
                if late:
                    A.next()
                for j in range(SLOTS):
                    act.wait_ge(raw_loaded[j], s * 32 + 32)
                    if not (isinstance(s, int) and s == 0):
                        act.wait_ge(unit_used, s * SLOTS + (j - SLOTS + 1))
                    T.mark(act.activation(wh[:, j, 0:size], raw[:, j, 0:size], ACT.Copy), hi_done)
                    if late:
                        T.mark(act.activation(ah[:, j, 0:n], late(j), ACT.Copy), ak_hi)

            def step_full():
                half = 4 * (par.base % 2)
                par.next()
                T.settle()
                act.wait_ge(unit_used, S.next() * SLOTS + SLOTS)
                return half

            def group_full():
                half = 4 * (par.base % 2)
                par.next()
                T.settle()
                act.wait_ge(turned, Q.next() + 1)
                return half

            def skip_group():
                par.next()
                Q.next()

            def read_ada(row=1):
                hb = step_full()
                if not (isinstance(par.now(), int) and S.now() == 1):
                    act.wait_ge(ada_stored, 16 * ada.now())
                ada.next()
                T.mark(act.activation(sums_row(row), ps[64:128, hb, :], ACT.Copy), act_evac)

            ada = Count()

            def rms(tiles, src, width, cols, waits=None):
                for t in tiles:
                    if waits:
                        waits(t)
                    if T.last is not None:
                        T.settle()
                    T.mark(act.activation(junk[:, 0:width], src(t), ACT.Square, scale=float(width) ** -0.5,
                                          accum_out=st[:, cols[0] + t:cols[0] + t + 1]), act_own)
                T.settle()
                n = len(tiles)
                return act.activation(st[:, cols[1] + tiles[0]:cols[1] + tiles[0] + n],
                                      st[:, cols[0] + tiles[0]:cols[0] + tiles[0] + n], ACT.Sqrt, bias=epsc[:, 0:1])

            def norm_rows(nt, part):
                tiles = tiles_of(nt, part)
                rms_parts[0] += 1
                T.mark(rms(tiles, lambda t: res[:, t, :], D, (0, 4)), rms_done)
                act.wait_ge(rstd_ready, rms_parts[0])
                for t in tiles:
                    if t % 2:
                        T.mark(act.activation(xn[:, t, :], res[:, t, :], ACT.Copy, scale=st[:, 8 + t:9 + t]), xn_act)

            rms_parts = [0]

            def prep(nt):
                norms[0] += 1
                act.wait_ge(acol_ready, norms[0])
                for half in range(2):
                    hb = group_full()
                    if half and nt == 4:
                        act.wait_ge(u_low, 4 * norms[0] - 2)
                    for b, c, f, k in blocks_of(nt, half, 0):
                        T.mark(act.activation(normed_block(nt, half, b, c), ps[:, hb + b, c * 256:(c + 1) * 256],
                                              ACT.Identity, scale=acol[:, k, f:f + 1], bias=shift(k, f)), act_own)
                    T.settle()
                    u, x = parts_of(uh, nt, half)
                    T.mark(act.activation(u[:, 0:2, :], x[:, 0:2, :], ACT.Copy), u_high)
                    halves[0] += 1
                    act.wait_ge(u_half, halves[0])
                    T.mark(act.activation(u[:, 2:4, :], x[:, 2:4, :], ACT.Copy), act_evac)

            def start_late(src, n, done):
                if done:
                    act.wait_ge(emptied, done)
                T.settle()
                A.next()
                for j in range(SLOTS):
                    T.mark(act.activation(ah[:, j, 0:n], src(j), ACT.Copy), ak_hi)

            shift0 = [0]
            halves = [0]

            def shift(k, f):
                return 0.0 if shift0[0] is None else mcol[:, k, shift0[0] + f:shift0[0] + f + 1]

            split()
            skip_group()
            skip_group()
            act.wait_ge(cols_ready, 1)
            T.mark(act.activation(cs[:, :, :].rearrange("p f c -> p c f"),
                                  fcol[:, 0:16].rearrange("p (c f) -> p c f", c=2), ACT.Silu), silu_c)
            T.settle()
            T.mark(act.activation(ch[:, :, 0:64].rearrange("p f (c n) -> p f c n", c=2),
                                  cs[:, :, :].unsqueeze(3).to_broadcast([P, 8, 2, 32]), ACT.Copy), cvec_hi)
            for c in range(4):
                split()
                read_ada(1 + c % 2)
                if c:
                    skip_group()
                if c > 1:
                    act.wait_ge(eps_set, 1)
                    act.wait_ge(x_loaded, 32)
                    norm_rows(4, c - 2)
            skip_group()
            skip_group()
            prep(4)
            act.wait_ge(z_abs, 1)
            T.mark(act.activation(lgt[:, 2, :], lgt[:, 1, :], ACT.Exp, scale=-1.0), lg_exp)

            act.wait_ge(const_loaded, 16)
            act.wait_ge(lg_ready, 1)
            def take_gated(k):
                for pairs in range(2):
                    hb = group_full()
                    T.mark(act.activation(yt[:, k + 2 * pairs, :], ps[:, hb, :], ACT.Copy), act_evac)

            def head(h, k, before):
                split()
                hb = step_full()
                T.mark(act.activation(qk[:, 2:4, :], ps[:, hb + 2:hb + 4, :], ACT.Copy), act_evac)
                split()
                hb = step_full()
                T.mark(act.activation(vres, ps[:, hb:hb + 4, :], ACT.Copy), act_evac)
                read_ada()
                split()
                if before:
                    take_gated(k)
                for z in range(2):
                    T.mark(act.activation(dec[:, z, :], kdist[:, z, :], ACT.Exp,
                                          scale=lgt[:, 4, ds(h + 4 * z, 1)]), (act_own, decay_exp)[z])
                hb = group_full()
                T.mark(act.activation(qkt[:, 0:2, :], ps[:, hb:hb + 2, :], ACT.Copy), act_evac)
                split()
                read_ada()
                split()
                hb = step_full()
                T.mark(act.activation(sgf, ps[:, hb:hb + 4, :], ACT.Silu), act_evac)
                skip_group()
                split()
                read_ada()
                split()
                read_ada()
                split()
                hb = step_full()
                T.mark(act.activation(sgb, ps[:, hb:hb + 4, :], ACT.Silu), act_evac)
                for z in range(2):
                    hb = group_full()
                    T.mark(rms(range(4), lambda t: ps[:, hb + t, :], RDV, (16 + 4 * z, 24 + 4 * z)), act_evac)

            head(0, 0, False)
            with act.Fori(0, RH - 1) as i:
                for c, n in ((W, 8), (S, 8), (Q, 6), (par, 14), (ada, 4)):
                    c.enter(i, n)
                T.enter(i, {hi_done: 32, act_evac: 13, act_own: 9, decay_exp: 1})
                head(i + 1, i * 4, True)
            for c in (W, S, Q, par, ada):
                c.leave(RH - 1)
            T.leave(RH - 1)
            skip_group()
            skip_group()
            for n in range(4):
                if n == 3:
                    start_late(lambda j: yt[:, j, :], TOK, 0)
                split()
                read_ada()
            take_gated(4 * (RH - 1))


            def project(nt, steps, source, after, last_size=UNIT):
                n = nt * P
                act.wait_ge(emptied, after)
                T.settle()
                if steps > 2:
                    with act.Fori(0, steps - 2) as i:
                        W.enter(i, 1)
                        A.enter(i, 1)
                        T.enter(i, {hi_done: 4, ak_hi: 4})
                        split(UNIT, lambda j: source(i * 4 + (4 + j)), n)
                    W.leave(steps - 2)
                    A.leave(steps - 2)
                    T.leave(steps - 2)
                k0 = 4 * (steps - 1)
                split(last_size, lambda j: source(k0 + (j // 2 if last_size < UNIT else j)), n)
                S.base += steps
                finish_rows(nt)

            def rows_full(part):
                if part == 0:
                    projections[0] += 1
                    act.wait_ge(rows_done, projections[0])
                else:
                    act.wait_ge(unit_used, S.now() * SLOTS)

            def finish_rows(nt):
                halves = [4 * ((par.base + z) % 2) for z in range(nt // 2)]
                par.base += nt // 2
                bank = lambda t: halves[t // 2] + 2 * (t % 2)
                for part in range(2):
                    rows_full(part)
                    T.mark(rms(tiles_of(nt, part), lambda t: ps[:, bank(t):bank(t) + 2, :], D, (0, 4)), act_evac)
                    if part:
                        split()
                    wait_residual(part)
                    norm_rows(nt, part)

            def wait_residual(part):
                act.wait_ge(h_ready, 2 * projections[0] - 1 + part)

            projections = [0]
            F = Count()

            def read_ffn(ft, n):
                p = par.base % 2
                hb = step_full()
                for m in range(2):
                    T.mark(act.activation(lin[:, p, m, 0:n], ps[:, hb + 2 + m, 0:n], ACT.Identity,
                                          scale=conv_col(n, ft + (FT + m)), bias=conv_col(n, ft + (3 * FT + m))),
                           (act_own, ffn_lin)[m])
                act.wait_ge(ffn_conv, F.next() + 1)
                T.mark(act.activation(lin[:, p, :, 0:n], lin[:, p, :, 0:n], ACT.Silu), act_evac)

            project(4, 4, lambda k: yt[:, k, :], par.now())
            shift0[0] = 24
            prep(4)
            first = par.now()
            with act.Fori(0, 5) as i:
                for c, n in ((W, 2), (S, 2), (par, 2), (F, 2)):
                    c.enter(i, n)
                T.enter(i, {hi_done: 8, act_evac: 2, act_own: 2, ffn_lin: 2})
                split()
                read_ffn(i * 4, TOK)
                split()
                read_ffn(i * 4 + 2, TOK)
            for c in (W, S, par, F):
                c.leave(5)
            T.leave(5)
            split()
            start_late(lambda j: hid[:, j, :], TOK, first + 2)
            read_ffn(20, TOK)
            after = par.now()
            skip_group()
            project(4, 6, lambda k: hid[:, k, :], after, 512)
            shift0[0] = 0
            prep(4)

            act.wait_ge(lam_dots, 1)
            T.mark(act.activation(lamt[:, 2:4], lamt[:, 0:2], ACT.Exp), lam_exp)
            def take_qk(size):
                split(size)
                hb = step_full()
                T.mark(act.activation(dqk[:, 2:4, 256:512], ps[:, hb + 2:hb + 4, 256:512], ACT.Copy), act_evac)

            def take_v():
                split()
                hb = step_full()
                T.mark(act.activation(dv[:, 0:2, :], ps[:, hb:hb + 2, 0:256], ACT.Copy), act_evac)

            def attend_pair(i, steps):
                hb = group_full()
                T.mark(act.activation(dqt, ps[:, hb, :].rearrange("p (h n) -> p h n", h=2), ACT.Copy), act_own)
                T.mark(act.activation(dkt[:, 0, :], ps[:, hb + 1, :], ACT.Copy), act_evac)
                for h in range(2):
                    hb = group_full()
                    act.wait_ge(nmax_ready, i * 2 + (h + 1))
                    for b in range(4):
                        T.mark(act.activation(dpr[:, h, b, :], ps[:, hb + b, :], ACT.Exp, scale=DD ** -0.5,
                                              bias=st[:, 40 + 4 * h + b:41 + 4 * h + b],
                                              accum_out=st[:, 48 + 4 * h + b:49 + 4 * h + b]),
                               act_evac if b == 3 else act_own)
                if steps:
                    take_qk(512)
                for h in range(2):
                    hb = group_full()
                    T.mark(act.activation(dpt[:, h, 0:2, :], ps[:, hb, :].rearrange("p (k n) -> p k n", k=2), ACT.Copy), act_evac)
                for h in range(2):
                    hb = group_full()
                    T.mark(rms(range(2), lambda t: ps[:, hb, t * P:(t + 1) * P], P, (16 + 2 * h, 20 + 2 * h)), act_evac)
                if steps:
                    take_v()
                hb = group_full()
                T.mark(act.activation(ah8[:, ds(i * 2, 2), :], ps[:, hb, :].rearrange("p (h n) -> p h n", h=2), ACT.Copy,
                                      scale=lamt[:, 5:6]), act_evac)

            take_qk(512)
            take_v()
            with act.Fori(0, DH // 2 - 1) as i:
                for c, n in ((W, 2), (S, 2), (Q, 8), (par, 10)):
                    c.enter(i, n)
                T.enter(i, {hi_done: 8, act_evac: 10, act_own: 11})
                attend_pair(i, True)
            for c in (W, S, Q, par):
                c.leave(DH // 2 - 1)
            T.leave(DH // 2 - 1)
            attend_pair(DH // 2 - 1, False)
            split()
            S.base += 2
            finish_rows(2)
            shift0[0] = 24
            prep(2)
            first = par.now()
            with act.Fori(0, 5) as i:
                for c, n in ((W, 2), (S, 2), (par, 2), (F, 2)):
                    c.enter(i, n)
                T.enter(i, {hi_done: 8, act_evac: 2, act_own: 2, ffn_lin: 2})
                split()
                read_ffn(i * 4, SEQ)
                split()
                read_ffn(i * 4 + 2, SEQ)
            for c in (W, S, par, F):
                c.leave(5)
            T.leave(5)
            split()
            start_late(lambda j: hid2[:, j, :], SEQ, first + 2)
            read_ffn(20, SEQ)
            project(2, 6, lambda k: hid2[:, k, :], par.now(), 512)
            shift0[0] = None
            prep(2)

            def read_half(dst):
                hb = step_full()
                T.mark(act.activation(dst[:, 0:2, :], ps[:, hb:hb + 2, 0:SEQ], ACT.Copy), act_evac)

            def read_values(dst):
                hb = step_full()
                T.mark(act.activation(dst, ps[:, hb, :], ACT.Copy), act_evac)

            split()
            read_half(qkt5[:, 0])
            split()
            read_half(qkt5[:, 1])
            split()
            read_values(vab[:, 0, :])
            split()
            read_half(qkt5[:, 2])
            split()
            read_half(qkt5[:, 3])
            split()
            read_values(vab[:, 2, :])
            split(144)
            read_half(qkt5[:, 4])
            split()
            hb = step_full()
            for t in range(2):
                T.mark(act.activation(ki2[:, t, :].rearrange("p (z n) -> p z n", z=2),
                                      ps[:, hb + t, 0:64].unsqueeze(1).to_broadcast([P, 2, 64]), ACT.Copy), (act_own, act_evac)[t])
            split()
            hb = step_full()
            for m in range(4):
                T.mark(act.activation(xcv[:, m, :], ps[:, hb + m, 0:SEQ], ACT.Identity,
                                      scale=gcol[:, CW0 + 12 + m:CW0 + 13 + m], bias=gcol[:, CB0 + m:CB0 + m + 1]),
                       xc_lin if m == 3 else act_own)
            split()
            hb = step_full()
            T.mark(act.activation(gy, ps[:, hb:hb + 4, 0:SEQ], ACT.Gelu_apprx_tanh), act_evac)
            def take_gate(c):
                split()
                hb = step_full()
                if c == 2:
                    act.wait_ge(yc_lo, 1)
                if c == 4:
                    act.wait_ge(emptied, indexed)
                T.mark(act.activation(gates3[c // 2][:, :, c % 2, :], ps[:, hb:hb + 2, :], ACT.Sigmoid), act_evac)

            skip_group()
            take_gate(0)
            hb = group_full()
            for z, (dst, b0) in enumerate(((rt, BR0), (it, BI0))):
                for m in range(4):
                    T.mark(act.activation(dst[:, m, :], ps[:, hb + 2 * z + m // 2, (m % 2) * SEQ:(m % 2 + 1) * SEQ],
                                          ACT.Sigmoid, bias=gcol[:, b0 + m:b0 + m + 1]),
                           act_evac if (z, m) == (1, 3) else act_own)
            for t, n in ((1, SEQ), (0, P)):
                hb = group_full()
                if t == 0:
                    act.wait_ge(emptied, par.now() - 2)
                banks = 4 if n == SEQ else 2
                T.mark(act.activation(rl[:, 0:banks * 2, :], ps[:, hb:hb + banks, :].rearrange("p b (x n) -> p (b x) n", x=2),
                                      ACT.Relu), act_evac)
                if t == 1:
                    act.wait_ge(lru_arg, 1)
                    T.mark(act.activation(la, rt, ACT.Exp, scale=-1.0), act_own)
                    T.mark(act.activation(lt, rt, ACT.Tanh), lru_fun)
                    take_gate(1)
            indexed = par.now()
            act.wait_ge(lru_sq, 1)
            T.mark(act.activation(lt, lt, ACT.Sqrt), lru_root)
            skip_group()

            def softmax(n):
                act.wait_ge(nmax_ready, DH + n + 1)
                e, c = lg[:, n % 2, :], 40 + 16 * (n % 2)
                for x in range(8):
                    c0, w = (x * SEQ, SEQ) if x < 4 else (1024 + (x - 4) * P, P)
                    T.mark(act.activation(e[:, c0:c0 + w], e[:, c0:c0 + w], ACT.Exp, bias=st[:, c + x:c + 1 + x],
                                          accum_out=st[:, c + 8 + x:c + 9 + x]), exp_done if x == 7 else act_own)

            act.wait_ge(yc_ready, 1)
            T.mark(act.activation(uh[:, 0:4, SEQ:TOK], gy, ACT.Copy), yc_hi)
            softmax(0)
            for n in range(4):
                take_gate(2 + n)
                hb = group_full()
                T.mark(act.activation(pts[:, 0:1024].rearrange("p (b n) -> p b n", b=2), ps[:, hb:hb + 2, :], ACT.Copy), act_evac)
                if n < 3:
                    skip_group()
                hb = group_full()
                T.mark(act.activation(ah8[:, 2 * n:2 * n + 2, :], ps[:, hb, :].rearrange("p (x n) -> p x n", x=2), ACT.Copy), act_evac)
                if n < 3:
                    softmax(n + 1)
            for _ in range(3):
                split()
                S.next()
                par.next()
            hb = group_full()
            T.mark(act.activation(uh[:, :, SEQ:TOK], ps[:, hb:hb + 4, :].rearrange("p b (x n) -> p (b x) n", x=2), ACT.Copy), act_evac)
            split()
            S.base += 2
            par.next()
            for part in range(2):
                rows_full(part)
                if part:
                    split()
                wait_residual(part)
                norm_rows(2, part)
            prep(2)
            def read_hidden(k):
                split()
                hb = step_full()
                T.mark(act.activation(hid3[:, ds(k, 4), :], ps[:, hb:hb + 4, 0:SEQ], ACT.Relu), act_evac)

            first = par.now()
            with act.Fori(0, 3) as i:
                for c, n in ((W, 2), (S, 2), (par, 2)):
                    c.enter(i, n)
                T.enter(i, {hi_done: 8, act_evac: 2})
                for z in range(2):
                    read_hidden(i * 8 + 4 * z)
            for c in (W, S, par):
                c.leave(3)
            T.leave(3)
            read_hidden(24)
            start_late(lambda j: hid3[:, j, :], SEQ, first + 1)
            read_hidden(28)
            act.wait_ge(emptied, par.now())
            T.settle()
            with act.Fori(0, 7) as i:
                W.enter(i, 1)
                A.enter(i, 1)
                T.enter(i, {hi_done: 4, ak_hi: 4})
                split(UNIT, lambda j: hid3[:, i * 4 + (4 + j), :], SEQ)
            W.leave(7)
            A.leave(7)
            T.leave(7)
            S.base += 8
            for t in range(2):
                rows_full(t)
                wait_residual(t)
                T.mark(rms((t,), lambda t: res[:, t, :], D, (0, 4)), rms_done)

        @block.vector
        def _(vec):
            T = Track(vec)
            W, S, Q, par, E = Count(), Count(), Count(), Count(), Count()
            norms = [0]

            def split(size=UNIT, late=None, n=0, units=range(SLOTS)):
                s = W.next() if units[-1] == SLOTS - 1 else W.now()
                x = A.next() if late else None
                for j in units:
                    vec.wait_ge(hi_done, s * SLOTS + (j + 1))
                    T.mark(vec.tensor_tensor(wl[:, j, 0:size], raw[:, j, 0:size], wh[:, j, 0:size], ALU.subtract), lo_done)
                    if late:
                        vec.wait_ge(ak_hi, x * SLOTS + (j + 1))
                        T.mark(vec.tensor_tensor(al[:, j, 0:n], late(j), ah[:, j, 0:n], ALU.subtract), ak_lo)

            def step_full():
                half = 4 * (par.base % 2)
                par.next()
                T.settle()
                vec.wait_ge(unit_used, S.next() * SLOTS + SLOTS)
                return half

            def group_full():
                half = 4 * (par.base % 2)
                par.next()
                T.settle()
                vec.wait_ge(turned, Q.next() + 1)
                return half

            def tick(sem):
                T.settle()
                T.mark(vec.memset(spare[:, :], 0.0), sem)

            def act_read():
                vec.wait_ge(act_evac, E.next() + 1)

            def close():
                act_read()
                tick(emptied)

            def take_cols(dst, n):
                hb = group_full()
                src = ps[:, hb, 0:n]
                if len(dst.shape) == 3:
                    src = src.rearrange("p (a b) -> p a b", a=dst.shape[1])
                T.mark(vec.tensor_copy(dst, src), cols_ready)
                tick(emptied)

            def read_ada(row=1):
                n = ada.next()
                hb = step_full()
                vec.wait_ge(bias_loaded, n * 16 + 16)
                act_read()
                T.mark(vec.tensor_tensor(sums_row(row), sums_row(row), adat[:, 0, :], ALU.add), vec_own)
                T.settle()
                T.mark(vec.tensor_tensor(sums_row(row), ps[0:64, hb, :], sums_row(row), ALU.add), ada_sum)
                tick(emptied)

            ada = Count()

            def norm_rows(nt, part, early=()):
                tiles = tiles_of(nt, part)
                rms_parts[0] += 1
                if early:
                    split(units=early)
                vec.wait_ge(rms_done, rms_parts[0])
                T.mark(vec.reciprocal(st[:, 8 + tiles[0]:9 + tiles[-1]], st[:, 4 + tiles[0]:5 + tiles[-1]]), rstd_ready)
                T.settle()
                for t in tiles:
                    if t % 2 == 0:
                        T.mark(vec.tensor_scalar(xn[:, t, :], res[:, t, :], st[:, 8 + t:9 + t], None, ALU.mult), xn_vec)

            rms_parts, highs = [0], [0]

            def prep(nt, gain0, scale0):
                for k in range(nt // 2):
                    if scale0 is None:
                        ins = vec.tensor_copy(acol[:, k, :], gcol[:, gain0:gain0 + 8])
                    else:
                        ins = vec.scalar_tensor_tensor(out=acol[:, k, :], in0=mcol[:, k, scale0:scale0 + 8], scalar=1.0,
                                                       in1=gcol[:, gain0:gain0 + 8], op0=ALU.add, op1=ALU.mult)
                    T.mark(ins, acol_ready if k == nt // 2 - 1 else vec_own)
                for half in range(2):
                    hb = group_full()
                    mine = blocks_of(nt, half, 1)
                    for b, c, f, k in mine:
                        T.mark(vec.tensor_scalar(normed_block(nt, half, b, c), ps[:, hb + b, c * 256:(c + 1) * 256],
                                                 acol[:, k, f:f + 1],
                                                 mcol[:, k, scale0 - 8 + f:scale0 - 7 + f] if scale0 is not None else 0.0,
                                                 ALU.mult, ALU.add), u_half if (b, c, f, k) == mine[-1] else vec_own)
                    u, x = parts_of(uh, nt, half)
                    low = parts_of(ul, nt, half)[0]
                    highs[0] += 1
                    vec.wait_ge(u_high, highs[0])
                    T.mark(vec.tensor_tensor(low[:, 0:2, :], x[:, 0:2, :], u[:, 0:2, :], ALU.subtract), u_low)
                    tick(emptied)
                    act_read()
                    T.mark(vec.tensor_tensor(low[:, 2:4, :], x[:, 2:4, :], u[:, 2:4, :], ALU.subtract), u_low)

            split()
            take_cols(fcol[:, 0:104], 104)
            take_cols(gcol[:, 0:113], 113)
            vec.wait_ge(cvec_hi, 1)
            T.mark(vec.tensor_tensor(ch[:, :, 64:128].rearrange("p f (c n) -> p f c n", c=2),
                                     cs[:, :, :].unsqueeze(3).to_broadcast([P, 8, 2, 32]),
                                     ch[:, :, 0:64].rearrange("p f (c n) -> p f c n", c=2), ALU.subtract), cvec_lo)
            def own(ins):
                T.mark(ins, vec_own)
                T.settle()

            def log_sigmoid():
                vec.wait_ge(decay_loaded, 32)
                own(vec.tensor_copy(lgt[:, 0, 8:12], gcol[:, LAM0:LAM0 + 4]))
                T.mark(vec.scalar_tensor_tensor(out=lgt[:, 1, :], in0=lgt[:, 0, :], scalar=-1.0, in1=lgt[:, 0, :],
                                                op0=ALU.mult, op1=ALU.max), z_abs)
                vec.wait_ge(lg_exp, 1)
                e, s, q = lgt[:, 2, :], lgt[:, 1, :], lgt[:, 3, :]
                own(vec.tensor_scalar(s, e, 2.0, None, ALU.add))
                own(vec.reciprocal(s, s))
                own(vec.tensor_tensor(s, e, s, ALU.mult))
                own(vec.tensor_tensor(e, s, s, ALU.mult))
                own(vec.tensor_scalar(q, e, 1.0 / 17, None, ALU.mult))
                for n in (15, 13, 11, 9, 7, 5, 3):
                    own(vec.scalar_tensor_tensor(out=q, in0=q, scalar=1.0 / n, in1=e, op0=ALU.add, op1=ALU.mult))
                own(vec.scalar_tensor_tensor(out=q, in0=q, scalar=1.0, in1=s, op0=ALU.add, op1=ALU.mult))
                own(vec.tensor_scalar(s, lgt[:, 0, :], 0.0, None, ALU.min))
                T.mark(vec.scalar_tensor_tensor(out=lgt[:, 4, :], in0=q, scalar=-2.0, in1=s, op0=ALU.mult, op1=ALU.add), lg_ready)

            def take_sums(c):
                hb = group_full()
                T.mark(vec.tensor_copy(mcol[:, :, 4 * c:4 * c + 4],
                                       ps[:, hb, 0:256].rearrange("p (b k x) -> p k b x", b=4, k=2)[:, :, :, 0]), vec_own)
                tick(emptied)

            for c in range(4):
                split()
                read_ada(1 + c % 2)
                if c:
                    take_sums(c - 1)
                if c > 1:
                    norm_rows(4, c - 2)
            take_sums(3)
            hb = group_full()
            T.mark(vec.tensor_copy(zst, ps[0:16, hb, 0:384]), zrow_ready)
            tick(emptied)
            prep(4, 0, 8)
            log_sigmoid()

            vec.wait_ge(const_loaded, 16)
            A = Count()

            def start_late(src, n):
                x = A.next()
                T.settle()
                for j in range(SLOTS):
                    vec.wait_ge(ak_hi, x * SLOTS + (j + 1))
                    T.mark(vec.tensor_tensor(al[:, j, 0:n], src(j), ah[:, j, 0:n], ALU.subtract), ak_lo)

            def take_gated(k):
                for pairs in range(2):
                    hb = group_full()
                    T.mark(vec.tensor_copy(yt[:, k + (2 * pairs + 1), :], ps[:, hb + 1, :]), vec_own)
                    close()

            def head(h, k, before):
                split()
                hb = step_full()
                for t in range(2):
                    q4 = ps[:, hb + t, :].rearrange("p (z h x n) -> p z h x n", z=2, h=2, x=2)
                    r4 = qkt[:, t, :].rearrange("p (z h x n) -> p z h x n", z=2, h=2, x=2)
                    s3 = ksin[:, t, :].rearrange("p (h x n) -> p h x n", h=2, x=2)
                    T.mark(vec.tensor_tensor(qk[:, t, :].rearrange("p (z n) -> p z n", z=2),
                                             ps[:, hb + t, :].rearrange("p (z n) -> p z n", z=2),
                                             kcos[:, t, :].unsqueeze(1).to_broadcast([P, 2, 256]), ALU.mult), vec_own)
                    for x in range(2):
                        T.mark(vec.tensor_tensor(r4[:, :, :, x, :], q4[:, :, :, 1 - x, :],
                                                 s3[:, :, x, :].unsqueeze(1).to_broadcast([P, 2, 2, 64]), ALU.mult), vec_own)
                T.settle()
                T.mark(vec.tensor_tensor(qk[:, 0, :], qk[:, 0, :], qkt[:, 0, :], ALU.add), vec_own)
                T.mark(vec.tensor_tensor(qk[:, 1, :], qk[:, 1, :], qkt[:, 1, :], ALU.add), vec_own)
                act_read()
                tick(qk_rot)
                tick(emptied)
                split()
                step_full()
                close()
                read_ada()
                split()
                if before:
                    take_gated(k)
                hb = group_full()
                T.mark(vec.tensor_copy(qkt[:, 2:4, :], ps[:, hb + 2:hb + 4, :]), vec_own)
                close()
                split()
                read_ada()
                split()
                step_full()
                close()
                vec.wait_ge(decay_exp, h + 1)
                T.mark(vec.tensor_tensor(dec[:, 0, 0:128], dec[:, 0, 0:128], kmask[:, 0, :], ALU.mult), vec_own)
                T.mark(vec.tensor_tensor(dec[:, 1, 384:512], dec[:, 1, 384:512], kmask[:, 1, :], ALU.mult), vec_own)
                T.settle()
                hb = group_full()
                for z, blocks in enumerate((FWD_BLOCKS, BWD_BLOCKS)):
                    o = 0
                    for n, (kt, q0, w, d0) in enumerate(blocks):
                        last = z == 1 and n == len(blocks) - 1
                        T.mark(vec.scalar_tensor_tensor(out=(pf, pb)[z][:, o:o + w], in0=ps[:, hb + kt, q0:q0 + w],
                                                        scalar=RDK ** -0.5, in1=dec[:, z, d0:d0 + w],
                                                        op0=ALU.mult, op1=ALU.mult), emptied if last else vec_own)
                        o += w
                split()
                read_ada()
                split()
                read_ada()
                split()
                step_full()
                close()
                for z, gate in enumerate((sgf, sgb)):
                    hb = group_full()
                    act_read()
                    T.mark(vec.reciprocal(st[:, 32 + 4 * z:36 + 4 * z], st[:, 24 + 4 * z:28 + 4 * z]), vec_own)
                    T.settle()
                    for t in range(4):
                        T.mark(vec.scalar_tensor_tensor(out=gate[:, t, :], in0=ps[:, hb + t, :],
                                                        scalar=st[:, 32 + 4 * z + t:33 + 4 * z + t], in1=gate[:, t, :],
                                                        op0=ALU.mult, op1=ALU.mult), emptied if t == 3 else vec_own)
                    if z:
                        T.settle()
                        T.mark(vec.tensor_tensor(sgf, sgf, sgb, ALU.add), y_ready)

            head(0, 0, False)
            with vec.Fori(0, RH - 1) as i:
                for c, n in ((W, 8), (S, 8), (Q, 6), (par, 14), (ada, 4), (E, 13)):
                    c.enter(i, n)
                T.enter(i, {lo_done: 32, emptied: 14, vec_own: 36, qk_rot: 1, y_ready: 1, ada_sum: 4})
                head(i + 1, i * 4, True)
            for c in (W, S, Q, par, ada, E):
                c.leave(RH - 1)
            T.leave(RH - 1)
            take_cols(mcol[:, :, :], 96)
            take_cols(fcol2[:, :], 88)
            for n in range(4):
                if n == 3:
                    start_late(lambda j: yt[:, j, :], TOK)
                split()
                read_ada()
            take_gated(4 * (RH - 1))


            F = Count()
            gates = [0, 0]

            def project(nt, steps, source, gate_dmas, last_size=UNIT):
                n = nt * P
                T.settle()
                if steps > 2:
                    with vec.Fori(0, steps - 2) as i:
                        W.enter(i, 1)
                        A.enter(i, 1)
                        T.enter(i, {lo_done: 4, ak_lo: 4})
                        split(UNIT, lambda j: source(i * 4 + (4 + j)), n)
                    W.leave(steps - 2)
                    A.leave(steps - 2)
                    T.leave(steps - 2)
                take_gates(nt, gate_dmas)
                k0 = 4 * (steps - 1)
                split(last_size, lambda j: source(k0 + (j // 2 if last_size < UNIT else j)), n)
                S.base += steps
                finish_rows(nt)

            def take_gates(nt, dmas):
                if gates[0] == 0:
                    vec.wait_ge(x_loaded, 64)
                gates[0] += 16 * dmas
                vec.wait_ge(gate_loaded, gates[0])
                for k in range(nt // 2):
                    T.mark(vec.tensor_tensor(gb[:, k, :], gb[:, k, :], gn, ALU.mult), vec_own)

            def finish_rows(nt):
                halves = [4 * ((par.base + z) % 2) for z in range(nt // 2)]
                par.base += nt // 2
                for part in range(2):
                    tiles = tiles_of(nt, part)
                    act_read()
                    T.settle()
                    T.mark(vec.reciprocal(st[:, 8 + tiles[0]:9 + tiles[-1]], st[:, 4 + tiles[0]:5 + tiles[-1]]), vec_own)
                    T.settle()
                    for t in tiles:
                        b = halves[t // 2] + 2 * (t % 2)
                        T.mark(vec.scalar_tensor_tensor(out=ytmp[:, t % 2, :].rearrange("p (c n) -> p c n", c=2), in0=ps[:, b:b + 2, :],
                                                        scalar=st[:, 8 + t:9 + t],
                                                        in1=gb[:, t // 2, :].rearrange("p (c n) -> p c n", c=2),
                                                        op0=ALU.mult, op1=ALU.mult), emptied if t % 2 else vec_own)
                    T.settle()
                    T.mark(vec.tensor_tensor(res[:, tiles[0]:tiles[-1] + 1, :], res[:, tiles[0]:tiles[-1] + 1, :],
                                             ytmp[:, tiles[0] % 2:tiles[-1] % 2 + 1, :], ALU.add), h_ready)
                    norm_rows(nt, part, range(2) if part else ())
                split(units=range(2, SLOTS))

            def read_ffn(ft, n):
                p = par.base % 2
                hb = step_full()
                seqs = n // SEQ
                vec.wait_ge(ffn_lin, F.next() + 1)
                views = [(lin[:, p, m, 0:n].rearrange("p (s n) -> p s n", s=seqs),
                          ps[:, hb + 2 + m, 0:n].rearrange("p (s n) -> p s n", s=seqs)) for m in range(2)]
                for tap in (0, 2):
                    for m, (x, g) in enumerate(views):
                        o, i_ = (x[:, :, 1:SEQ], g[:, :, 0:SEQ - 1]) if tap == 0 else (x[:, :, 0:SEQ - 1], g[:, :, 1:SEQ])
                        T.mark(vec.scalar_tensor_tensor(out=o, in0=i_, scalar=conv_col(n, ft + (tap * FT + m)),
                                                        in1=o, op0=ALU.mult, op1=ALU.add),
                               ffn_conv if (tap, m) == (2, 1) else vec_own)
                    if tap == 0:
                        T.settle()
                act_read()
                dst = hid if n == TOK else hid2
                T.mark(vec.tensor_tensor(dst[:, ds(ft, 2), :], lin[:, p, :, 0:n], ps[:, hb:hb + 2, 0:n], ALU.mult), emptied)

            project(4, 4, lambda k: yt[:, k, :], 3)
            prep(4, 16, 32)
            with vec.Fori(0, 5) as i:
                for c, n in ((W, 2), (S, 2), (par, 2), (F, 2), (E, 2)):
                    c.enter(i, n)
                T.enter(i, {lo_done: 8, emptied: 2, vec_own: 6, ffn_conv: 2})
                split()
                read_ffn(i * 4, TOK)
                split()
                read_ffn(i * 4 + 2, TOK)
            for c in (W, S, par, F, E):
                c.leave(5)
            T.leave(5)
            split()
            start_late(lambda j: hid[:, j, :], TOK)
            read_ffn(20, TOK)
            take_cols(mcol[:, :, :], 96)
            project(4, 6, lambda k: hid[:, k, :], 3, 512)
            prep(4, 32, 8)

            vec.wait_ge(kdif_loaded, 16)
            vec.wait_ge(lam_loaded, 64)
            for z in range(2):
                own(vec.tensor_tensor(lamq[:, z, :], lamq[:, z, :], lamq[:, 2 + z, :], ALU.mult))
                T.mark(vec.tensor_reduce(lamt[:, z:z + 1], lamq[:, z, :], AX.X, ALU.add), (vec_own, lam_dots)[z])
            vec.wait_ge(lam_exp, 1)
            own(vec.tensor_tensor(lamt[:, 4:5], lamt[:, 3:4], lamt[:, 2:3], ALU.subtract))
            own(vec.tensor_scalar(lamt[:, 4:5], lamt[:, 4:5], -LAM_INIT, None, ALU.add))
            own(vec.tensor_scalar(lamt[:, 5:6], gcol[:, SUB0:SUB0 + 1], 1.0 - LAM_INIT, None, ALU.mult))
            def take_qk(size):
                split(size)
                hb = step_full()
                for t in range(2):
                    z4 = ps[:, hb + t, :].rearrange("p (z h x n) -> p z h x n", z=8, h=2, x=2)
                    r4 = drot[:, t, :].rearrange("p (z h x n) -> p z h x n", z=8, h=2, x=2)
                    s3 = dsin[:, t, :].rearrange("p (h x n) -> p h x n", h=2, x=2)
                    T.mark(vec.tensor_tensor(dqk[:, t, :].rearrange("p (z n) -> p z n", z=8),
                                             ps[:, hb + t, :].rearrange("p (z n) -> p z n", z=8),
                                             dcos[:, t, :].unsqueeze(1).to_broadcast([P, 8, 64]), ALU.mult), vec_own)
                    for x in range(2):
                        T.mark(vec.tensor_tensor(r4[:, :, :, x, :], z4[:, :, :, 1 - x, :],
                                                 s3[:, :, x, :].unsqueeze(1).to_broadcast([P, 8, 2, 16]), ALU.mult), vec_own)
                T.settle()
                T.mark(vec.tensor_tensor(dqk[:, 0:2, :], dqk[:, 0:2, :], drot, ALU.add), vec_own)
                act_read()
                tick(qk_rot)
                tick(emptied)

            def take_v():
                split()
                hb = step_full()
                T.mark(vec.tensor_copy(dv[:, 2:4, :], ps[:, hb + 2:hb + 4, 0:256]), vec_own)
                close()

            def attend_pair(i, steps):
                hb = group_full()
                T.mark(vec.tensor_copy(dkt[:, 1, :], ps[:, hb + 2, :]), vec_own)
                close()
                for h in range(2):
                    hb = group_full()
                    T.mark(vec.tensor_reduce(st[:, 40 + 4 * h:44 + 4 * h], ps[:, hb:hb + 4, :], AX.X, ALU.max), vec_own)
                    T.settle()
                    T.mark(vec.tensor_scalar(st[:, 40 + 4 * h:44 + 4 * h], st[:, 40 + 4 * h:44 + 4 * h], -(DD ** -0.5), None, ALU.mult), nmax_ready)
                    close()
                    o = 48 + 4 * h
                    own(vec.reciprocal(st[:, o:o + 4], st[:, o:o + 4]))
                    own(vec.tensor_scalar(st[:, o + 2:o + 4], st[:, o + 2:o + 4], lamt[:, 4:5], None, ALU.mult))
                    for t in range(2):
                        T.mark(vec.tensor_scalar(dpr[:, h, 2 + t, :], dpr[:, h, 2 + t, :], st[:, o + 2 + t:o + 3 + t], None, ALU.mult), vec_own)
                    T.settle()
                    for t in range(2):
                        T.mark(vec.scalar_tensor_tensor(out=dpr[:, h, t, :], in0=dpr[:, h, t, :], scalar=st[:, o + t:o + 1 + t],
                                                        in1=dpr[:, h, 2 + t, :], op0=ALU.mult, op1=ALU.add), (vec_own, prob_ready)[t])
                if steps:
                    take_qk(512)
                for h in range(2):
                    hb = group_full()
                    T.mark(vec.tensor_copy(dpt[:, h, 2:4, :], ps[:, hb + 1, :].rearrange("p (k n) -> p k n", k=2)), vec_own)
                    close()
                for h in range(2):
                    hb = group_full()
                    act_read()
                    o = 24 + 2 * h
                    own(vec.reciprocal(st[:, o:o + 2], st[:, o - 4:o - 2]))
                    for t in range(2):
                        T.mark(vec.tensor_scalar(dy[:, h, t, :], ps[:, hb, t * P:(t + 1) * P], st[:, o + t:o + 1 + t], None, ALU.mult),
                               (vec_own, emptied)[t])
                if steps:
                    take_v()
                hb = group_full()
                act_read()
                T.mark(vec.scalar_tensor_tensor(out=al8[:, ds(i * 2, 2), :], in0=ps[:, hb, :].rearrange("p (h n) -> p h n", h=2),
                                                scalar=lamt[:, 5:6], in1=ah8[:, ds(i * 2, 2), :],
                                                op0=ALU.mult, op1=ALU.subtract), emptied)

            take_qk(512)
            take_v()
            with vec.Fori(0, DH // 2 - 1) as i:
                for c, n in ((W, 2), (S, 2), (Q, 8), (par, 10), (E, 10)):
                    c.enter(i, n)
                T.enter(i, {lo_done: 8, emptied: 10, vec_own: 27, qk_rot: 1, nmax_ready: 2, prob_ready: 2})
                attend_pair(i, True)
            for c in (W, S, Q, par, E):
                c.leave(DH // 2 - 1)
            T.leave(DH // 2 - 1)
            attend_pair(DH // 2 - 1, False)
            split()
            S.base += 2
            take_gates(2, 2)
            finish_rows(2)
            prep(2, 48, 32)
            with vec.Fori(0, 5) as i:
                for c, n in ((W, 2), (S, 2), (par, 2), (F, 2), (E, 2)):
                    c.enter(i, n)
                T.enter(i, {lo_done: 8, emptied: 2, vec_own: 6, ffn_conv: 2})
                split()
                read_ffn(i * 4, SEQ)
                split()
                read_ffn(i * 4 + 2, SEQ)
            for c in (W, S, par, F, E):
                c.leave(5)
            T.leave(5)
            split()
            start_late(lambda j: hid2[:, j, :], SEQ)
            read_ffn(20, SEQ)
            project(2, 6, lambda k: hid2[:, k, :], 2, 512)
            prep(2, MIXG0, None)

            def read_half(dst):
                hb = step_full()
                T.mark(vec.tensor_copy(dst[:, 2:4, :], ps[:, hb + 2:hb + 4, 0:SEQ]), vec_own)
                close()

            def read_values(dst):
                hb = step_full()
                T.mark(vec.tensor_copy(dst, ps[:, hb + 1, :]), vec_own)
                close()

            split()
            read_half(qkt5[:, 0])
            split()
            read_half(qkt5[:, 1])
            split()
            read_values(vab[:, 1, :])
            split()
            read_half(qkt5[:, 2])
            split()
            read_half(qkt5[:, 3])
            split()
            read_values(vab[:, 3, :])
            split(144)
            read_half(qkt5[:, 4])
            split()
            hb = step_full()
            act_read()
            T.mark(vec.tensor_copy(wiw, ps[:, hb:hb + 2, 64:72]), emptied)
            split()
            hb = step_full()
            vec.wait_ge(xc_lin, 1)
            for d in (1, 2, 3):
                T.settle()
                for m in range(4):
                    c = CW0 + 4 * (3 - d) + m
                    T.mark(vec.scalar_tensor_tensor(out=xcv[:, m, d:SEQ], in0=ps[:, hb + m, 0:SEQ - d], scalar=gcol[:, c:c + 1],
                                                    in1=xcv[:, m, d:SEQ], op0=ALU.mult, op1=ALU.add),
                           emptied if (d, m) == (3, 3) else vec_own)
            split()
            step_full()
            close()
            hb = group_full()
            T.mark(vec.tensor_copy(kit, ps[:, hb, 0:SEQ]), emptied)
            def take_gate():
                split()
                step_full()
                close()

            take_gate()
            group_full()
            close()
            for m in range(4):
                T.mark(vec.tensor_scalar(rt[:, m, :], rt[:, m, :], lgt[:, 4, 8 + m:9 + m], -8.0, ALU.mult, ALU.mult),
                       lru_arg if m == 3 else vec_own)
            T.mark(vec.tensor_tensor(it, it, xcv, ALU.mult), vec_own)

            for t, n in ((1, SEQ), (0, P)):
                group_full()
                act_read()
                v = rl.rearrange("p a b -> p (a b)")[:, 0:8 * n].rearrange("p (h n) -> p h n", h=8)
                own(vec.tensor_scalar(wk[:, t, 0:n], v[:, 0, :], wiw[:, t, 0:1], None, ALU.mult))
                for i in range(1, 8):
                    h = (i % 4) * 2 + i // 4
                    own(vec.scalar_tensor_tensor(out=wk[:, t, 0:n], in0=v[:, i, :], scalar=wiw[:, t, h:h + 1],
                                                 in1=wk[:, t, 0:n], op0=ALU.mult, op1=ALU.add))
                if t == 1:
                    vec.wait_ge(causal_loaded, 16)
                own(vec.scalar_tensor_tensor(out=wk[:, t, 0:n], in0=wk[:, t, 0:n], scalar=float(8 * HD) ** -0.5,
                                             in1=causal[:, t, 0:n], op0=ALU.mult, op1=ALU.add))
                tick(emptied)
                if t == 1:
                    vec.wait_ge(lru_fun, 1)
                    own(vec.tensor_tensor(rt, la, la, ALU.mult))
                    T.mark(vec.scalar_tensor_tensor(out=lt, in0=rt, scalar=1.0, in1=lt, op0=ALU.add, op1=ALU.mult), lru_sq)
                    take_gate()
            vec.wait_ge(lru_root, 1)
            T.settle()
            own(vec.tensor_tensor(it, it, lt, ALU.mult))
            for m in range(4):
                T.mark(vec.tensor_tensor_scan(out=xcv[:, m, :], data0=la[:, m, :], data1=it[:, m, :], initial=0.0,
                                              op0=ALU.mult, op1=ALU.add), vec_own)
            T.settle()
            T.mark(vec.tensor_tensor(gy, gy, xcv, ALU.mult), yc_ready)
            vec.wait_ge(yc_hi, 1)
            T.mark(vec.tensor_tensor(ul[:, 0:4, SEQ:TOK], gy, uh[:, 0:4, SEQ:TOK], ALU.subtract), yc_lo)

            def pick(rounds):
                for _ in range(rounds):
                    for t, n in ((1, SEQ), (0, P)):
                        T.mark(vec.max(out=st[:, 24 + 8 * t:32 + 8 * t], in_=wk[:, t, 0:n]), vec_own)
                    T.settle()
                    for t, n in ((1, SEQ), (0, P)):
                        T.mark(vec.match_replace(out=wk[:, t, 0:n], in_to_replace=st[:, 24 + 8 * t:32 + 8 * t],
                                                 in_values=wk[:, t, 0:n], imm_value=MARK), vec_own)
                    T.settle()

            def maxima(n):
                z, g = n // 2, n % 2
                hb = group_full()
                e = lg[:, g, :]
                e1, e0 = (e[:, 0:1024].rearrange("p (x n) -> p x n", x=4), e[:, 1024:1536].rearrange("p (x n) -> p x n", x=4))
                vec.wait_ge(z_loaded[g], 32 * (z + 1))
                T.mark(vec.scalar_tensor_tensor(out=e1, in0=ps[:, hb:hb + 2, :].rearrange("p b (x n) -> p (b x) n", x=2),
                                                scalar=HD ** -0.5, in1=zt[:, g, :, :], op0=ALU.mult, op1=ALU.add), vec_own)
                T.mark(vec.scalar_tensor_tensor(out=e0.rearrange("p (b x) n -> p b x n", b=2),
                                                in0=ps[:, hb + 2:hb + 4, 0:2 * P].rearrange("p b (x n) -> p b x n", x=2),
                                                scalar=HD ** -0.5, in1=zt[:, g, :, P:SEQ].rearrange("p (b x) n -> p b x n", b=2),
                                                op0=ALU.mult, op1=ALU.add), z_used)
                tick(emptied)
                if z:
                    T.mark(vec.tensor_tensor(e1, e1, maskb[:, 1, :].unsqueeze(1).to_broadcast([P, 4, SEQ]), ALU.add), vec_own)
                    T.mark(vec.tensor_tensor(e0, e0, maskb[:, 0, 0:P].unsqueeze(1).to_broadcast([P, 4, P]), ALU.add), vec_own)
                    T.settle()
                c = 40 + 16 * g
                T.mark(vec.tensor_reduce(st[:, c:c + 4], e1, AX.X, ALU.max, negate=True), vec_own)
                T.mark(vec.tensor_reduce(st[:, c + 4:c + 8], e0, AX.X, ALU.max, negate=True), nmax_ready)

            def normalise(n):
                e, c = lg[:, n % 2, :], 40 + 16 * (n % 2)
                e1, e0 = (e[:, 0:1024].rearrange("p (x n) -> p x n", x=4), e[:, 1024:1536].rearrange("p (x n) -> p x n", x=4))
                vec.wait_ge(exp_done, n + 1)
                own(vec.reciprocal(st[:, c + 8:c + 16], st[:, c + 8:c + 16]))
                T.mark(vec.tensor_tensor(e1, e1, st[:, c + 8:c + 12].unsqueeze(2).to_broadcast([P, 4, SEQ]), ALU.mult), vec_own)
                T.mark(vec.tensor_tensor(e0, e0, st[:, c + 12:c + 16].unsqueeze(2).to_broadcast([P, 4, P]), ALU.mult), prob_ready)

            def choose(last):
                T.settle()
                pick(TOPK // 16)
                if last:
                    for t, w in ((1, SEQ), (0, P)):
                        T.mark(vec.tensor_scalar(maskb[:, t, 0:w], wk[:, t, 0:w], MARK / 2, NEG, ALU.is_gt, ALU.mult), vec_own)

            maxima(0)
            choose(False)
            normalise(0)
            for n in range(4):
                take_gate()
                hb = group_full()
                T.mark(vec.tensor_copy(pts[:, 1024:1536], ps[:, hb + 2, :]), vec_own)
                close()
                if n < 3:
                    maxima(n + 1)
                hb = group_full()
                act_read()
                T.mark(vec.tensor_tensor(al8[:, 2 * n:2 * n + 2, :], ps[:, hb, :].rearrange("p (x n) -> p x n", x=2),
                                         ah8[:, 2 * n:2 * n + 2, :], ALU.subtract), emptied)
                if n == 0:
                    choose(True)
                if n < 3:
                    normalise(n + 1)
            for b in range(3):
                split()
                hb = step_full()
                o = mg if b == 0 else mt
                T.mark(vec.tensor_tensor(o, ps[:, hb:hb + 4, :], gates3[b].rearrange("p t c n -> p (t c) n"), ALU.mult), emptied)
                if b:
                    T.settle()
                    T.mark(vec.tensor_tensor(mg, mg, mt, ALU.add), merged if b == 2 else vec_own)
            hb = group_full()
            act_read()
            T.mark(vec.tensor_tensor(ul[:, :, SEQ:TOK], ps[:, hb:hb + 4, :].rearrange("p b (x n) -> p (b x) n", x=2),
                                     uh[:, :, SEQ:TOK], ALU.subtract), emptied)
            def add_plain(part):
                hb = 4 * (par.base % 2)
                if part == 0:
                    plain[0] += 1
                    vec.wait_ge(rows_done, 4 + plain[0])
                else:
                    vec.wait_ge(unit_used, S.now() * SLOTS)
                    par.next()
                T.settle()
                r2 = res[:, part, :].rearrange("p (c n) -> p c n", c=2)
                T.mark(vec.tensor_tensor(r2, r2, ps[:, hb + 2 * part:hb + 2 * part + 2, :], ALU.add), h_ready)

            plain = [0]
            split()
            S.base += 2
            for part in range(2):
                add_plain(part)
                if part:
                    tick(emptied)
                norm_rows(2, part, range(2) if part else ())
            split(units=range(2, SLOTS))
            prep(2, MLPG0, None)
            def read_hidden(k):
                split()
                step_full()
                act_read()
                v = hid3[:, ds(k, 4), :]
                T.mark(vec.tensor_tensor(v, v, v, ALU.mult), emptied)

            with vec.Fori(0, 3) as i:
                for c, n in ((W, 2), (S, 2), (par, 2), (E, 2)):
                    c.enter(i, n)
                T.enter(i, {lo_done: 8, emptied: 2})
                for z in range(2):
                    read_hidden(i * 8 + 4 * z)
            for c in (W, S, par, E):
                c.leave(3)
            T.leave(3)
            read_hidden(24)
            start_late(lambda j: hid3[:, j, :], SEQ)
            read_hidden(28)
            T.settle()
            with vec.Fori(0, 7) as i:
                W.enter(i, 1)
                A.enter(i, 1)
                T.enter(i, {lo_done: 4, ak_lo: 4})
                split(UNIT, lambda j: hid3[:, i * 4 + (4 + j), :], SEQ)
            W.leave(7)
            A.leave(7)
            T.leave(7)
            S.base += 8
            vec.wait_ge(gain_loaded, 16)
            for t in range(2):
                add_plain(t)
                vec.wait_ge(rms_done, rms_parts[0] + 1 + t)
                own(vec.reciprocal(st[:, 8 + t:9 + t], st[:, 4 + t:5 + t]))
                T.mark(vec.scalar_tensor_tensor(out=fout[:, t, :], in0=res[:, t, :], scalar=st[:, 8 + t:9 + t], in1=gn,
                                                op0=ALU.mult, op1=ALU.mult), out_ready)

        @block.gpsimd
        def _(pool):
            ada = Count()

            def load_rows(batch, parts, wait):
                if wait:
                    pool.wait_ge(cols_ready, wait)
                r = 0
                for v in parts:
                    n = int(np.prod(v.shape)) // P
                    src = bass.AP(v.tensor, v.offset, [[P, n], [1, P]])
                    pool.dma_start(rows[r:r + n, batch % 2, :], src).then_inc(rows_loaded[batch % 2], 16)
                    r += n

            def ada_rows(l, c0, row=1):
                n = ada.next()
                if not (isinstance(n, int) and n == 0):
                    pool.wait_ge(ada_sum, n)
                pool.wait_ge(ident_loaded, 16)
                pool.dma_start(adat[:, 0, :], a["ada_b"][l, ds(c0, 512)].unsqueeze(0).to_broadcast([64, 512])).then_inc(bias_loaded, 16)
                pool.wait_ge(ada_sum, n + 1)
                pool.wait_ge(ident_loaded, 16)
                pool.dma_start(mods[l, :, ds(c0, 512)], sums_row(row)[0:64:32, :]).then_inc(ada_stored, 16)

            pool.dma_start(ident[:, :], a["k_ident"]).then_inc(ident_loaded, 16)
            load_rows(0, [a["c"][0], a["c_ctx"], a["ffn_conv_w"][0], a["ffn_conv_b"][0]], 0)
            load_rows(1, [a["norm_g"], a["norm_mix_g_2"], a["norm_mlp_g_2"], a["conv_w_2"], a["conv_b_2"],
                          a["b_r_2"], a["b_i_2"], a["lru_lambda_2"], a["diff_subln"]], 0)
            pool.memset(epsc[:, :], EPS).then_inc(eps_set, 1)
            pool.dma_start(res[:, 0:2, :], a["x"][0].rearrange("(t p) n -> p t n", p=P)).then_inc(x_loaded, 16)
            pool.dma_start(res[:, 2:4, :], a["ctx"][0].rearrange("(t p) n -> p t n", p=P)).then_inc(x_loaded, 16)
            for z, name in enumerate(("ret_decay_f", "ret_decay_b")):
                pool.dma_start(lgt[:, 0, 4 * z:4 * z + 4], a[name].to_broadcast([P, RH])).then_inc(decay_loaded, 16)
            pool.wait_ge(eps_set, 1)
            pool.memset(tab[32:33, :], NEG).then_inc(tab_set, 1)
            pool.dma_start(tab[0:32, :], a["rel_bias_2"]).then_inc(hot_loaded, 16)
            pool.dma_start(hot, a["k_hot"]).then_inc(hot_loaded, 16)
            for c in range(4):
                ada_rows(0, c * 512, 1 + c % 2)
            pool.dma_start(kret, a["k_ret"]).then_inc(const_loaded, 16)
            pool.dma_start(kdif[:, :], a["k_dif"]).then_inc(kdif_loaded, 16)
            for h in range(RH):
                for c in (4 + 2 * h, 5 + 2 * h):
                    ada_rows(0, c * 512)
                if h == RH - 1:
                    pool.wait_ge(ada_stored, 16 * 18)
                    load_rows(3, [mods[0, 0, :], mods[0, 1, :]], 2)
                    load_rows(4, [a["ffn_conv_w"][1], a["ffn_conv_b"][1]], 2)
                for c in (2 * h, 2 * h + 1):
                    ada_rows(1, c * 512)
                if h == 0:
                    pool.wait_ge(zrow_ready, 1)
                    pool.dma_start(zrow, zst.unsqueeze(1).to_broadcast([2 * NH, P, 384])).then_inc(zrow_stored, 16)
            for c in range(8, 12):
                ada_rows(1, c * 512)
            pool.wait_ge(unit_used, S_RETO * SLOTS + 1)
            pool.dma_start(res[:, 0:2, :], a["x"][0].rearrange("(t p) n -> p t n", p=P)).then_inc(x_loaded, 16)
            pool.dma_start(res[:, 2:4, :], a["ctx"][0].rearrange("(t p) n -> p t n", p=P)).then_inc(x_loaded, 16)
            def load_gates(l, conds, part, gain):
                for c in range(conds):
                    pool.dma_start(gb[:, c, :], mods[l, c, part * D:(part + 1) * D].unsqueeze(0).to_broadcast([P, D])).then_inc(gate_loaded, 16)
                pool.dma_start(gn, a["norm_g"][l, gain].unsqueeze(0).to_broadcast([P, D])).then_inc(gate_loaded, 16)

            load_gates(0, 2, 2, 1)
            pool.wait_ge(unit_used, S_UP0 * SLOTS + 1)
            load_gates(0, 2, 5, 3)
            pool.wait_ge(ada_stored, 16 * 24)
            load_rows(5, [mods[1, 0, :], mods[1, 1, :]], 3)
            for z, name in enumerate(("diff_lq1", "diff_lq2", "diff_lk1", "diff_lk2")):
                pool.dma_start(lamq[:, z, :], a[name].to_broadcast([P, DD])).then_inc(lam_loaded, 16)
            pool.wait_ge(unit_used, S_DIF * SLOTS + 1)
            load_gates(1, 1, 2, 1)
            pool.wait_ge(unit_used, S_UP1 * SLOTS + 1)
            load_gates(1, 1, 5, 3)
            pool.wait_ge(unit_used, S_MIX * SLOTS + 1)
            for z, name in enumerate(("w_r_2", "w_i_2")):
                for half in range(2):
                    pool.dma_start(wri[64 * half:64 * half + 64, z, :, :],
                                   a[name][0].rearrange("(m b) c d -> b c m d", b=2)[half]).then_inc(mix_loaded, 16)
            pool.dma_start(causal, a["k_causal"].rearrange("p (t n) -> p t n", t=2)).then_inc(causal_loaded, 16)
            pool.wait_ge(zrow_stored, 16)
            for n in range(4):
                if n >= 2:
                    pool.wait_ge(z_used, n - 1)
                for odd in range(2):
                    skew = bass.AP(zrow.tensor, zrow.offset + (4 * n + odd) * P * 384 + 127, [[383, P], [2 * P * 384, 2], [1, SEQ]])
                    pool.dma_start(zt[:, n % 2, 2 * odd:2 * odd + 2, :], skew).then_inc(z_loaded[n % 2], 16)
            pool.wait_ge(unit_used, S_MUP * SLOTS + 1)
            pool.dma_start(gn, a["final_norm_g_2"].unsqueeze(0).to_broadcast([P, D])).then_inc(gain_loaded, 16)
            o2 = out[0].rearrange("(t p) n -> t p n", p=P)
            for t in range(2):
                pool.wait_ge(out_ready, t + 1)
                pool.dma_start(o2[t], fout[:, t, :]).then_inc(out_stored, 16)
            pool.wait_ge(out_stored, 32)


def kernel(**inputs):
    import concourse.bacc as bacc
    from concourse.bass_utils import run_bass_kernel_spmd

    nc = bacc.Bacc("TRN2", target_bir_lowering=False, num_devices=1)
    arrays = {**{k: np.ascontiguousarray(v) for k, v in inputs.items()}, **shape_constants()}
    feed, aps = {}, {}
    for name, v in arrays.items():
        feed[f"in_{name}"] = v
        aps[name] = nc.dram_tensor(f"in_{name}", v.shape, mybir.dt.from_np(v.dtype), kind="ExternalInput").ap()
    out = nc.dram_tensor("out_x", (1, SEQ, D), F32, kind="ExternalOutput").ap()
    build(nc, aps, out)
    r = run_bass_kernel_spmd(nc, [feed], core_ids=[0])
    return r.results[0]["out_x"]
```
